# Optimizing a Trainium2 kernel written in Bass

```python
import math
import jax
import jax.numpy as jnp
from jax import lax
import numpy as np

D_MODEL = 1024
BATCH = 1
SEQ = 512
DEPTH = 1

N_MIXERS = 4
QBLOCK = 128
NORM_EPS = 1e-6
NEG_BIG = -1e30
F32 = jnp.float32
DA_HEADS = 8
DA_HEAD_DIM = 64
DA_IN_WIDTH = 3 * DA_HEADS * 2 * DA_HEAD_DIM
NSA_HEADS = 16
NSA_KV_GROUPS = 2
NSA_HEAD_DIM = 64
NSA_QBLOCK = 64
CMP_BLOCK = 32
CMP_STRIDE = 16
CMP_HIDDEN = 256
SEL_BLOCK = 64
N_SELECT = 8
WINDOW = 512
NSA_IN_WIDTH = NSA_HEADS * NSA_HEAD_DIM + 6 * NSA_KV_GROUPS * NSA_HEAD_DIM + 3 * NSA_HEADS
GDN_HEADS = 8
GDN_HEAD_DIM = 128
GDN_CHUNK = 64
GDN_IN_WIDTH = 4 * GDN_HEADS * GDN_HEAD_DIM + 2 * GDN_HEADS
CONV_WIDTH = 4
LRU_WIDTH = D_MODEL
LRU_BLOCKS = 4
LRU_C = 8.0
N_GROUPS = 4
EXPERTS_PER_GROUP = 4
N_EXPERTS = N_GROUPS * EXPERTS_PER_GROUP
TOP_K_IN_GROUP = 2
D_EXPERT = 512


def rmsnorm(x, gain):
    xf = x.astype(F32)
    y = xf * lax.rsqrt(jnp.mean(xf * xf, -1, keepdims=True) + NORM_EPS)
    return (y * gain.astype(F32)).astype(x.dtype)

def l2norm(x):
    xf = x.astype(F32)
    return xf * lax.rsqrt(jnp.sum(xf * xf, -1, keepdims=True) + NORM_EPS)

def alibi_slopes(n):
    return jnp.asarray(2.0 ** (-8.0 * np.arange(1, n + 1) / n), dtype=F32)

def causal_depthwise_conv(x, w):
    k = w.shape[0]
    xp = jnp.pad(x, ((0, 0), (k - 1, 0), (0, 0)))
    return lax.conv_general_dilated(xp, w[:, None, :].astype(x.dtype), window_strides=(1,), padding='VALID',
                                    dimension_numbers=('NWC', 'WIO', 'NWC'), feature_group_count=x.shape[-1])

def diff_attention(x, w_in, q_gain, k_gain, lq1, lk1, lq2, lk2, subln, w_out, lambda_init):
    B, T, _ = x.shape
    H, dh = DA_HEADS, DA_HEAD_DIM
    q, k, v = jnp.split(x @ w_in, [2 * H * dh, 4 * H * dh], axis=-1)
    q = rmsnorm(q.reshape(B, T, H, 2, dh), q_gain) * (dh ** -0.5)
    k = rmsnorm(k.reshape(B, T, H, 2, dh), k_gain)
    v = v.reshape(B, T, H, 2 * dh)
    lam = (jnp.exp(jnp.sum(lq1.astype(F32) * lk1.astype(F32)))
           - jnp.exp(jnp.sum(lq2.astype(F32) * lk2.astype(F32))) + lambda_init)
    slopes = alibi_slopes(H)
    outs = []
    for s in range(0, T, QBLOCK):
        e = s + QBLOCK
        sc = jnp.einsum('bqhcd,bkhcd->bhcqk', q[:, s:e], k[:, :e]).astype(F32)
        dist = (jnp.arange(s, e)[:, None] - jnp.arange(e)[None, :]).astype(F32)
        sc = jnp.where(dist >= 0, sc - slopes[:, None, None, None] * dist, -jnp.inf)
        p = jax.nn.softmax(sc, axis=-1)
        pd = p[:, :, 0] - lam * p[:, :, 1]
        outs.append(jnp.einsum('bhqk,bkhe->bqhe', pd.astype(v.dtype), v[:, :e]))
    o = rmsnorm(jnp.concatenate(outs, axis=1), subln) * (1.0 - lambda_init)
    return o.reshape(B, T, H * 2 * dh) @ w_out

def nsa_attention(x, w_in, q_gain, k_gains, cmp_pos, cmp_w1, cmp_w2, w_out):
    B, T, _ = x.shape
    H, G, dh = NSA_HEADS, NSA_KV_GROUPS, NSA_HEAD_DIM
    P = H // G
    kvw = G * dh
    cuts = np.cumsum([H * dh] + [kvw] * 6).tolist()
    q, kc, vc, ks, vs, kw, vw, gl = jnp.split(x @ w_in, cuts, axis=-1)
    q = (rmsnorm(q.reshape(B, T, H, dh), q_gain) * (dh ** -0.5)).reshape(B, T, G, P, dh)
    gates = jax.nn.sigmoid(gl.reshape(B, T, G, P, 3))
    n_cmp = (T - CMP_BLOCK) // CMP_STRIDE + 1
    cidx = np.arange(n_cmp)[:, None] * CMP_STRIDE + np.arange(CMP_BLOCK)[None, :]

    def compress(t, c):
        tb = t.reshape(B, T, G, dh)[:, cidx] + cmp_pos[c][:, None, :]
        tb = tb.transpose(0, 1, 3, 2, 4).reshape(B, n_cmp, G, CMP_BLOCK * dh)
        return jax.nn.silu(tb @ cmp_w1[c]) @ cmp_w2[c]

    kcmp = rmsnorm(compress(kc, 0), k_gains[0])
    vcmp = compress(vc, 1)
    cmp_end = jnp.asarray(cidx[:, -1])
    n_sel = T // SEL_BLOCK
    k_top = min(N_SELECT, n_sel)

    def to_blocks(t):
        return t.reshape(B, n_sel, SEL_BLOCK, G, dh).transpose(0, 3, 1, 2, 4)

    ksb = to_blocks(rmsnorm(ks.reshape(B, T, G, dh), k_gains[1]))
    vsb = to_blocks(vs)
    cs = np.arange(n_cmp) * CMP_STRIDE
    ss0 = np.arange(n_sel) * SEL_BLOCK
    overlap = jnp.asarray(((cs[:, None] < ss0[None, :] + SEL_BLOCK)
                           & (cs[:, None] + CMP_BLOCK > ss0[None, :])).astype(np.float32))
    kwin = rmsnorm(kw.reshape(B, T, G, dh), k_gains[2])
    vwin = vw.reshape(B, T, G, dh)
    slopes = alibi_slopes(H).reshape(G, P)
    gather = jax.vmap(jax.vmap(lambda blocks, idx: blocks[idx]))
    blk_ids = jnp.arange(n_sel)
    outs = []
    for s in range(0, T, NSA_QBLOCK):
        e = s + NSA_QBLOCK
        qb = q[:, s:e]
        tpos = jnp.arange(s, e)
        dist_c = (tpos[:, None] - cmp_end[None, :]).astype(F32)
        valid_c = dist_c >= 0
        sc = jnp.einsum('bqgpd,bcgd->bgpqc', qb, kcmp).astype(F32) - slopes[:, :, None, None] * dist_c
        p_c = jax.nn.softmax(jnp.where(valid_c, sc, NEG_BIG), -1) * valid_c
        o_cmp = jnp.einsum('bgpqc,bcgd->bqgpd', p_c.astype(vcmp.dtype), vcmp)
        imp = jnp.einsum('bgpqc,cn->bgqn', p_c, overlap)
        qblk = tpos // SEL_BLOCK
        forced = (blk_ids[None, :] == 0) | (blk_ids[None, :] == qblk[:, None])
        future = blk_ids[None, :] > qblk[:, None]
        score = jnp.where(forced, 1e4, jnp.where(future, -1.0, imp))
        _, sel = lax.top_k(score, k_top)
        kg = gather(ksb, sel)
        vg = gather(vsb, sel)
        dist_s = (tpos[None, None, :, None, None]
                  - (sel[..., None] * SEL_BLOCK + jnp.arange(SEL_BLOCK))).astype(F32)
        ssc = (jnp.einsum('bqgpd,bgqksd->bgpqks', qb, kg).astype(F32)
               - slopes[None, :, :, None, None, None] * dist_s[:, :, None])
        ssc = jnp.where(dist_s[:, :, None] >= 0, ssc, -jnp.inf)
        p_s = jax.nn.softmax(ssc.reshape(B, G, P, NSA_QBLOCK, k_top * SEL_BLOCK), -1)
        o_sel = jnp.einsum('bgpqn,bgqnd->bqgpd', p_s.astype(vg.dtype),
                           vg.reshape(B, G, NSA_QBLOCK, k_top * SEL_BLOCK, dh))
        ws = max(0, s - WINDOW + 1)
        dist_w = (tpos[:, None] - jnp.arange(ws, e)[None, :]).astype(F32)
        valid_w = (dist_w >= 0) & (dist_w < WINDOW)
        swc = jnp.einsum('bqgpd,bkgd->bgpqk', qb, kwin[:, ws:e]).astype(F32) - slopes[:, :, None, None] * dist_w
        p_w = jax.nn.softmax(jnp.where(valid_w, swc, -jnp.inf), -1)
        o_win = jnp.einsum('bgpqk,bkgd->bqgpd', p_w.astype(vwin.dtype), vwin[:, ws:e])
        gb = gates[:, s:e]
        outs.append(gb[..., 0:1] * o_cmp + gb[..., 1:2] * o_sel + gb[..., 2:3] * o_win)
    o = jnp.concatenate(outs, axis=1).reshape(B, T, H * dh)
    return o @ w_out

def gated_deltanet(x, w_in, conv_w, a_log, dt_bias, out_gain, w_out):
    B, T, _ = x.shape
    H, dk = GDN_HEADS, GDN_HEAD_DIM
    C = GDN_CHUNK
    n = T // C
    W = H * dk
    qkv, z, b, a = jnp.split(x @ w_in, [3 * W, 4 * W, 4 * W + H], axis=-1)
    qkv = jax.nn.silu(causal_depthwise_conv(qkv, conv_w))
    q, k, v = jnp.split(qkv, 3, axis=-1)
    q = l2norm(q.reshape(B, T, H, dk)) * (dk ** -0.5)
    k = l2norm(k.reshape(B, T, H, dk))
    v = v.reshape(B, T, H, dk).astype(F32)
    beta = jax.nn.sigmoid(b.astype(F32))
    g = -jnp.exp(a_log.astype(F32)) * jax.nn.softplus(a.astype(F32) + dt_bias.astype(F32))

    def chunks(t):
        return jnp.moveaxis(t.reshape(B, n, C, H, *t.shape[3:]), 3, 1)

    q, k, v, beta, g = chunks(q), chunks(k), chunks(v), chunks(beta), chunks(g)
    gc = jnp.cumsum(g, axis=-1)
    tril = jnp.tril(jnp.ones((C, C), bool))
    decay = jnp.exp(jnp.where(tril, gc[..., :, None] - gc[..., None, :], -jnp.inf))
    kb = k * beta[..., None]
    lmat = jnp.einsum('bhnid,bhnjd->bhnij', kb, k) * decay * jnp.tril(jnp.ones((C, C), F32), -1)
    ia = lmat + jnp.eye(C, dtype=F32)
    u = lax.linalg.triangular_solve(ia, v * beta[..., None], left_side=True, lower=True, unit_diagonal=True)
    w = lax.linalg.triangular_solve(ia, kb * jnp.exp(gc)[..., None], left_side=True, lower=True, unit_diagonal=True)
    aqk = jnp.einsum('bhnid,bhnjd->bhnij', q, k) * decay

    def step(S, inp):
        qc, kc, uc, wc, gcc, aq = inp
        v_new = uc - jnp.einsum('bhck,bhkv->bhcv', wc, S)
        o = (jnp.einsum('bhck,bhkv->bhcv', qc * jnp.exp(gcc)[..., None], S)
             + jnp.einsum('bhij,bhjv->bhiv', aq, v_new))
        glast = gcc[..., -1:]
        S = S * jnp.exp(glast)[..., None] + jnp.einsum('bhck,bhcv->bhkv', kc * jnp.exp(glast - gcc)[..., None], v_new)
        return S, o

    xs = (jnp.moveaxis(q, 2, 0), jnp.moveaxis(k, 2, 0), jnp.moveaxis(u, 2, 0),
          jnp.moveaxis(w, 2, 0), jnp.moveaxis(gc, 2, 0), jnp.moveaxis(aqk, 2, 0))
    _, o = lax.scan(step, jnp.zeros((B, H, dk, dk), F32), xs)
    o = o.transpose(1, 0, 3, 2, 4).reshape(B, T, H, dk)
    o = rmsnorm(o, out_gain) * jax.nn.silu(z.reshape(B, T, H, dk).astype(F32))
    return o.astype(x.dtype).reshape(B, T, W) @ w_out

def rg_lru_block(x, w_in, conv_w, conv_b, w_a, b_a, w_x, b_x, lam, w_out):
    B, T, _ = x.shape
    gate, rec = jnp.split(x @ w_in, 2, axis=-1)
    gate = jax.nn.gelu(gate, approximate=True)
    xr = causal_depthwise_conv(rec, conv_w) + conv_b
    xb = xr.reshape(B, T, LRU_BLOCKS, -1)
    r = jax.nn.sigmoid((jnp.einsum('btnc,ncd->btnd', xb, w_a).reshape(B, T, -1) + b_a).astype(F32))
    i = jax.nn.sigmoid((jnp.einsum('btnc,ncd->btnd', xb, w_x).reshape(B, T, -1) + b_x).astype(F32))
    log_a = -LRU_C * r * jax.nn.softplus(-lam.astype(F32))
    a = jnp.exp(log_a)
    bterm = jnp.sqrt(1.0 - jnp.exp(2.0 * log_a)) * (i * xr.astype(F32))
    _, h = lax.associative_scan(lambda c1, c2: (c1[0] * c2[0], c2[0] * c1[1] + c2[1]), (a, bterm), axis=1)
    return (h.astype(x.dtype) * gate) @ w_out

def hier_moe(x, w_group, b_group, w_router, b_router, w_gate, w_up, w_down):
    B, T, D = x.shape
    n_tok = B * T
    xt = x.reshape(n_tok, D)
    logit_g = (xt @ w_group + b_group).astype(F32)
    prob_g = jax.nn.softmax(logit_g, -1)
    g_sel = jnp.argmax(logit_g, -1)
    gate_g = jnp.take_along_axis(prob_g, g_sel[:, None], -1)
    logit_e = (xt @ w_router + b_router).astype(F32).reshape(n_tok, N_GROUPS, EXPERTS_PER_GROUP)
    logit_e = jnp.take_along_axis(logit_e, g_sel[:, None, None], 1)[:, 0]
    top_v, top_i = lax.top_k(jax.nn.softmax(logit_e, -1), TOP_K_IN_GROUP)
    top_v = top_v / jnp.sum(top_v, -1, keepdims=True)
    w_in_group = jnp.sum(jax.nn.one_hot(top_i, EXPERTS_PER_GROUP, dtype=F32) * top_v[..., None], 1) * gate_g
    combine = jax.nn.one_hot(g_sel, N_GROUPS, dtype=F32)[:, :, None] * w_in_group[:, None, :]
    y = jnp.zeros_like(xt)
    for g in range(N_GROUPS):
        e = slice(g * EXPERTS_PER_GROUP, (g + 1) * EXPERTS_PER_GROUP)
        h = jax.nn.silu(jnp.einsum('nd,edf->nef', xt, w_gate[e])) * jnp.einsum('nd,edf->nef', xt, w_up[e])
        h = h * combine[:, g, :, None].astype(h.dtype)
        y = y + jnp.einsum('nef,efd->nd', h, w_down[e])
    return y.reshape(B, T, D)

def first_inputs(seed: int = 0) -> dict:
    key = jax.random.key(seed)
    keys = iter(jax.random.split(key, 48))

    def normal(shape, scale):
        return jax.random.normal(next(keys), shape, F32) * scale

    def gain(shape):
        return 1.0 + normal(shape, 0.02)

    def uniform(shape, lo, hi):
        return jax.random.uniform(next(keys), shape, F32, minval=lo, maxval=hi)

    nA, nB, nC, nD = [len(range(m, DEPTH, N_MIXERS)) for m in range(N_MIXERS)]
    D = D_MODEL
    rs = (2 * DEPTH) ** -0.5
    x = normal((BATCH, SEQ, D), 1.0)
    norm_mix = gain((DEPTH, D))
    norm_ffn = gain((DEPTH, D))
    da_w_in = normal((nA, D, DA_IN_WIDTH), D ** -0.5)
    da_q_norm = gain((nA, DA_HEAD_DIM))
    da_k_norm = gain((nA, DA_HEAD_DIM))
    da_lambda_q1 = normal((nA, DA_HEAD_DIM), 0.1)
    da_lambda_k1 = normal((nA, DA_HEAD_DIM), 0.1)
    da_lambda_q2 = normal((nA, DA_HEAD_DIM), 0.1)
    da_lambda_k2 = normal((nA, DA_HEAD_DIM), 0.1)
    da_subln = gain((nA, 2 * DA_HEAD_DIM))
    da_w_out = normal((nA, DA_HEADS * 2 * DA_HEAD_DIM, D), (DA_HEADS * 2 * DA_HEAD_DIM) ** -0.5 * rs)
    nsa_w_in = normal((nB, D, NSA_IN_WIDTH), D ** -0.5)
    nsa_q_norm = gain((nB, NSA_HEAD_DIM))
    nsa_k_norm = gain((nB, 3, NSA_HEAD_DIM))
    nsa_cmp_pos = normal((nB, 2, CMP_BLOCK, NSA_HEAD_DIM), 0.1)
    nsa_cmp_w1 = normal((nB, 2, CMP_BLOCK * NSA_HEAD_DIM, CMP_HIDDEN), (CMP_BLOCK * NSA_HEAD_DIM) ** -0.5)
    nsa_cmp_w2 = normal((nB, 2, CMP_HIDDEN, NSA_HEAD_DIM), CMP_HIDDEN ** -0.5)
    nsa_w_out = normal((nB, NSA_HEADS * NSA_HEAD_DIM, D), (NSA_HEADS * NSA_HEAD_DIM) ** -0.5 * rs)
    gdn_w_in = normal((nC, D, GDN_IN_WIDTH), D ** -0.5)
    gdn_conv_w = normal((nC, CONV_WIDTH, 3 * GDN_HEADS * GDN_HEAD_DIM), CONV_WIDTH ** -0.5)
    gdn_a_log = jnp.log(uniform((nC, GDN_HEADS), 1.0, 16.0))
    dt = jnp.exp(uniform((nC, GDN_HEADS), math.log(1e-3), math.log(0.1)))
    gdn_dt_bias = dt + jnp.log(-jnp.expm1(-dt))
    gdn_out_norm = gain((nC, GDN_HEAD_DIM))
    gdn_w_out = normal((nC, GDN_HEADS * GDN_HEAD_DIM, D), (GDN_HEADS * GDN_HEAD_DIM) ** -0.5 * rs)
    bw = LRU_WIDTH // LRU_BLOCKS
    lru_w_in = normal((nD, D, 2 * LRU_WIDTH), D ** -0.5)
    lru_conv_w = normal((nD, CONV_WIDTH, LRU_WIDTH), CONV_WIDTH ** -0.5)
    lru_conv_b = normal((nD, LRU_WIDTH), 0.1)
    lru_w_a = normal((nD, LRU_BLOCKS, bw, bw), bw ** -0.5)
    lru_b_a = normal((nD, LRU_WIDTH), 0.1)
    lru_w_x = normal((nD, LRU_BLOCKS, bw, bw), bw ** -0.5)
    lru_b_x = normal((nD, LRU_WIDTH), 0.1)
    a_c = uniform((nD, LRU_WIDTH), 0.9, 0.999)
    a0 = a_c ** (1.0 / LRU_C)
    lru_lambda = jnp.log(a0) - jnp.log1p(-a0)
    lru_w_out = normal((nD, LRU_WIDTH, D), LRU_WIDTH ** -0.5 * rs)
    moe_w_group = normal((DEPTH, D, N_GROUPS), D ** -0.5)
    moe_b_group = normal((DEPTH, N_GROUPS), 0.01)
    moe_w_router = normal((DEPTH, D, N_EXPERTS), D ** -0.5)
    moe_b_router = normal((DEPTH, N_EXPERTS), 0.01)
    moe_w_gate = normal((DEPTH, N_EXPERTS, D, D_EXPERT), D ** -0.5)
    moe_w_up = normal((DEPTH, N_EXPERTS, D, D_EXPERT), D ** -0.5)
    moe_w_down = normal((DEPTH, N_EXPERTS, D_EXPERT, D), D_EXPERT ** -0.5 * rs)
    return {'x': x, 'norm_mix': norm_mix, 'norm_ffn': norm_ffn,
            'da_w_in': da_w_in, 'da_q_norm': da_q_norm, 'da_k_norm': da_k_norm,
            'da_lambda_q1': da_lambda_q1, 'da_lambda_k1': da_lambda_k1,
            'da_lambda_q2': da_lambda_q2, 'da_lambda_k2': da_lambda_k2,
            'da_subln': da_subln, 'da_w_out': da_w_out,
            'nsa_w_in': nsa_w_in, 'nsa_q_norm': nsa_q_norm, 'nsa_k_norm': nsa_k_norm,
            'nsa_cmp_pos': nsa_cmp_pos, 'nsa_cmp_w1': nsa_cmp_w1, 'nsa_cmp_w2': nsa_cmp_w2,
            'nsa_w_out': nsa_w_out,
            'gdn_w_in': gdn_w_in, 'gdn_conv_w': gdn_conv_w, 'gdn_a_log': gdn_a_log,
            'gdn_dt_bias': gdn_dt_bias, 'gdn_out_norm': gdn_out_norm, 'gdn_w_out': gdn_w_out,
            'lru_w_in': lru_w_in, 'lru_conv_w': lru_conv_w, 'lru_conv_b': lru_conv_b,
            'lru_w_a': lru_w_a, 'lru_b_a': lru_b_a, 'lru_w_x': lru_w_x, 'lru_b_x': lru_b_x,
            'lru_lambda': lru_lambda, 'lru_w_out': lru_w_out,
            'moe_w_group': moe_w_group, 'moe_b_group': moe_b_group,
            'moe_w_router': moe_w_router, 'moe_b_router': moe_b_router,
            'moe_w_gate': moe_w_gate, 'moe_w_up': moe_w_up, 'moe_w_down': moe_w_down}

def first_block(x, norm_mix, norm_ffn,
              da_w_in, da_q_norm, da_k_norm, da_lambda_q1, da_lambda_k1, da_lambda_q2, da_lambda_k2,
              da_subln, da_w_out,
              nsa_w_in, nsa_q_norm, nsa_k_norm, nsa_cmp_pos, nsa_cmp_w1, nsa_cmp_w2, nsa_w_out,
              gdn_w_in, gdn_conv_w, gdn_a_log, gdn_dt_bias, gdn_out_norm, gdn_w_out,
              lru_w_in, lru_conv_w, lru_conv_b, lru_w_a, lru_b_a, lru_w_x, lru_b_x, lru_lambda, lru_w_out,
              moe_w_group, moe_b_group, moe_w_router, moe_b_router, moe_w_gate, moe_w_up, moe_w_down):
    for i in range(DEPTH):
        m, j = i % N_MIXERS, i // N_MIXERS
        h = rmsnorm(x, norm_mix[i])
        if m == 0:
            y = diff_attention(h, da_w_in[j], da_q_norm[j], da_k_norm[j], da_lambda_q1[j], da_lambda_k1[j],
                               da_lambda_q2[j], da_lambda_k2[j], da_subln[j], da_w_out[j],
                               0.8 - 0.6 * math.exp(-0.3 * i))
        elif m == 1:
            y = nsa_attention(h, nsa_w_in[j], nsa_q_norm[j], nsa_k_norm[j], nsa_cmp_pos[j],
                              nsa_cmp_w1[j], nsa_cmp_w2[j], nsa_w_out[j])
        elif m == 2:
            y = gated_deltanet(h, gdn_w_in[j], gdn_conv_w[j], gdn_a_log[j], gdn_dt_bias[j],
                               gdn_out_norm[j], gdn_w_out[j])
        else:
            y = rg_lru_block(h, lru_w_in[j], lru_conv_w[j], lru_conv_b[j], lru_w_a[j], lru_b_a[j],
                             lru_w_x[j], lru_b_x[j], lru_lambda[j], lru_w_out[j])
        x = x + y
        x = x + hier_moe(rmsnorm(x, norm_ffn[i]), moe_w_group[i], moe_b_group[i], moe_w_router[i],
                         moe_b_router[i], moe_w_gate[i], moe_w_up[i], moe_w_down[i])
    return x


DEPTH_2 = 2

CHUNK = 64
HEAD_DIM = 64
ROPE_THETA = 10000.0
EPS = 1e-6
NEG = -1e30

A_HEADS = 8
IDX_HEADS = 4
IDX_DIM = 64
IDX_TOPK_MAX = 256
B_HEADS = 8
B_PAST_CHUNKS = 8
B_REL_CLIP = 256
C_HEADS = 8
D_HEADS = 8
D_KV_HEADS = 2
D_GROUP = D_HEADS // D_KV_HEADS
D_WINDOW = 128
D_WINDOW_CHUNKS = -(-D_WINDOW // CHUNK)
D_FF = 2816
CONV_WIDTH_2 = 3

N_EVEN = (DEPTH_2 + 1) // 2
N_ODD = DEPTH_2 // 2

EVEN_SPLITS = (A_HEADS * HEAD_DIM, A_HEADS * HEAD_DIM, A_HEADS * HEAD_DIM,
               IDX_HEADS * IDX_DIM, IDX_DIM, IDX_HEADS,
               B_HEADS * HEAD_DIM, B_HEADS * HEAD_DIM, B_HEADS * HEAD_DIM)
ODD_SPLITS = (C_HEADS * HEAD_DIM, C_HEADS * HEAD_DIM, C_HEADS * HEAD_DIM, C_HEADS,
              D_HEADS * HEAD_DIM, D_KV_HEADS * HEAD_DIM, D_KV_HEADS * HEAD_DIM)
EVEN_IN = sum(EVEN_SPLITS)
ODD_IN = sum(ODD_SPLITS)
EVEN_OUT = (A_HEADS + B_HEADS) * HEAD_DIM
ODD_OUT = (C_HEADS + D_HEADS) * HEAD_DIM


def _split(t, sizes):
    return jnp.split(t, np.cumsum(sizes)[:-1].tolist(), axis=-1)

def rms_norm(x, g):
    xf = x.astype(jnp.float32)
    y = xf * lax.rsqrt(jnp.mean(xf * xf, axis=-1, keepdims=True) + EPS)
    return (y * g.astype(jnp.float32)).astype(x.dtype)

def layer_norm(x, g, b):
    xf = x.astype(jnp.float32)
    xc = xf - jnp.mean(xf, axis=-1, keepdims=True)
    y = xc * lax.rsqrt(jnp.mean(xc * xc, axis=-1, keepdims=True) + EPS)
    return (y * g.astype(jnp.float32) + b.astype(jnp.float32)).astype(x.dtype)

def rope_tables(seq, dim):
    inv = 1.0 / (ROPE_THETA ** (jnp.arange(0, dim, 2, dtype=jnp.float32) / dim))
    ang = jnp.arange(seq, dtype=jnp.float32)[:, None] * inv[None, :]
    return jnp.cos(ang), jnp.sin(ang)

def apply_rope(t, cos, sin):
    half = t.shape[-1] // 2
    shape = (1, t.shape[1]) + (1,) * (t.ndim - 3) + (half,)
    c = cos.reshape(shape)
    s = sin.reshape(shape)
    tf = t.astype(jnp.float32)
    t1, t2 = tf[..., :half], tf[..., half:]
    return jnp.concatenate([t1 * c - t2 * s, t2 * c + t1 * s], axis=-1).astype(t.dtype)

def dsa_sparse_attention(q, k, v, q_idx, k_idx, w_idx):
    bsz, seq, nh, dh = q.shape
    topk = min(IDX_TOPK_MAX, seq // 4)
    key_chunk = jnp.arange(seq) // CHUNK
    scale = dh ** -0.5

    def block(i):
        start = i * QBLOCK
        qb = lax.dynamic_slice_in_dim(q, start, QBLOCK, 1)
        qib = lax.dynamic_slice_in_dim(q_idx, start, QBLOCK, 1)
        wib = lax.dynamic_slice_in_dim(w_idx, start, QBLOCK, 1).astype(jnp.float32)
        q_chunk = (start + jnp.arange(QBLOCK)) // CHUNK
        admissible = key_chunk[None, :] <= q_chunk[:, None]
        rel = jax.nn.relu(jnp.einsum('bqhd,bsd->bqhs', qib, k_idx).astype(jnp.float32))
        score = jnp.einsum('bqhs,bqh->bqs', rel, wib)
        score = jnp.where(admissible[None], score, NEG)
        _, idx = lax.top_k(score, topk)
        valid = key_chunk[idx] <= q_chunk[None, :, None]
        k_sel = jax.vmap(lambda kb, ib: kb[ib])(k, idx)
        v_sel = jax.vmap(lambda vb, ib: vb[ib])(v, idx)
        logits = jnp.einsum('bqhd,bqkhd->bhqk', qb, k_sel).astype(jnp.float32) * scale
        logits = jnp.where(valid[:, None], logits, NEG)
        p = jax.nn.softmax(logits, axis=-1).astype(v.dtype)
        return jnp.einsum('bhqk,bqkhd->bqhd', p, v_sel)

    out = lax.map(block, jnp.arange(seq // QBLOCK))
    return jnp.moveaxis(out, 0, 1).reshape(bsz, seq, nh, dh)

def chunked_relpos_attention(q, k, v, rel_bias):
    bsz, seq, nh, dh = q.shape
    pad = B_PAST_CHUNKS * CHUNK
    band = pad + CHUNK
    kp = jnp.pad(k, ((0, 0), (pad, 0), (0, 0), (0, 0)))
    vp = jnp.pad(v, ((0, 0), (pad, 0), (0, 0), (0, 0)))
    kj = jnp.arange(band)
    dist = jnp.arange(CHUNK)[:, None] + pad - kj[None, :]
    bias = rel_bias[:, jnp.clip(dist, -B_REL_CLIP, B_REL_CLIP) + B_REL_CLIP].astype(jnp.float32)
    scale = dh ** -0.5

    def chunk(c):
        start = c * CHUNK
        qc = lax.dynamic_slice_in_dim(q, start, CHUNK, 1)
        kc = lax.dynamic_slice_in_dim(kp, start, band, 1)
        vc = lax.dynamic_slice_in_dim(vp, start, band, 1)
        valid = kj >= pad - start
        logits = jnp.einsum('bqhd,bshd->bhqs', qc, kc).astype(jnp.float32) * scale + bias[None]
        logits = jnp.where(valid, logits, NEG)
        p = jax.nn.softmax(logits, axis=-1).astype(v.dtype)
        return jnp.einsum('bhqs,bshd->bqhd', p, vc)

    out = lax.map(chunk, jnp.arange(seq // CHUNK))
    return jnp.moveaxis(out, 0, 1).reshape(bsz, seq, nh, dh)

def forgetting_attention(q, k, v, log_f):
    bsz, seq, nh, dh = q.shape
    f_cum = jnp.moveaxis(lax.cumsum(log_f, axis=1), 1, 2)
    pos = jnp.arange(seq)
    scale = dh ** -0.5

    def block(i):
        start = i * QBLOCK
        qb = lax.dynamic_slice_in_dim(q, start, QBLOCK, 1)
        fq = lax.dynamic_slice_in_dim(f_cum, start, QBLOCK, 2)
        causal = pos[None, :] <= (start + jnp.arange(QBLOCK))[:, None]
        logits = (jnp.einsum('bqhd,bshd->bhqs', qb, k).astype(jnp.float32) * scale
                  + fq[..., None] - f_cum[:, :, None, :])
        logits = jnp.where(causal, logits, NEG)
        p = jax.nn.softmax(logits, axis=-1).astype(v.dtype)
        return jnp.einsum('bhqs,bshd->bqhd', p, v)

    out = lax.map(block, jnp.arange(seq // QBLOCK))
    return jnp.moveaxis(out, 0, 1).reshape(bsz, seq, nh, dh)

def sink_window_gqa(q, k, v, sinks):
    bsz, seq, nh, dh = q.shape
    nb = seq // QBLOCK
    qb = q.reshape(bsz, nb, QBLOCK, D_KV_HEADS, D_GROUP, dh)
    kb = k.reshape(bsz, nb, QBLOCK, D_KV_HEADS, dh)
    vb = v.reshape(bsz, nb, QBLOCK, D_KV_HEADS, dh)
    kprev = jnp.pad(kb, ((0, 0), (1, 0), (0, 0), (0, 0), (0, 0)))[:, :-1]
    vprev = jnp.pad(vb, ((0, 0), (1, 0), (0, 0), (0, 0), (0, 0)))[:, :-1]
    kband = jnp.concatenate([kprev, kb], axis=2)
    vband = jnp.concatenate([vprev, vb], axis=2)
    sk = jnp.arange(2 * QBLOCK) - QBLOCK
    cdiff = jnp.arange(QBLOCK)[:, None] // CHUNK - sk[None, :] // CHUNK
    band_mask = (cdiff >= 0) & (cdiff <= D_WINDOW_CHUNKS)
    mask = band_mask[None] & ((jnp.arange(nb)[:, None, None] > 0) | (sk >= 0)[None, None, :])
    logits = jnp.einsum('bnqkgd,bnskd->bnkgqs', qb, kband).astype(jnp.float32) * (dh ** -0.5)
    logits = jnp.where(mask[None, :, None, None], logits, NEG)
    sink_col = jnp.broadcast_to(
        sinks.reshape(D_KV_HEADS, D_GROUP).astype(jnp.float32)[None, None, :, :, None, None],
        logits.shape[:-1] + (1,))
    p = jax.nn.softmax(jnp.concatenate([logits, sink_col], axis=-1), axis=-1)[..., :-1]
    out = jnp.einsum('bnkgqs,bnskd->bnqkgd', p.astype(v.dtype), vband)
    return out.reshape(bsz, seq, nh, dh)

def conv_gated_ffn(x, w_up, conv_w, conv_b, w_down):
    h = x @ w_up
    c = h.shape[-1]
    h = lax.conv_general_dilated(
        h, conv_w.reshape(CONV_WIDTH_2, 1, c).astype(h.dtype), window_strides=(1,),
        padding=[(CONV_WIDTH_2 - 1, 0)], dimension_numbers=('NWC', 'WIO', 'NWC'),
        feature_group_count=c) + conv_b.astype(h.dtype)
    g, u = jnp.split(h, 2, axis=-1)
    return (jax.nn.silu(g) * u) @ w_down

def even_mixer(xn, w_in, w_out, k_ln_g, k_ln_b, rel_bias, rope_h, rope_i):
    bsz, seq, _ = xn.shape
    qa, ka, va, qi, ki, wi, qb, kb, vb = _split(xn @ w_in, EVEN_SPLITS)
    heads = lambda t, n: t.reshape(bsz, seq, n, HEAD_DIM)
    qa = apply_rope(heads(qa, A_HEADS), *rope_h)
    ka = apply_rope(heads(ka, A_HEADS), *rope_h)
    qi = apply_rope(qi.reshape(bsz, seq, IDX_HEADS, IDX_DIM), *rope_i)
    ki = apply_rope(layer_norm(ki, k_ln_g, k_ln_b), *rope_i)
    ya = dsa_sparse_attention(qa, ka, heads(va, A_HEADS), qi, ki, wi)
    yb = chunked_relpos_attention(heads(qb, B_HEADS), heads(kb, B_HEADS), heads(vb, B_HEADS), rel_bias)
    y = jnp.concatenate([ya.reshape(bsz, seq, -1), yb.reshape(bsz, seq, -1)], axis=-1)
    return y @ w_out

def odd_mixer(xn, w_in, w_out, forget_b, sinks, rope_h):
    bsz, seq, _ = xn.shape
    qc, kc, vc, fc, qd, kd, vd = _split(xn @ w_in, ODD_SPLITS)
    heads = lambda t, n: t.reshape(bsz, seq, n, HEAD_DIM)
    log_f = jax.nn.log_sigmoid(fc.astype(jnp.float32) + forget_b.astype(jnp.float32))
    yc = forgetting_attention(heads(qc, C_HEADS), heads(kc, C_HEADS), heads(vc, C_HEADS), log_f)
    yd = sink_window_gqa(apply_rope(heads(qd, D_HEADS), *rope_h),
                         apply_rope(heads(kd, D_KV_HEADS), *rope_h),
                         heads(vd, D_KV_HEADS), sinks)
    y = jnp.concatenate([yc.reshape(bsz, seq, -1), yd.reshape(bsz, seq, -1)], axis=-1)
    return y @ w_out

def second_inputs(seed: int = 0) -> dict:
    key = jax.random.key(seed)
    ks = jax.random.split(key, 17)
    f32 = jnp.float32
    nrm = lambda k, shape, s: jax.random.normal(k, shape, f32) * s
    return {
        'x': nrm(ks[0], (BATCH, SEQ, D_MODEL), 1.0),
        'norm_mix_g': 1.0 + nrm(ks[1], (DEPTH_2, D_MODEL), 0.1),
        'norm_ffn_g': 1.0 + nrm(ks[2], (DEPTH_2, D_MODEL), 0.1),
        'norm_out_g': 1.0 + nrm(ks[3], (D_MODEL,), 0.1),
        'even_w_in': nrm(ks[4], (N_EVEN, D_MODEL, EVEN_IN), D_MODEL ** -0.5),
        'even_w_out': nrm(ks[5], (N_EVEN, EVEN_OUT, D_MODEL), EVEN_OUT ** -0.5),
        'idx_k_ln_g': 1.0 + nrm(ks[6], (N_EVEN, IDX_DIM), 0.1),
        'idx_k_ln_b': nrm(ks[7], (N_EVEN, IDX_DIM), 0.02),
        'rel_bias': nrm(ks[8], (N_EVEN, B_HEADS, 2 * B_REL_CLIP + 1), 0.5),
        'odd_w_in': nrm(ks[9], (N_ODD, D_MODEL, ODD_IN), D_MODEL ** -0.5),
        'odd_w_out': nrm(ks[10], (N_ODD, ODD_OUT, D_MODEL), ODD_OUT ** -0.5),
        'forget_b': jax.random.uniform(ks[11], (N_ODD, C_HEADS), f32, 1.0, 5.0),
        'sinks': nrm(ks[12], (N_ODD, D_HEADS), 1.0),
        'ffn_w_up': nrm(ks[13], (DEPTH_2, D_MODEL, 2 * D_FF), D_MODEL ** -0.5),
        'ffn_conv_w': nrm(ks[14], (DEPTH_2, CONV_WIDTH_2, 2 * D_FF), CONV_WIDTH_2 ** -0.5),
        'ffn_conv_b': nrm(ks[15], (DEPTH_2, 2 * D_FF), 0.02),
        'ffn_w_down': nrm(ks[16], (DEPTH_2, D_FF, D_MODEL), D_FF ** -0.5),
    }

def second_block(x, norm_mix_g, norm_ffn_g, norm_out_g, even_w_in, even_w_out, idx_k_ln_g, idx_k_ln_b,
              rel_bias, odd_w_in, odd_w_out, forget_b, sinks, ffn_w_up, ffn_conv_w, ffn_conv_b, ffn_w_down):
    seq = x.shape[1]
    rope_h = rope_tables(seq, HEAD_DIM)
    rope_i = rope_tables(seq, IDX_DIM)
    h = x
    for layer in range(DEPTH_2):
        j = layer // 2
        xn = rms_norm(h, norm_mix_g[layer])
        if layer % 2 == 0:
            mix = even_mixer(xn, even_w_in[j], even_w_out[j], idx_k_ln_g[j], idx_k_ln_b[j],
                             rel_bias[j], rope_h, rope_i)
        else:
            mix = odd_mixer(xn, odd_w_in[j], odd_w_out[j], forget_b[j], sinks[j], rope_h)
        h = h + mix
        h = h + conv_gated_ffn(rms_norm(h, norm_ffn_g[layer]), ffn_w_up[layer], ffn_conv_w[layer],
                               ffn_conv_b[layer], ffn_w_down[layer])
    return rms_norm(h, norm_out_g)


def setup_inputs(seed=0):
    out = dict(first_inputs(seed))
    for name, value in second_inputs(seed + 1).items():
        if name != "x":
            out[name + "_2"] = value
    return out


def reference(
    x, norm_mix, norm_ffn, da_w_in, da_q_norm, da_k_norm, da_lambda_q1, da_lambda_k1,
    da_lambda_q2, da_lambda_k2, da_subln, da_w_out, nsa_w_in, nsa_q_norm, nsa_k_norm,
    nsa_cmp_pos, nsa_cmp_w1, nsa_cmp_w2, nsa_w_out, gdn_w_in, gdn_conv_w, gdn_a_log,
    gdn_dt_bias, gdn_out_norm, gdn_w_out, lru_w_in, lru_conv_w, lru_conv_b, lru_w_a, lru_b_a,
    lru_w_x, lru_b_x, lru_lambda, lru_w_out, moe_w_group, moe_b_group, moe_w_router,
    moe_b_router, moe_w_gate, moe_w_up, moe_w_down, norm_mix_g_2, norm_ffn_g_2, norm_out_g_2,
    even_w_in_2, even_w_out_2, idx_k_ln_g_2, idx_k_ln_b_2, rel_bias_2, odd_w_in_2, odd_w_out_2,
    forget_b_2, sinks_2, ffn_w_up_2, ffn_conv_w_2, ffn_conv_b_2, ffn_w_down_2,
):
    x = first_block(
        x, norm_mix, norm_ffn, da_w_in, da_q_norm, da_k_norm, da_lambda_q1, da_lambda_k1,
        da_lambda_q2, da_lambda_k2, da_subln, da_w_out, nsa_w_in, nsa_q_norm, nsa_k_norm,
        nsa_cmp_pos, nsa_cmp_w1, nsa_cmp_w2, nsa_w_out, gdn_w_in, gdn_conv_w, gdn_a_log,
        gdn_dt_bias, gdn_out_norm, gdn_w_out, lru_w_in, lru_conv_w, lru_conv_b, lru_w_a,
        lru_b_a, lru_w_x, lru_b_x, lru_lambda, lru_w_out, moe_w_group, moe_b_group,
        moe_w_router, moe_b_router, moe_w_gate, moe_w_up, moe_w_down,
    )
    return second_block(
        x, norm_mix_g_2, norm_ffn_g_2, norm_out_g_2, even_w_in_2, even_w_out_2, idx_k_ln_g_2,
        idx_k_ln_b_2, rel_bias_2, odd_w_in_2, odd_w_out_2, forget_b_2, sinks_2, ffn_w_up_2,
        ffn_conv_w_2, ffn_conv_b_2, ffn_w_down_2,
    )


_drawn_inputs = setup_inputs


def setup_inputs(seed=0):
    import zlib

    import numpy as np

    out = dict(_drawn_inputs(seed))
    spreads = {}
    factors = {'da_q_norm': 3.175,
     'da_k_norm': 2.86,
     'da_lambda_k2': 5.115,
     'moe_b_group': 3.511,
     'moe_b_router': 16.874,
     'idx_k_ln_b_2': 45.192,
     'sinks_2': 37.552,
     'ffn_conv_b_2': 8.668,
     'norm_ffn': 3.338,
     'norm_mix_g_2': 3.858,
     'idx_k_ln_g_2': 8.0,
     'rel_bias_2': 4.61}
    for name, (base, spread) in spreads.items():
        noise = np.random.default_rng([zlib.crc32(name.encode()), seed]).standard_normal(out[name].shape)
        drawn = base * np.exp(spread * noise) if base else spread * noise
        out[name] = jnp.asarray(drawn.astype(out[name].dtype))
    for name, factor in factors.items():
        out[name] = (out[name] * factor).astype(out[name].dtype)
    return out
```

```python
from contextlib import ExitStack

import numpy as np

import concourse.bass as bass
from concourse import mybir

F32 = mybir.dt.float32
F32R = mybir.dt.float32r
I32 = mybir.dt.int32
U32 = mybir.dt.uint32
ALU = mybir.AluOpType
ACT = mybir.ActivationFunctionType
AX_X = mybir.AxisListType.X

P = 128
T = 512
D = 1024
DC = D // P
TT = T // P
EPS = 1e-6
NEG = -1e30
HUGE = 3e38
TAKEN = -3e38
LAMBDA_INIT = 0.2
HD = 64
QK_SCALE = HD ** -0.5
N_EXP, N_GRP, EPG, D_EXP = 16, 4, 4, 512
PAIRS = 2 * T
MAX_TILES = PAIRS // P + N_EXP - 1
FF = 2816
FC = FF // P
TOPK = min(256, T // 4)
CHUNK = 64

OFF = [0, 128, 384, 768]
PW = 1280

CONSTS = {}
_at = 0
for _n, _w in [("ident", P), ("blk64", P), ("inv_d", P), ("inv_p", P), ("rot", P), ("tri", P), ("ones", P),
               ("cmask", P), ("cband", T), ("sband", 2 * P), ("cos", T), ("sin", T), ("tileid", 24 * N_EXP)]:
    CONSTS[_n] = (_at, _at + _w)
    _at += _w
N_CONST = _at

PARAMS = {}
_at = 0
for _n, _w in [("g_mix", DC), ("g_ffn", DC), ("g_mix2", 2 * DC), ("g_ffn2", 2 * DC), ("g_out", DC), ("qg", 1),
               ("kg", 1), ("subln", 1), ("lng", 1), ("lnb", 1), ("convw", 2 * 2 * FC * 3), ("convb", 2 * 2 * FC),
               ("sinks", 8), ("fb", 1), ("rb", 20), ("lam", 4 * HD)]:
    PARAMS[_n] = (_at, _at + _w)
    _at += _w
N_PARAM = _at


def shape_constants():
    c = np.zeros((P, N_CONST), np.float32)

    def put(name, value):
        a, b = CONSTS[name]
        c[:, a:b] = value

    p = np.arange(P)
    put("ident", np.eye(P))
    put("blk64", (p[:, None] // HD == p[None, :] // HD) / HD)
    put("inv_d", 1.0 / D)
    put("inv_p", 1.0 / P)
    rot = np.zeros((P, P))
    for m in range(P):
        if m % HD < HD // 2:
            rot[m + HD // 2, m] = -1.0
        else:
            rot[m - HD // 2, m] = 1.0
    put("rot", rot)
    put("tri", p[:, None] < p[None, :])
    put("ones", 1.0)
    later = np.where(p[None, :] // CHUNK <= p[:, None] // CHUNK, 0.0, NEG)
    put("cmask", later)
    band = np.arange(T)[None, :] - (T - P)
    dist = p[:, None] - band
    put("cband", np.where(dist >= 0, 0.0, NEG))
    window = np.arange(2 * P)[None, :] - P
    gap = p[:, None] // CHUNK - window // CHUNK
    put("sband", np.where((gap >= 0) & (gap <= 2), 0.0, NEG))
    inv = (1.0 / (np.float32(10000.0) ** (np.arange(0, HD, 2, dtype=np.float32) / np.float32(HD)))).astype(np.float32)
    ang = (np.arange(T, dtype=np.float32)[:, None] * inv[None, :]).astype(np.float32)
    put("cos", np.cos(ang).T[p % (HD // 2)])
    put("sin", np.sin(ang).T[p % (HD // 2)])
    put("tileid", np.repeat(np.arange(24), N_EXP)[None, :])
    slopes = (2.0 ** (-8.0 * np.arange(1, 9) / 8)).astype(np.float32)
    alibi = np.where(dist >= 0, -slopes[:, None, None] * dist.astype(np.float32), np.float32(NEG)).astype(np.float32)
    rec = np.zeros((P, 2, TT, 4), np.int32)
    tok = np.arange(TT)[None, :] * P + p[:, None]
    for k in range(2):
        rec[:, k, :, 0] = tok
        rec[:, k, :, 1] = k * T + tok
    empty = np.zeros((24 * P, 4), np.int32)
    empty[:, 0] = T
    empty[:, 1] = PAIRS
    return c, alibi, rec, empty


def emit_wait(eng, sem, value):
    if isinstance(value, int) and value <= 0:
        return
    eng.wait_ge(sem, value)


def wait_apart(eng, sem, value, passed):
    emit_wait(eng, sem, value)
    eng.sem_inc(passed, 1)


def repeat(eng, n, body, peel=1):
    for i in range(peel):
        body(i)
    with eng.Fori(peel, n) as i:
        body(i)


class Stage(ExitStack):

    def __init__(self, nc, name):
        super().__init__()
        self.nc, self.name, self.sems = nc, name, []

    def sem(self, name):
        s = self.nc.alloc_semaphore(f"{self.name}_{name}")
        self.sems.append(s)
        return s

    def dma_sem(self, name):
        return self.nc.alloc_semaphore(f"{self.name}_{name}")

    def __exit__(self, *exc):
        if exc[0] is None:
            for s in self.sems:
                self.nc.gpsimd.sem_clear(s)
                self.nc.release_semaphore(s)
        return super().__exit__(*exc)


class Chip:

    def __init__(self, nc, ctx, a):
        self.nc, self.ctx, self.a = nc, ctx, a

        def sb(name, shape, dt=F32):
            return ctx.enter_context(nc.sbuf_tensor(name, shape, dt))

        self.ps = ctx.enter_context(nc.psum_tensor("ps", [P, 8, 512], F32))
        self.const = sb("const", [P, N_CONST])
        self.param = sb("param", [P, N_PARAM])
        self.h = sb("h", [P, DC, T])
        self.eps = sb("eps", [P, 1])
        self.zero = sb("zero", [P, 1])

    def product(self, out, w, x, start, stop):
        (wh, wl), (xh, xl) = w, x
        mm = self.nc.tensor.matmul
        mm(out, wh, xh, start=start, stop=False)
        mm(out, wh, xl, start=False, stop=False)
        return mm(out, wl, xh, start=False, stop=stop)

    def k(self, name):
        x, y = CONSTS[name]
        return self.const[:, x:y]

    def p(self, name, i=0, n=None):
        x, y = PARAMS[name]
        return self.param[:, x + i:(y if n is None else x + i + n)]

    def bank(self, i):
        return self.ps[:, i, :]


def stage_load(c):
    nc, a = c.nc, c.a
    with Stage(nc, "load") as ctx:
        s_in, s_scratch = ctx.sem("in"), ctx.sem("scratch")
        with nc.Block("load") as block:
            @block.sync
            def _(sp):
                sp.dma_start(c.h[:, :, :], a["xT"]).then_inc(s_in, 16)
                sp.dma_start(c.param[:, :], a["params"]).then_inc(s_in, 16)
                sp.dma_start(c.const[:, :], a["consts"]).then_inc(s_in, 16)
                sp.wait_ge(s_in, 48)

            @block.scalar
            def _(act):
                act.dma_start(a["plist"], a["empty"]).then_inc(s_scratch, 16)
                act.dma_start(a["relrows"], bass.AP(a["relE"].tensor, 0, [[640, 8], [0, P], [1, 640]]))\
                   .then_inc(s_scratch, 16)
                act.wait_ge(s_scratch, 32)

            @block.vector
            def _(dve):
                nc.vector.memset(c.eps[:, :], EPS)
                nc.vector.memset(c.zero[:, :], 0.0)


def stage_norm(c, name, gain, x, xn=None):
    nc = c.nc
    with Stage(nc, name) as ctx:
        sem = ctx.sem
        sq = ctx.enter_context(nc.sbuf_tensor(f"{name}_sq", [P, DC, T], F32))
        lg = ctx.enter_context(nc.sbuf_tensor(f"{name}_lg", [P, T], F32))
        rs = ctx.enter_context(nc.sbuf_tensor(f"{name}_rs", [P, T], F32))
        y = sq if xn is None else xn
        squared, squared_v, summed, logged, inverted, scaled, rounded = (
            sem(n) for n in ("squared", "squared_v", "summed", "logged", "inverted", "scaled", "rounded"))
        with nc.Block(name) as block:
            @block.scalar
            def _(act):
                for i in range(0, DC, 2):
                    nc.scalar.activation(sq[:, i, :], c.h[:, i, :], ACT.Square).then_inc(squared, 1)
                act.wait_ge(summed, 1)
                nc.scalar.activation(lg[:, :], c.bank(0), ACT.Ln, bias=c.eps[:, 0:1]).then_inc(logged, 1)
                act.wait_ge(logged, 1)
                nc.scalar.activation(rs[:, :], lg[:, :], ACT.Exp, scale=-0.5).then_inc(inverted, 1)
                for i in range(DC):
                    act.wait_ge(scaled, i + 1)
                    nc.scalar.copy(x[0][:, i, :], y[:, i, :]).then_inc(rounded, 1)

            @block.tensor
            def _(pe):
                for i in range(DC):
                    pe.wait_ge((squared, squared_v)[i % 2], i // 2 + 1)
                    mm = nc.tensor.matmul(c.bank(0), c.k("inv_d"), sq[:, i, :], start=(i == 0), stop=(i == DC - 1))
                mm.then_inc(summed, 1)

            @block.vector
            def _(dve):
                for i in range(1, DC, 2):
                    nc.vector.tensor_tensor(sq[:, i, :], c.h[:, i, :], c.h[:, i, :], ALU.mult).then_inc(squared_v, 1)
                dve.wait_ge(inverted, 1)
                for i in range(DC):
                    nc.vector.scalar_tensor_tensor(out=y[:, i, :], in0=c.h[:, i, :], scalar=gain[:, i:i + 1],
                                                   in1=rs[:, :], op0=ALU.mult, op1=ALU.mult).then_inc(scaled, 1)
                    if i % 2:
                        dve.wait_ge(rounded, i)
                        nc.vector.tensor_tensor(x[1][:, i - 1, :], y[:, i - 1, :], x[0][:, i - 1, :].bitcast(F32),
                                                ALU.subtract)

            @block.gpsimd
            def _(pool):
                for i in range(1, DC, 2):
                    pool.wait_ge(rounded, i + 1)
                    nc.gpsimd.tensor_tensor(x[1][:, i, :], y[:, i, :], x[0][:, i, :].bitcast(F32), ALU.subtract)


def stage_back(c, name, w, src, nk):
    nc = c.nc
    with Stage(nc, name) as ctx:
        sem = ctx.sem
        slab = [ctx.enter_context(nc.sbuf_tensor(f"{name}_w{i}", [P, nk, P], F32)) for i in range(2)]
        high = [ctx.enter_context(nc.sbuf_tensor(f"{name}_wh{i}", [P, nk, P], F32R)) for i in range(2)]
        low = [ctx.enter_context(nc.sbuf_tensor(f"{name}_wl{i}", [P, nk, P], F32R)) for i in range(2)]
        w_in = [sem(f"w_in{i}") for i in range(2)]
        rounded, split, projected, added = sem("rounded"), sem("split"), sem("projected"), sem("added")
        with nc.Block(name) as block:
            @block.sync
            def _(sp):
                def load(i):
                    for b in range(2):
                        emit_wait(sp, split, 2 * i - 1 + b)
                        sp.dma_start(slab[b][:, :, :], w[bass.ds(2 * i + b, 1)].rearrange("a p k m -> (a p) k m"))\
                          .then_inc(w_in[b], 16)
                repeat(sp, DC // 2, load)

            @block.scalar
            def _(act):
                def round_(i):
                    for b in range(2):
                        act.wait_ge(w_in[b], 16 * i + 16)
                        emit_wait(act, projected, 2 * i - 1 + b)
                        nc.scalar.copy(high[b][:, :, :], slab[b][:, :, :]).then_inc(rounded, 1)
                repeat(act, DC // 2, round_)

            @block.gpsimd
            def _(pool):
                def rest(i):
                    for b in range(2):
                        pool.wait_ge(rounded, 2 * i + b + 1)
                        nc.gpsimd.tensor_tensor(low[b][:, :, :], slab[b][:, :, :], high[b][:, :, :].bitcast(F32),
                                                ALU.subtract).then_inc(split, 1)
                repeat(pool, DC // 2, rest)

            @block.tensor
            def _(pe):
                def project(i):
                    for b in range(2):
                        pe.wait_ge(split, 2 * i + b + 1)
                        emit_wait(pe, added, 2 * i - 1 + b)
                        for j in range(nk):
                            mm = c.product(c.bank(b), (high[b][:, j, :], low[b][:, j, :]),
                                           (src[0][:, j, :], src[1][:, j, :]), j == 0, j == nk - 1)
                        mm.then_inc(projected, 1)
                repeat(pe, DC // 2, project)

            @block.vector
            def _(dve):
                def add(i):
                    for b in range(2):
                        dve.wait_ge(projected, 2 * i + b + 1)
                        hc = c.h[:, bass.ds(2 * i + b, 1), :].rearrange("p a t -> p (a t)")
                        nc.vector.tensor_tensor(hc, c.bank(b), hc, ALU.add).then_inc(added, 1)
                repeat(dve, DC // 2, add)


def stage_attention(c, name, kind, n, w, x, first, bias=None):
    nc = c.nc
    diff, rope = kind == "diff", kind in ("dsa", "sink")
    banded = kind in ("diff", "rel")
    direct = kind in ("rel", "forget")
    comb = 1 if diff else 2
    order = [(3, 0), (3, 1), (2, 0), (2, 1), (1, 0), (0, 0), (1, 1), (0, 1)]
    col = {(3, 0): 0, (3, 1): 1, (2, 0): 2, (2, 1): 3, (1, 0): 4, (1, 1): 5, (0, 0): 6, (0, 1): 7}
    scored_at = [1, 2, 3, 4, 5, 5, 6, 6]
    seq = {t: i + 1 for i, t in enumerate(order)}

    def keys(qt):
        return (128 * max(qt - 1, 0) if kind == "sink" else 0), 128 * (qt + 1)

    def score_bank(qt, s):
        k0, k1 = keys(qt)
        if qt == 3:
            return c.ps[:, s, 0:k1 - k0]
        if qt == 2:
            return c.ps[:, 2 + s, 0:k1 - k0]
        return c.ps[:, s, 0:k1 - k0] if qt == 1 else c.ps[:, s, 256:384]

    with Stage(nc, name) as ctx:
        sem = ctx.sem
        sb = lambda x, shape: ctx.enter_context(nc.sbuf_tensor(f"{name}_{x}", shape, F32))
        slab = sb("w", [P, 3, DC, P])
        high, low = (ctx.enter_context(nc.sbuf_tensor(f"{name}_{i}", [P, 3, DC, P], F32R)) for i in ("wh", "wl"))
        qT, kT, v = sb("qT", [P, T]), sb("kT", [P, T]), sb("v", [P, TT, P])
        raw = None if direct else sb("raw", [P, 2, T])
        tmp = None if direct else sb("tmp", [P, 2, T])
        tmp2 = None if direct else sb("tmp2", [P, 2, T])
        prob = sb("prob", [P, 2, PW])
        probT = sb("probT", [P, comb, TT, T])
        btile = sb("btile", [P, 1 if diff else 2, T]) if banded else None
        nmax, total, inv = sb("nmax", [P, 8]), sb("total", [P, 8]), sb("inv", [P, 8])
        esink = sb("esink", [P, 8]) if kind == "sink" else None
        sink_u = sb("sink_u", [P, 2, 2]) if kind == "sink" else None
        (q_in, k_in, v_in, b_in, b_ok, q_proj, k_proj, v_proj, q_raw, k_raw, q_help, k_help, q_half, k_half, q_half2,
         k_half2, q_ok, k_ok, v_ok, scored, shifted, expd, inv_ok, inv2_ok, scaled, normed, turned, copied, pv_done,
         o_ok, sink_ok) = (
            sem(x) for x in ("q_in", "k_in", "v_in", "b_in", "b_ok", "q_proj", "k_proj", "v_proj", "q_raw", "k_raw",
                             "q_help", "k_help", "q_half", "k_half", "q_half2", "k_half2", "q_ok", "k_ok", "v_ok",
                             "scored", "shifted", "expd", "inv_ok", "inv2_ok", "scaled", "normed", "turned",
                             "copied", "pv_done", "o_ok", "sink_ok"))
        rounded, split = ([sem(f"{i}_{j}") for j in "qkv"] for i in ("rounded", "split"))
        o_high, logged = sem("o_high"), sem("logged")
        passed_pe, passed_dve = sem("passed_pe"), sem("passed_dve")
        ngrp = 4 if diff else 8

        def sl(s, qt):
            k0, k1 = keys(qt)
            return prob[:, s, OFF[qt]:OFF[qt] + k1 - k0]

        def bias_tile(s, qt):
            if kind == "diff":
                return btile[:, 0, T - P - P * qt:T]
            if kind == "rel":
                return btile[:, s, T - P - P * qt:T]
            return bias(s, qt)

        def rounds(body, eng):
            body(0, True, False, True)
            with eng.Fori(1, n - 1) as u:
                body(u, True, True, True)
            body(n - 1, True, True, False)
            body(n, False, True, False)

        with nc.Block(name) as block:
            @block.sync
            def _(sp):
                def load(u):
                    for i, landed in enumerate((q_in, k_in, v_in)):
                        emit_wait(sp, split[i], u)
                        src = w[bass.ds(u, 1), i] if not isinstance(u, int) else w[u:u + 1, i]
                        sp.dma_start(slab[:, i, :, :], src.rearrange("a p k m -> (a p) k m")).then_inc(landed, 16)
                    if banded:
                        emit_wait(sp, shifted, u * 8)
                        nb = 1 if diff else 2
                        src = bias[bass.ds(u * nb, nb)] if not isinstance(u, int) else bias[u * nb:(u + 1) * nb]
                        sp.dma_start(btile[:, :, :], src.rearrange("h p m -> p h m")).then_inc(b_in, 16)
                load(0)
                with sp.Fori(1, n) as u:
                    load(u)

            @block.gpsimd
            def _(pool):
                def rest(i, u):
                    pool.wait_ge(rounded[i], u + 1)
                    nc.gpsimd.tensor_tensor(low[:, i, :, :], slab[:, i, :, :], high[:, i, :, :].bitcast(F32),
                                            ALU.subtract).then_inc(split[i], 1)

                if kind == "rel":
                    def mask(u):
                        pool.wait_ge(b_in, 16 * u + 16)
                        for s in range(2):
                            d = btile[:, s, T - P:T]
                            nc.gpsimd.tensor_tensor(d, d, c.k("cmask"), ALU.add).then_inc(b_ok, 1)
                if rope:
                    def turn(u, i):
                        have, half, ready = ((q_raw, q_half, q_ok), (k_raw, k_half, k_ok))[i]
                        pool.wait_ge(have, u + 1)
                        emit_wait(pool, ready, u)
                        nc.gpsimd.tensor_tensor(tmp[:, i, :], raw[:, i, :], c.k("cos"), ALU.mult).then_inc(half, 1)

                def body(u, project, attend, ahead):
                    if kind == "rel" and project:
                        mask(u)
                    for i in range(3):
                        if ahead:
                            rest(i, u + 1)
                        if rope and project and i < 2:
                            turn(u, i)

                for i in range(3):
                    rest(i, 0)
                rounds(body, pool)

            @block.tensor
            def _(pe):
                def scores(u, tiles):
                    for qt, s in tiles:
                        k0, k1 = keys(qt)
                        out, hd = score_bank(qt, s), slice(HD * s, HD * s + HD)
                        if kind == "forget":
                            f = c.fneg[0:1, bass.ds(2 * (u - 1) + s, 1), k0:k1].rearrange("p a t -> p (a t)")
                            nc.tensor.matmul(out, c.k("ones")[0:1, :], f, start=True, stop=False)
                        mm = nc.tensor.matmul(out, qT[hd, P * qt:P * qt + P], kT[hd, k0:k1],
                                              start=(kind != "forget"), stop=True)
                        if qt != 1:
                            mm.then_inc(scored, 1)

                def turn(u, g):
                    for j in range(TT):
                        if g:
                            pe.wait_ge(copied, (u - 1) * 4 * comb + j + 1)
                        for qt in range(j, min(TT, j + 2) if kind == "sink" else TT):
                            k0, _ = keys(qt)
                            at = OFF[qt] + P * j - k0
                            mm = nc.tensor.transpose(c.ps[:, j, P * qt:P * qt + P], prob[:, g, at:at + P],
                                                     c.k("ident"))
                        mm.then_inc(turned, 1)

                def project_fm(slot, bank_i, done, u):
                    pe.wait_ge(split[slot], u + 1)
                    for i in range(DC):
                        mm = c.product(c.bank(bank_i), (high[:, slot, i, :], low[:, slot, i, :]),
                                       (x[0][:, i, :], x[1][:, i, :]), i == 0, i == DC - 1)
                    mm.then_inc(done, 1)

                def project_v(u, tiles):
                    for tt in tiles:
                        for i in range(DC):
                            mm = c.product(c.ps[:, 6, P * tt:P * tt + P],
                                           [part[:, i, P * tt:P * tt + P] for part in x],
                                           (high[:, 2, i, :], low[:, 2, i, :]), i == 0, i == DC - 1)
                    if TT - 1 in tiles:
                        mm.then_inc(v_proj, 1)

                def help_fm(i, bank_i, have, done, u):
                    pe.wait_ge(have, u + 1)
                    nc.tensor.matmul(c.bank(bank_i), c.k("rot") if rope else c.k("blk64"),
                                     raw[:, i, :] if rope else tmp[:, i, :], start=True, stop=True).then_inc(done, 1)

                def body(u, project, attend, ahead):
                    if attend:
                        pe.wait_ge(q_ok, u)
                        wait_apart(pe, k_ok, u, passed_pe)
                        scores(u, order[:4])
                    if project:
                        emit_wait(pe, q_ok, u)
                        project_fm(0, 4, q_proj, u)
                    if attend:
                        wait_apart(pe, shifted, (u - 1) * 8 + 1, passed_pe)
                        scores(u, order[4:6])
                        wait_apart(pe, shifted, (u - 1) * 8 + 2, passed_pe)
                        scores(u, order[6:])
                    if project:
                        emit_wait(pe, k_ok, u)
                        project_fm(1, 5, k_proj, u)
                        if not direct:
                            help_fm(0, 4, q_raw, q_help, u)
                    if attend:
                        pe.wait_ge(normed, ngrp * u)
                        turn(u, 0)
                    if project:
                        pe.wait_ge(split[2], u + 1)
                        emit_wait(pe, v_ok, u)
                        project_v(u, (0, 1))
                        if not direct:
                            help_fm(1, 5, k_raw, k_help, u)
                    if attend and comb == 2:
                        turn(u, 1)
                    if project:
                        project_v(u, (2, 3))
                    if attend:
                        pe.wait_ge(v_ok, u)
                        for g in range(comb):
                            rows = slice(0, P) if diff else slice(HD * g, HD * g + HD)
                            if kind != "sink":
                                for j in range(TT):
                                    pe.wait_ge(copied, (u - 1) * 4 * comb + 4 * g + j + 1)
                                    mm = nc.tensor.matmul(c.ps[rows, 7, P * j:T], v[:, j, rows],
                                                          probT[:, g, j, P * j:T], start=(j == 0), stop=(j == TT - 1))
                            else:
                                pe.wait_ge(copied, (u - 1) * 4 * comb + 4 * g + TT)
                                for qt in range(TT):
                                    for j in range(max(qt - 1, 0), qt + 1):
                                        mm = nc.tensor.matmul(
                                            c.ps[rows, 7, P * qt:P * qt + P], v[:, j, rows],
                                            probT[:, g, j, P * qt:P * qt + P], start=(j == max(qt - 1, 0)),
                                            stop=(j == qt))
                        mm.then_inc(pv_done, 1)
                rounds(body, pe)

            @block.scalar
            def _(act):
                def exps(u, tiles):
                    for qt, s in tiles:
                        i = col[qt, s]
                        act.wait_ge(shifted, (u - 1) * 8 + seq[qt, s])
                        if kind == "sink":
                            nc.scalar.activation(esink[:, i:i + 1], nmax[:, i:i + 1], ACT.Exp,
                                                 bias=sink_u[:, s, 0:1])
                        nc.scalar.activation(sl(s, qt), sl(s, qt), ACT.Exp, bias=nmax[:, i:i + 1], scale=-1.0,
                                             accum_out=total[:, i:i + 1]).then_inc(expd, 1)

                def copy_turned(u, g):
                    for j in range(TT):
                        hi = min(T, P * (j + 2)) if kind == "sink" else T
                        act.wait_ge(turned, (u - 1) * 4 * comb + 4 * g + j + 1)
                        nc.scalar.copy(probT[:, g, j, P * j:hi], c.ps[:, j, P * j:hi]).then_inc(copied, 1)

                def round_(i, landed, used, u):
                    act.wait_ge(landed, 16 * u + 16)
                    emit_wait(act, used, u)
                    nc.scalar.copy(high[:, i, :, :], slab[:, i, :, :]).then_inc(rounded[i], 1)

                def raw_out(i, bank_i, proj, have, u):
                    act.wait_ge(proj, u + 1)
                    if diff:
                        nc.scalar.copy(raw[:, i, :], c.bank(bank_i))
                        nc.scalar.activation(tmp[:, i, :], c.bank(bank_i), ACT.Square).then_inc(have, 1)
                    else:
                        nc.scalar.activation(raw[:, i, :], c.bank(bank_i), ACT.Copy,
                                             scale=QK_SCALE if i == 0 else 1.0).then_inc(have, 1)

                def body(u, project, attend, ahead):
                    if attend:
                        exps(u, order[:4])
                    if project and not direct:
                        emit_wait(act, q_ok, u)
                        raw_out(0, 4, q_proj, q_raw, u)
                    if attend:
                        exps(u, order[4:])
                    if ahead:
                        round_(0, q_in, q_proj, u + 1)
                    if project and not direct:
                        emit_wait(act, k_ok, u)
                        raw_out(1, 5, k_proj, k_raw, u)
                    if ahead and not direct:
                        round_(1, k_in, k_proj, u + 1)
                    if project and direct:
                        if attend:
                            act.wait_ge(scored, 6 * u)
                        act.wait_ge(q_proj, u + 1)
                        nc.scalar.activation(qT[:, :], c.bank(4), ACT.Copy, scale=QK_SCALE).then_inc(q_ok, 1)
                        act.wait_ge(k_proj, u + 1)
                        nc.scalar.activation(kT[:, :], c.bank(5), ACT.Copy).then_inc(k_ok, 1)
                    if ahead and direct:
                        round_(1, k_in, k_proj, u + 1)
                    if attend:
                        for g in range(comb):
                            copy_turned(u, g)
                    if project and diff:
                        for i, (helped, half, bank_i) in enumerate(((q_help, q_half, 4), (k_help, k_half, 5))):
                            act.wait_ge(helped, u + 1)
                            nc.scalar.activation(tmp[:, i, :], c.bank(bank_i), ACT.Ln, bias=c.eps[:, 0:1])\
                              .then_inc(logged, 1)
                            act.wait_ge(logged, 2 * u + i + 1)
                            nc.scalar.activation(tmp[:, i, :], tmp[:, i, :], ACT.Exp, scale=-0.5).then_inc(half, 1)
                    if ahead:
                        round_(2, v_in, v_proj, u + 1)
                    if attend:
                        act.wait_ge(pv_done, u)
                        oc = c.o[0][:, bass.ds(first + u - 1, 1), :].rearrange("p a t -> p (a t)")
                        nc.scalar.copy(oc, c.bank(7)).then_inc(o_ok if diff else o_high, 1)

                round_(0, q_in, q_proj, 0)
                round_(1, k_in, k_proj, 0)
                round_(2, v_in, v_proj, 0)
                rounds(body, act)

            @block.vector
            def _(dve):
                def shift(u, tiles, at):
                    for t, (qt, s) in enumerate(tiles):
                        i = col[qt, s]
                        wait_apart(dve, scored, (u - 1) * 6 + scored_at[at + t], passed_dve)
                        nc.vector.tensor_tensor_reduce(
                            out=sl(s, qt), in0=score_bank(qt, s), in1=bias_tile(s, qt), scale=-1.0,
                            scalar=(sink_u[:, s, 1:2] if kind == "sink" else HUGE), op0=ALU.add, op1=ALU.min,
                            accum_out=nmax[:, i:i + 1]).then_inc(shifted, 1)

                def normalise(u, tiles, half):
                    x = slice(4 * half, 4 * half + 4)
                    dve.wait_ge(expd, (u - 1) * 8 + 4 * half + 4)
                    if kind == "sink":
                        nc.vector.tensor_tensor(total[:, x], total[:, x], esink[:, x], ALU.add).then_inc(inv2_ok, 1)
                        dve.wait_ge(inv2_ok, (u - 1) * 2 + half + 1)
                    nc.vector.reciprocal(inv[:, x], total[:, x]).then_inc(inv_ok, 1)
                    dve.wait_ge(inv_ok, (u - 1) * 2 + half + 1)
                    if diff:
                        odd = inv[:, 4 * half + 1:4 * half + 4:2]
                        nc.vector.tensor_scalar(odd, odd, c.neglam[:, 0:1], None, ALU.mult).then_inc(inv2_ok, 1)
                        qts = [3, 2] if half == 0 else [1, 0]
                        for qt in qts:
                            i = col[qt, 0]
                            nc.vector.tensor_scalar(sl(0, qt), sl(0, qt), inv[:, i:i + 1], None, ALU.mult)\
                              .then_inc(scaled, 1)
                        dve.wait_ge(inv2_ok, (u - 1) * 2 + half + 1)
                        for m, qt in enumerate(qts):
                            i = col[qt, 1]
                            dve.wait_ge(scaled, (u - 1) * 4 + 2 * half + m + 1)
                            nc.vector.scalar_tensor_tensor(out=sl(0, qt), in0=sl(1, qt), scalar=inv[:, i:i + 1],
                                                           in1=sl(0, qt), op0=ALU.mult, op1=ALU.add)\
                              .then_inc(normed, 1)
                    else:
                        for qt, s in tiles:
                            i = col[qt, s]
                            nc.vector.tensor_scalar(sl(s, qt), sl(s, qt), inv[:, i:i + 1], None, ALU.mult)\
                              .then_inc(normed, 1)

                def finish(i, bank_i, half, half2, helped, dst, gain, ok, u):
                    if diff:
                        dve.wait_ge(half, u + 1)
                        nc.vector.scalar_tensor_tensor(out=dst, in0=raw[:, i, :], scalar=gain, in1=tmp[:, i, :],
                                                       op0=ALU.mult, op1=ALU.mult).then_inc(ok, 1)
                    else:
                        dve.wait_ge(helped, u + 1)
                        nc.vector.tensor_tensor(tmp2[:, i, :], c.bank(bank_i), c.k("sin"), ALU.mult)\
                          .then_inc(half2, 1)
                        dve.wait_ge(half, u + 1)
                        dve.wait_ge(half2, u + 1)
                        nc.vector.tensor_tensor(dst, tmp[:, i, :], tmp2[:, i, :], ALU.add).then_inc(ok, 1)

                def body(u, project, attend, ahead):
                    if attend:
                        if banded:
                            dve.wait_ge(b_in if diff else b_ok, 16 * u if diff else 2 * u)
                        if kind == "sink":
                            s0 = PARAMS["sinks"][0]
                            pair = c.param[:, bass.ds(s0 + 2 * (u - 1), 2)]
                            nc.vector.tensor_copy(sink_u[:, :, 0], pair).then_inc(sink_ok, 1)
                            nc.vector.tensor_scalar(sink_u[:, :, 1], pair, -1.0, None, ALU.mult).then_inc(sink_ok, 1)
                            dve.wait_ge(sink_ok, 2 * u)
                        shift(u, order[:4], 0)
                        normalise(u, order[:4], 0)
                        shift(u, order[4:], 4)
                        normalise(u, order[4:], 1)
                    if project and not direct:
                        finish(0, 4, q_half, q_half2, q_help, qT[:, :], c.qgain[:, 0:1] if diff else None, q_ok, u)
                        finish(1, 5, k_half, k_half2, k_help, kT[:, :], c.p("kg") if diff else None, k_ok, u)
                    if project:
                        dve.wait_ge(v_proj, u + 1)
                        if attend:
                            dve.wait_ge(pv_done, u)
                        nc.vector.tensor_copy(v[:, :, :].rearrange("p a e -> p (a e)"), c.bank(6)).then_inc(v_ok, 1)
                    if attend and not diff:
                        dve.wait_ge(o_high, u)
                        at = bass.ds(first + u - 1, 1)
                        nc.vector.tensor_tensor(
                            c.o[1][:, at, :].rearrange("p a t -> p (a t)"), c.bank(7),
                            c.o[0][:, at, :].bitcast(F32).rearrange("p a t -> p (a t)"), ALU.subtract)\
                          .then_inc(o_ok, 1)
                rounds(body, dve)


def stage_diff_prepare(c):
    nc = c.nc
    with Stage(nc, "dprep") as ctx:
        sem = ctx.sem
        scratch = ctx.enter_context(nc.sbuf_tensor("dprep_s", [P, 2, HD], F32))
        dots = ctx.enter_context(nc.sbuf_tensor("dprep_d", [P, 2], F32))
        ex = ctx.enter_context(nc.sbuf_tensor("dprep_e", [P, 2], F32))
        dif = ctx.enter_context(nc.sbuf_tensor("dprep_f", [P, 1], F32))
        dotted, expd, step = sem("dotted"), sem("expd"), sem("step")
        with nc.Block("dprep") as block:
            @block.vector
            def _(dve):
                for i in range(2):
                    nc.vector.tensor_tensor_reduce(
                        out=scratch[:, i, :], in0=c.p("lam", 2 * i * HD, HD), in1=c.p("lam", (2 * i + 1) * HD, HD),
                        scale=1.0, scalar=0.0, op0=ALU.mult, op1=ALU.add, accum_out=dots[:, i:i + 1])\
                      .then_inc(dotted, 1)
                nc.vector.tensor_scalar(c.qgain[:, :], c.p("qg"), QK_SCALE, None, ALU.mult)
                dve.wait_ge(expd, 1)
                nc.vector.tensor_tensor(dif[:, :], ex[:, 1:2], ex[:, 0:1], ALU.subtract).then_inc(step, 1)
                dve.wait_ge(step, 1)
                nc.vector.tensor_scalar(c.neglam[:, :], dif[:, :], LAMBDA_INIT, None, ALU.subtract)

            @block.scalar
            def _(act):
                act.wait_ge(dotted, 2)
                nc.scalar.activation(ex[:, :], dots[:, :], ACT.Exp).then_inc(expd, 1)


def stage_subln(c, o, parts):
    nc = c.nc
    with Stage(nc, "subln") as ctx:
        sem = ctx.sem
        sq = ctx.enter_context(nc.sbuf_tensor("subln_sq", [P, DC, T], F32))
        rs = ctx.enter_context(nc.sbuf_tensor("subln_rs", [P, DC, T], F32))
        g = ctx.enter_context(nc.sbuf_tensor("subln_g", [P, 1], F32))
        squared, meaned, logged, inverted, gained, scaled, rounded = (
            sem(n) for n in ("squared", "meaned", "logged", "inverted", "gained", "scaled", "rounded"))
        with nc.Block("subln") as block:
            @block.scalar
            def _(act):
                for i in range(DC):
                    nc.scalar.activation(sq[:, i, :], o[:, i, :], ACT.Square).then_inc(squared, 1)
                for i in range(DC):
                    act.wait_ge(meaned, i + 1)
                    nc.scalar.activation(sq[:, i, :], c.bank(i), ACT.Ln, bias=c.eps[:, 0:1]).then_inc(logged, 1)
                for i in range(DC):
                    act.wait_ge(logged, i + 1)
                    nc.scalar.activation(rs[:, i, :], sq[:, i, :], ACT.Exp, scale=-0.5).then_inc(inverted, 1)
                    act.wait_ge(scaled, i + 1)
                    nc.scalar.copy(parts[0][:, i, :], o[:, i, :]).then_inc(rounded, 1)

            @block.tensor
            def _(pe):
                for i in range(DC):
                    pe.wait_ge(squared, i + 1)
                    nc.tensor.matmul(c.bank(i), c.k("inv_p"), sq[:, i, :], start=True, stop=True)\
                      .then_inc(meaned, 1)

            @block.vector
            def _(dve):
                nc.vector.tensor_scalar(g[:, :], c.p("subln"), 1.0 - LAMBDA_INIT, None, ALU.mult).then_inc(gained, 1)
                dve.wait_ge(gained, 1)
                for i in range(DC):
                    dve.wait_ge(inverted, i + 1)
                    nc.vector.scalar_tensor_tensor(out=o[:, i, :], in0=o[:, i, :], scalar=g[:, 0:1],
                                                   in1=rs[:, i, :], op0=ALU.mult, op1=ALU.mult).then_inc(scaled, 1)

            @block.gpsimd
            def _(pool):
                for i in range(DC):
                    pool.wait_ge(rounded, i + 1)
                    nc.gpsimd.tensor_tensor(parts[1][:, i, :], o[:, i, :], parts[0][:, i, :].bitcast(F32),
                                            ALU.subtract)


def stage_ffn_up(c, name, layer, w, x, out):
    nc = c.nc
    with Stage(nc, name) as ctx:
        sem = ctx.sem
        sb = lambda x, shape: ctx.enter_context(nc.sbuf_tensor(f"{name}_{x}", shape, F32))
        slab = [sb(f"w{b}", [P, 2, DC, P]) for b in range(2)]
        high, low = ([ctx.enter_context(nc.sbuf_tensor(f"{name}_{i}{v}", [P, DC, P], F32R)) for v in range(2)]
                     for i in ("wh", "wl"))
        acc, prod = sb("acc", [P, 4, T]), sb("prod", [P, 2, T])
        w_in = [sem(f"w_in{b}") for b in range(2)]
        rounded, split, projected, based, tap1, tap0, gated, multiplied, out_high, done = (
            sem(n) for n in ("rounded", "split", "projected", "based", "tap1", "tap0", "gated", "multiplied",
                             "out_high", "done"))
        cw, cb = PARAMS["convw"][0] + layer * 2 * FC * 3, PARAMS["convb"][0] + layer * 2 * FC

        def weight(j, v, tap):
            return c.param[:, bass.ds(cw + (j + v * FC) * 3 + tap, 1)]

        with nc.Block(name) as block:
            @block.sync
            def _(sp):
                def load(i):
                    for b in range(2):
                        emit_wait(sp, split, 4 * i - 2 + 2 * b)
                        sp.dma_start(slab[b][:, :, :, :], w[bass.ds(2 * i + b, 1)].rearrange("a p x k m -> (a p) x k m"))\
                          .then_inc(w_in[b], 16)
                repeat(sp, FC // 2, load)

            @block.gpsimd
            def _(pool):
                def rest(i):
                    for b in range(2):
                        for v in range(2):
                            pool.wait_ge(rounded, 4 * i + 2 * b + v + 1)
                            nc.gpsimd.tensor_tensor(low[v][:, :, :], slab[b][:, v, :, :],
                                                    high[v][:, :, :].bitcast(F32), ALU.subtract).then_inc(split, 1)
                repeat(pool, FC // 2, rest)

            @block.tensor
            def _(pe):
                def project(i):
                    for b in range(2):
                        for v in range(2):
                            pe.wait_ge(split, 4 * i + 2 * b + v + 1)
                            emit_wait(pe, tap0, 4 * (i - 1) + 2 * b + v + 1 if not isinstance(i, int) else 0)
                            for j in range(DC):
                                mm = c.product(c.bank(2 * b + v), (high[v][:, j, :], low[v][:, j, :]),
                                               (x[0][:, j, :], x[1][:, j, :]), j == 0, j == DC - 1)
                            mm.then_inc(projected, 1)
                repeat(pe, FC // 2, project)

            @block.scalar
            def _(act):
                def round_(i, b, v):
                    act.wait_ge(w_in[b], 16 * i + 16)
                    emit_wait(act, projected, 4 * i + 2 * b + v - 1)
                    nc.scalar.copy(high[v][:, :, :], slab[b][:, v, :, :]).then_inc(rounded, 1)

                def first_tap(i, last):
                    for b in range(2):
                        for v in range(2):
                            act.wait_ge(projected, 4 * i + 2 * b + v + 1)
                            emit_wait(act, multiplied, 2 * i - 1 + b if not isinstance(i, int) else 0)
                            if b == 0:
                                round_(i, 1, v)
                            elif not last:
                                round_(i + 1, 0, v)
                            nc.scalar.activation(
                                acc[:, 2 * b + v, :], c.bank(2 * b + v), ACT.Identity,
                                bias=c.param[:, bass.ds(cb + 2 * i + b + v * FC, 1)],
                                scale=weight(2 * i + b, v, 2)).then_inc(based, 1)
                            if v == 0:
                                act.wait_ge(tap0, 4 * i + 2 * b + 1)
                                nc.scalar.activation(acc[:, 2 * b, :], acc[:, 2 * b, :], ACT.Silu).then_inc(gated, 1)
                        act.wait_ge(multiplied, 2 * i + b + 1)
                        nc.scalar.copy(out[0][:, bass.ds(2 * i + b, 1), :].rearrange("p a t -> p (a t)"),
                                       prod[:, b, :]).then_inc(out_high, 1)

                round_(0, 0, 0)
                round_(0, 0, 1)
                first_tap(0, False)
                with act.Fori(1, FC // 2 - 1) as i:
                    first_tap(i, False)
                first_tap(FC // 2 - 1, True)

            @block.vector
            def _(dve):
                def convolve(i):
                    for b in range(2):
                        for v in range(2):
                            n = 4 * i + 2 * b + v + 1
                            y = acc[:, 2 * b + v, :]
                            raw = c.bank(2 * b + v)
                            dve.wait_ge(based, n)
                            nc.vector.scalar_tensor_tensor(
                                out=y[:, 1:T], in0=raw[:, 0:T - 1], scalar=weight(2 * i + b, v, 1), in1=y[:, 1:T],
                                op0=ALU.mult, op1=ALU.add).then_inc(tap1, 1)
                            dve.wait_ge(tap1, n)
                            nc.vector.scalar_tensor_tensor(
                                out=y[:, 2:T], in0=raw[:, 0:T - 2], scalar=weight(2 * i + b, v, 0), in1=y[:, 2:T],
                                op0=ALU.mult, op1=ALU.add).then_inc(tap0, 1)
                        dve.wait_ge(gated, 2 * i + b + 1)
                        dve.wait_ge(tap0, 4 * i + 2 * b + 2)
                        emit_wait(dve, done, 2 * i - 1 + b if not isinstance(i, int) else 0)
                        nc.vector.tensor_tensor(prod[:, b, :], acc[:, 2 * b, :], acc[:, 2 * b + 1, :], ALU.mult)\
                          .then_inc(multiplied, 1)
                        dve.wait_ge(out_high, 2 * i + b + 1)
                        at = bass.ds(2 * i + b, 1)
                        nc.vector.tensor_tensor(
                            out[1][:, at, :].rearrange("p a t -> p (a t)"), prod[:, b, :],
                            out[0][:, at, :].bitcast(F32).rearrange("p a t -> p (a t)"), ALU.subtract)\
                          .then_inc(done, 1)
                repeat(dve, FC // 2, convolve)


def stage_route(c):
    nc, a = c.nc, c.a
    with Stage(nc, "route") as ctx:
        sem = ctx.sem
        sb = lambda x, shape, dt=F32: ctx.enter_context(nc.sbuf_tensor(f"route_{x}", shape, dt))
        wr = sb("w", [P, DC, 20])
        rows = sb("rows", [P, TT, D])
        L = sb("L", [P, TT, 20])
        gmax, taken, fresh = sb("gmax", [P, TT]), sb("taken", [P, TT]), sb("fresh", [P, TT])
        eq = sb("eq", [P, TT, 4])
        selg = sb("selg", [P, TT, 4])
        ex, gsum, gate = sb("ex", [P, TT, 4]), sb("gsum", [P, TT]), sb("gate", [P, TT])
        le, tmp4 = sb("le", [P, TT, 4]), sb("tmp4", [P, TT, 4])
        s12 = sb("s12", [P, 2, TT, 4])
        val = sb("val", [P, 2, TT])
        wt = sb("wt", [P, 2, TT])
        M = sb("M", [P, 2, TT, N_EXP])
        Ms = sb("Ms", [P, TT, N_EXP])
        cnt, tiles, incl, excl = (sb(x, [P, N_EXP]) for x in ("cnt", "tiles", "incl", "excl"))
        pos = sb("pos", [P, TT, N_EXP])
        tm = sb("tm", [P, 2, TT, N_EXP])
        dst = sb("dst", [P, 2, TT])
        dsti = sb("dsti", [P, 2, TT], U32)
        rec = sb("rec", [P, 2, TT, 4], I32)
        cmp = sb("cmp", [1, 24, N_EXP])
        tl = sb("tl", [1, 25])
        w_in, rec_in, turned, copied, logits, step, expd, exp_in, counted, placed, stored, back = (
            sem(x) for x in ("w_in", "rec_in", "turned", "copied", "logits", "step", "expd", "exp_in", "counted",
                             "placed", "stored", "back"))
        listed = ctx.dma_sem("listed")
        fwd_tiles = sem("fwd_tiles")
        with nc.Block("route") as block:
            @block.sync
            def _(sp):
                sp.dma_start(wr[:, :, :], a["w_route"]).then_inc(w_in, 16)
                sp.dma_start(rec[:, :, :, :], a["rec"]).then_inc(rec_in, 16)
                for tt in range(TT):
                    sp.wait_ge(copied, 2 * tt + 2)
                    sp.dma_start(a["hrows"][tt * P:(tt + 1) * P, :], rows[:, tt, :]).then_inc(stored, 16)
                sp.wait_ge(listed, 16 * 8)
                sp.dma_start(c.slots[:, :, :], a["plist"].rearrange("(t p) x -> p t x", p=P)).then_inc(back, 16)
                sp.wait_ge(back, 16)
                sp.wait_ge(stored, 16 * TT)

            @block.tensor
            def _(pe):
                pe.wait_ge(w_in, 16)
                for tt in range(TT):
                    for i in range(DC):
                        mm = nc.tensor.matmul(c.ps[:, 4, 20 * tt:20 * tt + 20], c.xn[:, i, P * tt:P * tt + P],
                                              wr[:, i, :], start=(i == 0), stop=(i == DC - 1))
                mm.then_inc(logits, 1)
                for tt in range(TT):
                    for half in range(2):
                        n = 2 * tt + half
                        if n >= 4:
                            pe.wait_ge(copied, n - 3)
                        for i in range(4):
                            mm = nc.tensor.transpose(c.ps[:, n % 4, P * i:P * i + P],
                                                     c.xn[:, 4 * half + i, P * tt:P * tt + P], c.k("ident"))
                        mm.then_inc(turned, 1)
                pe.wait_ge(counted, 1)
                for tt in range(TT):
                    for j in range(tt + 1):
                        nc.tensor.matmul(c.ps[:, 5, N_EXP * tt:N_EXP * tt + N_EXP],
                                         c.k("tri") if j == tt else c.k("ones"), Ms[:, j, :],
                                         start=(j == 0), stop=(j == tt))
                for j in range(TT):
                    mm = nc.tensor.matmul(c.ps[:, 5, 64:64 + N_EXP], c.k("ones"), Ms[:, j, :],
                                          start=(j == 0), stop=(j == TT - 1))
                mm.then_inc(placed, 1)

            @block.scalar
            def _(act):
                for tt in range(TT):
                    for half in range(2):
                        n = 2 * tt + half
                        act.wait_ge(turned, n + 1)
                        nc.scalar.copy(rows[:, tt, 512 * half:512 * half + 512], c.bank(n % 4)).then_inc(copied, 1)
                for i, t in enumerate((ex, le)):
                    act.wait_ge(exp_in, i + 1)
                    nc.scalar.activation(t[:, :, :], t[:, :, :], ACT.Exp).then_inc(expd, 1)

            @block.vector
            def _(dve):
                n = [0]

                def then(ins):
                    n[0] += 1
                    ins.then_inc(step, 1)
                    dve.wait_ge(step, n[0])

                tt_ = nc.vector.tensor_tensor

                def first_equal(out, x, top):
                    then(nc.vector.tensor_tensor(eq[:, :, :], x, top.unsqueeze(2).broadcast_to([P, TT, 4]), ALU.is_equal))
                    then(nc.vector.memset(taken[:, :], 0.0))
                    for j in range(4):
                        then(nc.vector.tensor_scalar(fresh[:, :], taken[:, :], -1.0, 1.0, ALU.mult, ALU.add))
                        then(tt_(out[:, :, j], eq[:, :, j], fresh[:, :], ALU.mult))
                        if j < 3:
                            then(tt_(taken[:, :], taken[:, :], out[:, :, j], ALU.add))

                def wide(x):
                    return x.unsqueeze(2).broadcast_to([P, TT, 4])

                dve.wait_ge(logits, 1)
                then(tt_(L[:, :, :], c.ps[:, 4, 0:80].rearrange("p (t e) -> p t e", t=TT),
                         c.p("rb").unsqueeze(1).broadcast_to([P, TT, 20]), ALU.add))
                then(nc.vector.tensor_reduce(gmax[:, :], L[:, :, 0:4], AX_X, ALU.max))
                first_equal(selg, L[:, :, 0:4], gmax[:, :])
                n[0] += 0
                tt_(ex[:, :, :], L[:, :, 0:4], wide(gmax[:, :]), ALU.subtract).then_inc(exp_in, 1)
                dve.wait_ge(expd, 1)
                then(nc.vector.tensor_reduce(gsum[:, :], ex[:, :, :], AX_X, ALU.add))
                then(nc.vector.reciprocal(gate[:, :], gsum[:, :]))
                then(tt_(le[:, :, :], L[:, :, 4:8], wide(selg[:, :, 0]), ALU.mult))
                for g in range(1, 4):
                    then(tt_(tmp4[:, :, :], L[:, :, 4 + 4 * g:8 + 4 * g], wide(selg[:, :, g]), ALU.mult))
                    then(tt_(le[:, :, :], le[:, :, :], tmp4[:, :, :], ALU.add))
                then(nc.vector.tensor_reduce(gmax[:, :], le[:, :, :], AX_X, ALU.max))
                tt_(le[:, :, :], le[:, :, :], wide(gmax[:, :]), ALU.subtract).then_inc(exp_in, 1)
                dve.wait_ge(expd, 2)
                then(nc.vector.tensor_reduce(gsum[:, :], le[:, :, :], AX_X, ALU.add))
                then(nc.vector.reciprocal(gsum[:, :], gsum[:, :]))
                then(tt_(le[:, :, :], le[:, :, :], wide(gsum[:, :]), ALU.mult))
                then(nc.vector.tensor_reduce(val[:, 0, :], le[:, :, :], AX_X, ALU.max))
                first_equal(s12[:, 0], le[:, :, :], val[:, 0, :])
                then(nc.vector.scalar_tensor_tensor(out=le[:, :, :], in0=s12[:, 0], scalar=-2.0, in1=le[:, :, :],
                                                    op0=ALU.mult, op1=ALU.add))
                then(nc.vector.tensor_reduce(val[:, 1, :], le[:, :, :], AX_X, ALU.max))
                first_equal(s12[:, 1], le[:, :, :], val[:, 1, :])
                then(tt_(gsum[:, :], val[:, 0, :], val[:, 1, :], ALU.add))
                then(nc.vector.reciprocal(gsum[:, :], gsum[:, :]))
                then(tt_(gsum[:, :], gsum[:, :], gate[:, :], ALU.mult))
                for k in range(2):
                    then(tt_(wt[:, k, :], val[:, k, :], gsum[:, :], ALU.mult))
                for k in range(2):
                    for g in range(4):
                        then(tt_(M[:, k, :, 4 * g:4 * g + 4], s12[:, k], wide(selg[:, :, g]), ALU.mult))
                tt_(Ms[:, :, :], M[:, 0], M[:, 1], ALU.add).then_inc(counted, 1)
                dve.wait_ge(placed, 1)
                then(nc.vector.tensor_copy(cnt[:, :], c.ps[:, 5, 64:64 + N_EXP]))
                then(nc.vector.tensor_scalar(tiles[:, :], cnt[:, :], 0.0, None, ALU.is_gt))
                for k in range(1, 4):
                    then(nc.vector.scalar_tensor_tensor(out=tiles[:, :], in0=cnt[:, :], scalar=float(P * k),
                                                        in1=tiles[:, :], op0=ALU.is_gt, op1=ALU.add))
                then(nc.vector.tensor_tensor_scan(incl[:, :], c.k("ones")[:, 0:N_EXP], tiles[:, :], 0.0,
                                                  ALU.mult, ALU.add))
                then(tt_(excl[:, :], incl[:, :], tiles[:, :], ALU.subtract))
                then(nc.vector.tensor_scalar(excl[:, :], excl[:, :], float(P), None, ALU.mult))
                then(tt_(pos[:, :, :], c.ps[:, 5, 0:64].rearrange("p (t e) -> p t e", t=TT),
                         excl[:, :].unsqueeze(1).broadcast_to([P, TT, N_EXP]), ALU.add))
                for k in range(2):
                    then(tt_(tm[:, k], M[:, k], pos[:, :, :], ALU.mult))
                    then(nc.vector.tensor_reduce(dst[:, k, :], tm[:, k], AX_X, ALU.add))
                then(nc.vector.tensor_copy(dsti[:, :, :], dst[:, :, :]))
                dve.wait_ge(rec_in, 16)
                then(nc.vector.tensor_copy(rec[:, :, :, 2].bitcast(F32), wt[:, :, :]))
                then(tt_(cmp[:, :, :], incl[0:1, :].unsqueeze(1).broadcast_to([1, 24, N_EXP]),
                         c.k("tileid")[0:1, :].rearrange("p (i e) -> p i e", i=24), ALU.is_le))
                then(nc.vector.tensor_reduce(tl[:, 0:24], cmp[:, :, :], AX_X, ALU.add))
                then(nc.vector.tensor_copy(tl[:, 23:24], incl[0:1, 15:16]))
                then(nc.vector.tensor_scalar(tl[:, 24:25], incl[0:1, 15:16], 1.0, None, ALU.subtract))
                nc.vector.tensor_copy(c.tiles[:, :], tl[:, :]).then_inc(fwd_tiles, 1)

            @block.gpsimd
            def _(pool):
                pool.wait_ge(fwd_tiles, 1)
                for k in range(2):
                    for tt in range(TT):
                        nc.gpsimd.indirect_dma_start(
                            out=a["plist"], out_offset=bass.IndirectOffsetOnAxis(ap=dsti[:, k, tt:tt + 1], axis=0),
                            in_=rec[:, k, tt, :], in_offset=None).then_inc(listed, 16)


def stage_experts(c):
    nc, a = c.nc, c.a
    with Stage(nc, "moe") as ctx:
        sem = ctx.sem
        sb = lambda x, shape, dt=F32: ctx.enter_context(nc.sbuf_tensor(f"moe_{x}", shape, dt))
        wg, wu, wd = sb("wg", [P, DC, D_EXP]), sb("wu", [P, DC, D_EXP]), sb("wd", [P, D_EXP // P, D])
        xg, xgT = sb("xg", [P, D]), sb("xgT", [P, DC, P])
        hh, hT, y = sb("hh", [P, D_EXP]), sb("hT", [P, 4, P]), sb("y", [P, D])
        gi, si = sb("gi", [P, 4], I32), sb("si", [P, 4], I32)
        (g_in, u_in, d_in, zeroed, idx, turned, xcopied, gated, upped, silued, hready, hturned, hcopied,
         downed, ycopied, sidx) = (
            sem(x) for x in ("g_in", "u_in", "d_in", "zeroed", "idx", "turned", "xcopied", "gated",
                             "upped", "silued", "hready", "hturned", "hcopied", "downed", "ycopied", "sidx"))
        passed_pool = sem("passed_pool")
        gathered, scattered = ctx.dma_sem("gathered"), ctx.dma_sem("scattered")

        def count(eng):
            return eng.value_load(c.tiles[0:1, 23:24], min_val=PAIRS // P, max_val=MAX_TILES)

        def last(eng):
            return eng.value_load(c.tiles[0:1, 24:25], min_val=PAIRS // P - 1, max_val=MAX_TILES - 1)

        with nc.Block("experts") as block:
            @block.sync
            def _(sp):
                def load(i, free, landed, dst, src):
                    e = sp.value_load(c.tiles[0:1, bass.ds(i, 1)], min_val=0, max_val=N_EXP - 1)
                    emit_wait(sp, free, i)
                    sp.dma_start(dst[:, :, :], src[bass.ds(e, 1)].rearrange("a p k m -> (a p) k m"))\
                      .then_inc(landed, 16)

                def body(i):
                    load(i, gated, g_in, wg, a["w_gate"])
                    load(i, upped, u_in, wu, a["w_up"])
                    if not isinstance(i, int) or i:
                        load(i - 1, downed, d_in, wd, a["w_down"])

                repeat(sp, count(sp), body, peel=2)
                load(last(sp), downed, d_in, wd, a["w_down"])

            @block.gpsimd
            def _(pool):
                nc.gpsimd.memset(xg[:, :], 0.0).then_inc(zeroed, 1)
                pool.wait_ge(zeroed, 1)

                def gather(i):
                    emit_wait(pool, turned, 2 * i)
                    emit_wait(pool, gathered, 16 * i)
                    src = c.slots[:, bass.ds(i, 1), 0:2].rearrange("p a x -> p (a x)")
                    nc.gpsimd.tensor_copy(gi[:, 0:2], src).then_inc(idx, 1)
                    wait_apart(pool, idx, i + 1, passed_pool)
                    nc.gpsimd.indirect_dma_start(
                        out=xg[:, :], out_offset=None, in_=a["hrows"],
                        in_offset=bass.IndirectOffsetOnAxis(ap=gi[:, 0:1].bitcast(U32), axis=0),
                        bounds_check=T - 1, oob_is_err=False).then_inc(gathered, 16)

                def scatter(i):
                    pool.wait_ge(ycopied, 2 * i + 2)
                    src = c.slots[:, bass.ds(i, 1), 0:2].rearrange("p a x -> p (a x)")
                    nc.gpsimd.tensor_copy(si[:, 0:2], src).then_inc(sidx, 1)
                    wait_apart(pool, sidx, i + 1, passed_pool)
                    nc.gpsimd.indirect_dma_start(
                        out=a["yrows"], out_offset=bass.IndirectOffsetOnAxis(ap=si[:, 1:2].bitcast(U32), axis=0),
                        in_=y[:, :], in_offset=None, bounds_check=PAIRS - 1, oob_is_err=False)\
                      .then_inc(scattered, 16)
                    wait_apart(pool, scattered, 16 * i + 16, passed_pool)

                def body(i):
                    gather(i + 1)
                    if not isinstance(i, int) or i:
                        scatter(i - 1)

                gather(0)
                n = count(pool)
                repeat(pool, n, body)
                scatter(last(pool))
                pool.wait_ge(gathered, 16 * n + 16)

            @block.tensor
            def _(pe):
                def turn_x(i):
                    pe.wait_ge(gathered, 16 * i + 16)
                    for half in range(2):
                        emit_wait(pe, xcopied, 2 * i)
                        for j in range(4):
                            mm = nc.tensor.transpose(c.ps[:, half, P * j:P * j + P],
                                                     xg[:, 512 * half + P * j:512 * half + P * j + P], c.k("ident"))
                        mm.then_inc(turned, 1)

                def down(i):
                    pe.wait_ge(hcopied, i + 1)
                    pe.wait_ge(d_in, 16 * i + 16)
                    for half in range(2):
                        emit_wait(pe, ycopied, 2 * i)
                        for j in range(4):
                            mm = nc.tensor.matmul(c.bank(5 + half), hT[:, j, :], wd[:, j, 512 * half:512 * half + 512],
                                                  start=(j == 0), stop=(j == 3))
                    mm.then_inc(downed, 1)

                def body(i):
                    pe.wait_ge(xcopied, 2 * i + 2)
                    for bank_i, slab, landed, done in ((2, wg, g_in, gated), (3, wu, u_in, upped)):
                        pe.wait_ge(landed, 16 * i + 16)
                        emit_wait(pe, hready, i)
                        for j in range(DC):
                            mm = nc.tensor.matmul(c.bank(bank_i), xgT[:, j, :], slab[:, j, :],
                                                  start=(j == 0), stop=(j == DC - 1))
                        mm.then_inc(done, 1)
                    turn_x(i + 1)
                    if not isinstance(i, int) or i:
                        down(i - 1)
                    pe.wait_ge(hready, i + 1)
                    emit_wait(pe, hcopied, i)
                    for j in range(4):
                        mm = nc.tensor.transpose(c.ps[:, 4, P * j:P * j + P], hh[:, P * j:P * j + P], c.k("ident"))
                    mm.then_inc(hturned, 1)

                turn_x(0)
                repeat(pe, count(pe), body, peel=2)
                down(last(pe))

            @block.scalar
            def _(act):
                def copy_x(i):
                    for half in range(2):
                        act.wait_ge(turned, 2 * i + half + 1)
                        emit_wait(act, upped, i)
                        nc.scalar.copy(xgT[:, 4 * half:4 * half + 4, :].rearrange("p a t -> p (a t)"), c.bank(half))\
                          .then_inc(xcopied, 1)

                def copy_y(i):
                    act.wait_ge(downed, i + 1)
                    emit_wait(act, scattered, 16 * i)
                    for half in range(2):
                        nc.scalar.copy(y[:, 512 * half:512 * half + 512], c.bank(5 + half)).then_inc(ycopied, 1)

                def body(i):
                    act.wait_ge(gated, i + 1)
                    emit_wait(act, hturned, i)
                    nc.scalar.activation(hh[:, :], c.bank(2), ACT.Silu).then_inc(silued, 1)
                    copy_x(i + 1)
                    if not isinstance(i, int) or i:
                        copy_y(i - 1)

                copy_x(0)
                repeat(act, count(act), body, peel=2)
                copy_y(last(act))

            @block.vector
            def _(dve):
                def body(i):
                    dve.wait_ge(silued, i + 1)
                    dve.wait_ge(upped, i + 1)
                    wcol = c.slots[:, bass.ds(i, 1), 2:3].bitcast(F32).rearrange("p a x -> p (a x)")
                    nc.vector.scalar_tensor_tensor(out=hh[:, :], in0=hh[:, :], scalar=wcol, in1=c.bank(3),
                                                   op0=ALU.mult, op1=ALU.mult).then_inc(hready, 1)
                    dve.wait_ge(hturned, i + 1)
                    emit_wait(dve, downed, i)
                    nc.vector.tensor_copy(hT[:, :, :].rearrange("p a t -> p (a t)"), c.bank(4)).then_inc(hcopied, 1)
                repeat(dve, count(dve), body, peel=2)


def stage_combine(c):
    nc, a = c.nc, c.a
    with Stage(nc, "comb") as ctx:
        sem = ctx.sem
        y = ctx.enter_context(nc.sbuf_tensor("comb_y", [P, 2, TT, D], F32))
        y_in = [sem(f"y_in{t}") for t in range(TT)]
        summed, turned, added = sem("summed"), sem("turned"), sem("added")
        with nc.Block("combine") as block:
            @block.sync
            def _(sp):
                rows = a["yrows"].rearrange("(k t p) d -> t p k d", k=2, p=P)
                for tt in range(TT):
                    sp.dma_start(y[:, :, tt, :], rows[tt]).then_inc(y_in[tt], 16)

            @block.vector
            def _(dve):
                for tt in range(TT):
                    dve.wait_ge(y_in[tt], 16)
                    nc.vector.tensor_tensor(y[:, 0, tt, :], y[:, 0, tt, :], y[:, 1, tt, :], ALU.add)\
                      .then_inc(summed, 1)
                for i in range(DC):
                    dve.wait_ge(turned, i + 1)
                    nc.vector.tensor_tensor(c.h[:, i, :], c.bank(i), c.h[:, i, :], ALU.add).then_inc(added, 1)

            @block.tensor
            def _(pe):
                for i in range(DC):
                    for tt in range(TT):
                        pe.wait_ge(summed, tt + 1)
                        mm = nc.tensor.transpose(c.ps[:, i, P * tt:P * tt + P], y[:, 0, tt, P * i:P * i + P],
                                                 c.k("ident"))
                    mm.then_inc(turned, 1)


def stage_select(c):
    nc, a = c.nc, c.a
    with Stage(nc, "sel") as ctx:
        sem = ctx.sem
        sb = lambda x, shape: ctx.enter_context(nc.sbuf_tensor(f"sel_{x}", shape, F32))
        w = sb("w", [P, 3, DC, P])
        ww = sb("ww", [P, DC, 4])
        raw, tmp, tmp2 = sb("raw", [P, 3, T]), sb("tmp", [P, 3, T]), sb("tmp2", [P, T])
        fin = sb("fin", [P, 3, T])
        wi = sb("wi", [P, TT, 4])
        rel = sb("rel", [P, 2, 4, T])
        work = sb("work", [P, 4, T])
        m8 = sb("m8", [P, 8])
        w_in, projected, weighed, evac, meaned, step, sq, varred, rooted, rotated, ready, scored, reluded, accd = (
            sem(x) for x in ("w_in", "projected", "weighed", "evac", "meaned", "step", "sq", "varred", "rooted",
                             "rotated", "ready", "scored", "reluded", "accd"))
        kready = sem("kready")
        with nc.Block("select") as block:
            @block.sync
            def _(sp):
                sp.dma_start(w[:, :, :, :], a["w_idx"].rearrange("i p k m -> p i k m")).then_inc(w_in, 16)
                sp.dma_start(ww[:, :, :], a["w_idxw"]).then_inc(w_in, 16)

            @block.tensor
            def _(pe):
                pe.wait_ge(w_in, 32)
                for i in (2, 0, 1):
                    for j in range(DC):
                        mm = nc.tensor.matmul(c.bank(i), w[:, i, j, :], c.xn[:, j, :], start=(j == 0),
                                              stop=(j == DC - 1))
                    mm.then_inc(projected, 1)
                for tt in range(TT):
                    for j in range(DC):
                        mm = nc.tensor.matmul(c.ps[:, 3, 4 * tt:4 * tt + 4], c.xn[:, j, P * tt:P * tt + P],
                                              ww[:, j, :], start=(j == 0), stop=(j == DC - 1))
                mm.then_inc(weighed, 1)
                pe.wait_ge(evac, 1)
                nc.tensor.matmul(c.bank(4), c.k("blk64"), raw[:, 2, :], start=True, stop=True).then_inc(meaned, 1)
                pe.wait_ge(sq, 1)
                nc.tensor.matmul(c.bank(5), c.k("blk64"), tmp[:, 2, :], start=True, stop=True).then_inc(varred, 1)
                for i in (0, 1):
                    pe.wait_ge(evac, 2 + i)
                    nc.tensor.matmul(c.bank(i), c.k("rot"), raw[:, i, :], start=True, stop=True).then_inc(rotated, 1)
                pe.wait_ge(kready, 1)
                nc.tensor.matmul(c.bank(2), c.k("rot"), raw[:, 2, :], start=True, stop=True).then_inc(rotated, 1)
                pe.wait_ge(ready, 3)
                for t, qt in enumerate((1, 2, 3)):
                    for h in range(4):
                        hd = slice(HD * (h % 2), HD * (h % 2) + HD)
                        if t:
                            pe.wait_ge(reluded, 4 * (t - 1) + h + 1)
                        nc.tensor.matmul(c.ps[:, 4 + h, 0:P * (qt + 1)], fin[hd, h // 2, P * qt:P * qt + P],
                                         fin[hd, 2, 0:P * (qt + 1)], start=True, stop=True).then_inc(scored, 1)

            @block.scalar
            def _(act):
                for n, i in enumerate((2, 0, 1)):
                    act.wait_ge(projected, n + 1)
                    nc.scalar.copy(raw[:, i, :], c.bank(i)).then_inc(evac, 1)
                act.wait_ge(step, 1)
                nc.scalar.activation(tmp[:, 2, :], raw[:, 2, :], ACT.Square).then_inc(sq, 1)
                act.wait_ge(varred, 1)
                nc.scalar.activation(tmp[:, 2, :], c.bank(5), ACT.Sqrt, bias=c.eps[:, 0:1]).then_inc(rooted, 1)
                for t, qt in enumerate((1, 2, 3)):
                    for h in range(4):
                        act.wait_ge(scored, 4 * t + h + 1)
                        if t == 2:
                            act.wait_ge(accd, 4)
                        nc.scalar.activation(rel[:, t % 2, h, 0:P * (qt + 1)], c.ps[:, 4 + h, 0:P * (qt + 1)],
                                             ACT.Relu).then_inc(reluded, 1)

            @block.vector
            def _(dve):
                n = [0]

                def then(ins):
                    n[0] += 1
                    ins.then_inc(step, 1)
                    dve.wait_ge(step, n[0])

                dve.wait_ge(meaned, 1)
                then(nc.vector.tensor_tensor(raw[:, 2, :], raw[:, 2, :], c.bank(4), ALU.subtract))
                dve.wait_ge(rooted, 1)
                then(nc.vector.reciprocal(tmp2[:, :], tmp[:, 2, :]))
                then(nc.vector.tensor_tensor(raw[:, 2, :], raw[:, 2, :], tmp2[:, :], ALU.mult))
                nc.vector.tensor_scalar(raw[:, 2, :], raw[:, 2, :], c.p("lng"), c.p("lnb"), ALU.mult, ALU.add)\
                  .then_inc(kready, 1)
                dve.wait_ge(kready, 1)
                for m, i in enumerate((0, 1, 2)):
                    dve.wait_ge(evac, 3)
                    then(nc.vector.tensor_tensor(tmp[:, i, :], raw[:, i, :], c.k("cos"), ALU.mult))
                    dve.wait_ge(rotated, m + 1)
                    then(nc.vector.tensor_tensor(tmp2[:, :], c.bank(i), c.k("sin"), ALU.mult))
                    nc.vector.tensor_tensor(fin[:, i, :], tmp[:, i, :], tmp2[:, :], ALU.add).then_inc(ready, 1)
                    dve.wait_ge(ready, m + 1)
                dve.wait_ge(weighed, 1)
                then(nc.vector.tensor_copy(wi[:, :, :].rearrange("p a e -> p (a e)"), c.ps[:, 3, 0:4 * TT]))
                nc.vector.tensor_copy(c.selb[:, 0:P], c.k("cmask"))
                for t, qt in enumerate((1, 2, 3)):
                    nk = P * (qt + 1)
                    x = work[:, t, 0:nk]
                    for h in range(4):
                        dve.wait_ge(reluded, 4 * t + h + 1)
                        r = rel[:, t % 2, h, 0:nk]
                        if h == 0:
                            then(nc.vector.tensor_scalar(x, r, wi[:, qt, 0:1], None, ALU.mult))
                        else:
                            then(nc.vector.scalar_tensor_tensor(out=x, in0=r, scalar=wi[:, qt, h:h + 1], in1=x,
                                                                op0=ALU.mult, op1=ALU.add))
                    then(nc.vector.tensor_tensor(x[:, nk - P:nk], x[:, nk - P:nk], c.k("cmask"), ALU.add))
                    nc.vector.memset(m8[:, :], 0.0).then_inc(accd, 4)
                    dve.wait_ge(accd, 4 * t + 4)
                    for r in range(TOPK // 8):
                        then(nc.vector.max(m8[:, :], x))
                        then(nc.vector.match_replace(x, m8[:, :], x, TAKEN))
                    b = c.selb[:, OFF[qt]:OFF[qt] + nk]
                    then(nc.vector.tensor_scalar(b, x, 0.5 * TAKEN, NEG, ALU.is_gt, ALU.mult))
                    then(nc.vector.tensor_tensor(b[:, nk - P:nk], b[:, nk - P:nk], c.k("cmask"), ALU.add))


def stage_forget_prepare(c):
    nc, a = c.nc, c.a
    with Stage(nc, "fg") as ctx:
        sem = ctx.sem
        sb = lambda x, shape: ctx.enter_context(nc.sbuf_tensor(f"fg_{x}", shape, F32))
        w = sb("w", [P, DC, 8])
        x, ab, e, one, cum = sb("x", [8, T]), sb("ab", [8, T]), sb("e", [8, T]), sb("one", [8, T]), sb("cum", [8, T])
        low = sb("low", [8, T])
        w_in, projected, biased, lg, step, spread = (
            sem(n) for n in ("w_in", "projected", "biased", "lg", "step", "spread"))
        ast = sem("ast")
        with nc.Block("forget") as block:
            @block.sync
            def _(sp):
                sp.dma_start(w[:, :, :], a["w_forget"]).then_inc(w_in, 16)
                sp.wait_ge(step, 4)
                sp.dma_start(c.fneg[0:1, :, :], cum[:, :]).then_inc(spread, 16)
                sp.wait_ge(spread, 16)

            @block.tensor
            def _(pe):
                pe.wait_ge(w_in, 16)
                for j in range(DC):
                    mm = nc.tensor.matmul(c.ps[0:8, 0, :], w[:, j, :], c.xn[:, j, :], start=(j == 0),
                                          stop=(j == DC - 1))
                mm.then_inc(projected, 1)

            @block.scalar
            def _(act):
                act.wait_ge(biased, 1)
                nc.scalar.activation(ab[:, :], x[:, :], ACT.Abs).then_inc(ast, 1)
                act.wait_ge(ast, 1)
                nc.scalar.activation(e[:, :], ab[:, :], ACT.Exp, scale=-1.0).then_inc(ast, 1)
                act.wait_ge(ast, 2)
                nc.scalar.activation(ab[:, :], e[:, :], ACT.Ln, bias=c.k("ones")[0:8, 0:1]).then_inc(lg, 1)

            @block.vector
            def _(dve):
                nc.vector.memset(one[:, :], 1.0).then_inc(step, 1)
                dve.wait_ge(projected, 1)
                fb = PARAMS["fb"][0]
                nc.vector.tensor_scalar(x[:, :], c.ps[0:8, 0, :], c.param[0:8, fb:fb + 1], None, ALU.add)\
                  .then_inc(biased, 1)
                dve.wait_ge(biased, 1)
                nc.vector.tensor_scalar(low[:, :], x[:, :], 0.0, None, ALU.min).then_inc(step, 1)
                dve.wait_ge(lg, 1)
                dve.wait_ge(step, 2)
                nc.vector.tensor_tensor(low[:, :], ab[:, :], low[:, :], ALU.subtract).then_inc(step, 1)
                dve.wait_ge(step, 3)
                nc.vector.tensor_tensor_scan(cum[:, :], one[:, :], low[:, :], 0.0, ALU.mult, ALU.add)\
                  .then_inc(step, 1)


def stage_store(c):
    nc = c.nc
    with Stage(nc, "store") as ctx:
        s = ctx.sem("out")
        with nc.Block("store") as block:
            @block.sync
            def _(sp):
                sp.dma_start(c.a["out"], c.xn[:, :, :]).then_inc(s, 16)
                sp.wait_ge(s, 16)


def build(nc, a, until=None):
    with ExitStack() as ctx:
        c = Chip(nc, ctx, a)

        def tensors(stack, *wanted):
            return [stack.enter_context(nc.sbuf_tensor(n, s, d)) for n, s, d in wanted]

        def parts(stack, name, chunks):
            return tensors(stack, (name + "_high", [P, chunks, T], F32R), (name + "_low", [P, chunks, T], F32R))

        def feed_forward(layer, gain):
            with ExitStack() as outer:
                hidden = parts(outer, f"ff{layer}", FC)
                with ExitStack() as inner:
                    x = parts(inner, f"ffx{layer}", DC)
                    stage_norm(c, f"ffnorm{layer}", gain, x)
                    stage_ffn_up(c, f"up{layer}", layer, a[f"w_ff_up{layer}"], x, hidden)
                stage_back(c, f"down{layer}", a[f"w_ff_down{layer}"], hidden, FC)

        stage_load(c)
        with ExitStack() as outer:
            c.o = parts(outer, "o1", DC)
            with ExitStack() as inner:
                x = parts(inner, "x1", DC)
                (o,) = tensors(inner, ("o1_whole", [P, DC, T], F32))
                c.qgain, c.neglam = tensors(inner, ("qgain", [P, 1], F32), ("neglam", [P, 1], F32))
                stage_norm(c, "norm1", c.p("g_mix"), x)
                stage_diff_prepare(c)
                c.o, split = (o, None), c.o
                stage_attention(c, "diff", "diff", 8, a["w_da"], x, 0, bias=a["alibi"])
                c.o = split
                stage_subln(c, o, c.o)
            stage_back(c, "da_out", a["w_da_out"], c.o, DC)
        if until == 2:
            return c
        with ExitStack() as outer:
            c.slots, c.tiles = tensors(outer, ("slots", [P, 24, 4], I32), ("tiles", [1, 25], I32))
            with ExitStack() as inner:
                x = parts(inner, "x2", DC)
                (c.xn,) = tensors(inner, ("x2_whole", [P, DC, T], F32))
                stage_norm(c, "norm2", c.p("g_ffn"), x, c.xn)
                stage_route(c)
            stage_experts(c)
            stage_combine(c)
        if until == 3:
            return c
        with ExitStack() as outer:
            c.o = parts(outer, "o3", DC)
            with ExitStack() as inner:
                x = parts(inner, "x3", DC)
                c.xn, c.selb = tensors(inner, ("x3_whole", [P, DC, T], F32), ("selb", [P, PW], F32))
                stage_norm(c, "norm3", c.p("g_mix2", 0, DC), x, c.xn)
                stage_select(c)
                stage_attention(c, "dsa", "dsa", 4, a["w_dsa"], x, 0,
                                bias=lambda s, qt: c.selb[:, OFF[qt]:OFF[qt] + P * (qt + 1)])
                stage_attention(c, "rel", "rel", 4, a["w_rel"], x, 4,
                                bias=bass.AP(a["relrows"].tensor, P - 1, [[P * 640, 8], [639, P], [1, T]]))
            stage_back(c, "even_out", a["w_even_out"], c.o, DC)
        feed_forward(0, c.p("g_ffn2", 0, DC))
        if until == 5:
            return c
        with ExitStack() as outer:
            c.o = parts(outer, "o5", DC)
            with ExitStack() as inner:
                x = parts(inner, "x5", DC)
                c.xn, c.fneg = tensors(inner, ("x5_whole", [P, DC, T], F32), ("fneg", [1, 8, T], F32))
                stage_norm(c, "norm5", c.p("g_mix2", DC, DC), x, c.xn)
                stage_forget_prepare(c)
                stage_attention(c, "forget_att", "forget", 4, a["w_fgt"], x, 0,
                                bias=lambda s, qt: c.k("cband")[:, T - P - P * qt:T])
                stage_attention(c, "sink", "sink", 4, a["w_snk"], x, 4,
                                bias=lambda s, qt: c.k("sband")[:, (P if qt == 0 else 0):2 * P])
            stage_back(c, "odd_out", a["w_odd_out"], c.o, DC)
        feed_forward(1, c.p("g_ffn2", DC, DC))
        with ExitStack() as inner:
            x = parts(inner, "x7", DC)
            (c.xn,) = tensors(inner, ("x7_whole", [P, DC, T], F32))
            stage_norm(c, "norm7", c.p("g_out"), x, c.xn)
            stage_store(c)
        return c


def pack(inputs):
    i = {k: np.asarray(v) for k, v in inputs.items()}

    def cols(x):
        return np.ascontiguousarray(x.reshape(-1, P).T)

    def fm(w):
        k, m = w.shape
        return np.ascontiguousarray(w.reshape(k // P, P, m // P, P).transpose(2, 1, 0, 3))

    def mv(w):
        k, m = w.shape
        return np.ascontiguousarray(w.reshape(k // P, P, m).transpose(1, 0, 2))

    def qkv(q, k, v):
        return np.ascontiguousarray(np.stack([fm(q), fm(k), fm(v)], axis=1))

    par = np.zeros((P, N_PARAM), np.float32)

    def put(name, value):
        x, y = PARAMS[name]
        par[:, x:y] = value

    put("g_mix", cols(i["norm_mix"]))
    put("g_ffn", cols(i["norm_ffn"]))
    put("g_mix2", cols(i["norm_mix_g_2"]))
    put("g_ffn2", cols(i["norm_ffn_g_2"]))
    put("g_out", cols(i["norm_out_g_2"]))
    put("qg", np.tile(i["da_q_norm"][0], 2)[:, None])
    put("kg", np.tile(i["da_k_norm"][0], 2)[:, None])
    put("subln", i["da_subln"][0][:, None])
    put("lng", np.tile(i["idx_k_ln_g_2"][0], 2)[:, None])
    put("lnb", np.tile(i["idx_k_ln_b_2"][0], 2)[:, None])
    put("convw", i["ffn_conv_w_2"].reshape(2, 3, 2 * FC, P).transpose(3, 0, 2, 1).reshape(P, -1))
    put("convb", i["ffn_conv_b_2"].reshape(2 * 2 * FC, P).T)
    put("sinks", i["sinks_2"][0][None, :])
    par[0:8, PARAMS["fb"][0]] = i["forget_b_2"][0]
    put("rb", np.concatenate([i["moe_b_group"][0], i["moe_b_router"][0]])[None, :])
    put("lam", np.concatenate([i[f"da_lambda_{x}"][0] for x in ("q1", "k1", "q2", "k2")])[None, :])

    consts, alibi, rec, empty = shape_constants()
    wd = i["da_w_in"][0]
    we, wo = i["even_w_in_2"][0], i["odd_w_in_2"][0]
    ki = we[:, 1792:1856]
    ug = i["ffn_w_up_2"]
    out = {
        "xT": np.ascontiguousarray(i["x"][0].T.reshape(DC, P, T).transpose(1, 0, 2)),
        "params": par, "consts": consts, "alibi": alibi, "rec": rec, "empty": empty,
        "relE": np.ascontiguousarray(i["rel_bias_2"][0][:, np.clip(511 - np.arange(640), -256, 256) + 256]),
        "w_da": qkv(wd[:, 0:1024], wd[:, 1024:2048], wd[:, 2048:3072]),
        "w_da_out": fm(i["da_w_out"][0]),
        "w_route": mv(np.concatenate([i["moe_w_group"][0], i["moe_w_router"][0]], axis=1)),
        "w_gate": np.ascontiguousarray(i["moe_w_gate"][0].reshape(N_EXP, DC, P, D_EXP).transpose(0, 2, 1, 3)),
        "w_up": np.ascontiguousarray(i["moe_w_up"][0].reshape(N_EXP, DC, P, D_EXP).transpose(0, 2, 1, 3)),
        "w_down": np.ascontiguousarray(i["moe_w_down"][0].reshape(N_EXP, 4, P, D).transpose(0, 2, 1, 3)),
        "w_dsa": qkv(we[:, 0:512], we[:, 512:1024], we[:, 1024:1536]),
        "w_idx": fm(np.concatenate([we[:, 1536:1792], ki, ki], axis=1)),
        "w_idxw": mv(we[:, 1856:1860]),
        "w_rel": qkv(we[:, 1860:2372], we[:, 2372:2884], we[:, 2884:3396]),
        "w_even_out": fm(i["even_w_out_2"][0]),
        "w_fgt": qkv(wo[:, 0:512], wo[:, 512:1024], wo[:, 1024:1536]),
        "w_forget": mv(wo[:, 1536:1544]),
        "w_snk": qkv(wo[:, 1544:2056],
                     *(np.concatenate([wo[:, s + HD * g:s + HD * g + HD] for g in (0, 1) for _ in range(4)], axis=1)
                       for s in (2056, 2184))),
        "w_odd_out": fm(i["odd_w_out_2"][0]),
    }
    for layer in range(2):
        f = fm(ug[layer])
        out[f"w_ff_up{layer}"] = np.ascontiguousarray(np.stack([f[:FC], f[FC:]], axis=2))
        out[f"w_ff_down{layer}"] = fm(i["ffn_w_down_2"][layer])
    return out


SCRATCH = {"plist": ((24 * P, 4), I32), "relrows": ((8, P, 640), F32), "hrows": ((T, D), F32),
           "yrows": ((PAIRS, D), F32)}


def kernel(**inputs):
    import concourse.bacc as _bacc
    from concourse.bass_utils import run_bass_kernel_spmd as _run

    nc = _bacc.Bacc("TRN2", target_bir_lowering=False, num_devices=1)
    arrays, a = {}, {}
    for name, x in pack(inputs).items():
        arrays[f"in_{name}"] = x
        a[name] = nc.dram_tensor(f"in_{name}", x.shape, mybir.dt.from_np(x.dtype), kind="ExternalInput").ap()
    for name, (shape, dt) in SCRATCH.items():
        a[name] = nc.dram_tensor(name, shape, dt, kind="Internal").ap()
    a["out"] = nc.dram_tensor("out_0", (P, DC, T), F32, kind="ExternalOutput").ap()
    build(nc, a)
    r = _run(nc, [arrays], core_ids=[0])
    got = r.results[0]["out_0"]
    return np.ascontiguousarray(got.transpose(2, 1, 0).reshape(1, T, D))
```

```python
from contextlib import ExitStack

import numpy as np

import concourse.bass as bass
from concourse import mybir

F32 = mybir.dt.float32
F32R = mybir.dt.float32r
I32 = mybir.dt.int32
U32 = mybir.dt.uint32
ALU = mybir.AluOpType
ACT = mybir.ActivationFunctionType
AX_X = mybir.AxisListType.X

P = 128
T = 512
D = 1024
DC = D // P
TT = T // P
EPS = 1e-6
NEG = -1e30
HUGE = 3e38
TAKEN = -3e38
LAMBDA_INIT = 0.2
HD = 64
QK_SCALE = HD ** -0.5
N_EXP, N_GRP, EPG, D_EXP = 16, 4, 4, 512
PAIRS = 2 * T
MAX_TILES = PAIRS // P + N_EXP - 1
FF = 2816
FC = FF // P
TOPK = min(256, T // 4)
CHUNK = 64

OFF = [0, 128, 384, 768]
PW = 1280

CONSTS = {}
_at = 0
for _n, _w in [("ident", P), ("blk64", P), ("inv_d", P), ("inv_p", P), ("rot", P), ("tri", P), ("ones", P),
               ("cmask", P), ("cband", T), ("sband", 2 * P), ("cos", T), ("sin", T), ("tileid", 24 * N_EXP)]:
    CONSTS[_n] = (_at, _at + _w)
    _at += _w
N_CONST = _at

PARAMS = {}
_at = 0
for _n, _w in [("g_mix", DC), ("g_ffn", DC), ("g_mix2", 2 * DC), ("g_ffn2", 2 * DC), ("g_out", DC), ("qg", 1),
               ("kg", 1), ("subln", 1), ("lng", 1), ("lnb", 1), ("convw", 2 * 2 * FC * 3), ("convb", 2 * 2 * FC),
               ("sinks", 8), ("fb", 1), ("rb", 20), ("lam", 4 * HD)]:
    PARAMS[_n] = (_at, _at + _w)
    _at += _w
N_PARAM = _at


def shape_constants():
    c = np.zeros((P, N_CONST), np.float32)

    def put(name, value):
        a, b = CONSTS[name]
        c[:, a:b] = value

    p = np.arange(P)
    put("ident", np.eye(P))
    put("blk64", (p[:, None] // HD == p[None, :] // HD) / HD)
    put("inv_d", 1.0 / D)
    put("inv_p", 1.0 / P)
    rot = np.zeros((P, P))
    for m in range(P):
        if m % HD < HD // 2:
            rot[m + HD // 2, m] = -1.0
        else:
            rot[m - HD // 2, m] = 1.0
    put("rot", rot)
    put("tri", p[:, None] < p[None, :])
    put("ones", 1.0)
    later = np.where(p[None, :] // CHUNK <= p[:, None] // CHUNK, 0.0, NEG)
    put("cmask", later)
    band = np.arange(T)[None, :] - (T - P)
    dist = p[:, None] - band
    put("cband", np.where(dist >= 0, 0.0, NEG))
    window = np.arange(2 * P)[None, :] - P
    gap = p[:, None] // CHUNK - window // CHUNK
    put("sband", np.where((gap >= 0) & (gap <= 2), 0.0, NEG))
    inv = (1.0 / (np.float32(10000.0) ** (np.arange(0, HD, 2, dtype=np.float32) / np.float32(HD)))).astype(np.float32)
    ang = (np.arange(T, dtype=np.float32)[:, None] * inv[None, :]).astype(np.float32)
    put("cos", np.cos(ang).T[p % (HD // 2)])
    put("sin", np.sin(ang).T[p % (HD // 2)])
    put("tileid", np.repeat(np.arange(24), N_EXP)[None, :])
    slopes = (2.0 ** (-8.0 * np.arange(1, 9) / 8)).astype(np.float32)
    alibi = np.where(dist >= 0, -slopes[:, None, None] * dist.astype(np.float32), np.float32(NEG)).astype(np.float32)
    rec = np.zeros((P, 2, TT, 4), np.int32)
    tok = np.arange(TT)[None, :] * P + p[:, None]
    for k in range(2):
        rec[:, k, :, 0] = tok
        rec[:, k, :, 1] = k * T + tok
    empty = np.zeros((24 * P, 4), np.int32)
    empty[:, 0] = T
    empty[:, 1] = PAIRS
    return c, alibi, rec, empty


def emit_wait(eng, sem, value):
    if isinstance(value, int) and value <= 0:
        return
    eng.wait_ge(sem, value)


def wait_apart(eng, sem, value, passed):
    emit_wait(eng, sem, value)
    eng.sem_inc(passed, 1)


def repeat(eng, n, body, peel=1):
    for i in range(peel):
        body(i)
    with eng.Fori(peel, n) as i:
        body(i)


class Stage(ExitStack):

    def __init__(self, nc, name):
        super().__init__()
        self.nc, self.name, self.sems = nc, name, []

    def sem(self, name):
        s = self.nc.alloc_semaphore(f"{self.name}_{name}")
        self.sems.append(s)
        return s

    def dma_sem(self, name):
        return self.nc.alloc_semaphore(f"{self.name}_{name}")

    def __exit__(self, *exc):
        if exc[0] is None:
            for s in self.sems:
                self.nc.gpsimd.sem_clear(s)
                self.nc.release_semaphore(s)
        return super().__exit__(*exc)


class Chip:

    def __init__(self, nc, ctx, a):
        self.nc, self.ctx, self.a = nc, ctx, a

        def sb(name, shape, dt=F32):
            return ctx.enter_context(nc.sbuf_tensor(name, shape, dt))

        self.ps = ctx.enter_context(nc.psum_tensor("ps", [P, 8, 512], F32))
        self.const = sb("const", [P, N_CONST])
        self.param = sb("param", [P, N_PARAM])
        self.h = sb("h", [P, DC, T])
        self.eps = sb("eps", [P, 1])
        self.zero = sb("zero", [P, 1])
        self.list_empty = nc.alloc_semaphore("list_empty")
        self.rel_spread = nc.alloc_semaphore("rel_spread")

    def product(self, out, w, x, start, stop):
        (wh, wl), (xh, xl) = w, x
        mm = self.nc.tensor.matmul
        mm(out, wh, xh, start=start, stop=False)
        mm(out, wh, xl, start=False, stop=False)
        return mm(out, wl, xh, start=False, stop=stop)

    def k(self, name):
        x, y = CONSTS[name]
        return self.const[:, x:y]

    def p(self, name, i=0, n=None):
        x, y = PARAMS[name]
        return self.param[:, x + i:(y if n is None else x + i + n)]

    def bank(self, i):
        return self.ps[:, i, :]


def stage_load(c):
    nc, a = c.nc, c.a
    with Stage(nc, "load") as ctx:
        s_in = ctx.sem("in")
        with nc.Block("load") as block:
            @block.sync
            def _(sp):
                sp.dma_start(c.h[:, :, :], a["xT"]).then_inc(s_in, 16)
                sp.dma_start(c.const[:, :], a["consts"]).then_inc(s_in, 16)
                sp.dma_start(c.param[:, :], a["params"]).then_inc(s_in, 16)
                sp.wait_ge(s_in, 48)
            @block.vector
            def _(dve):
                nc.vector.memset(c.eps[:, :], EPS)
                nc.vector.memset(c.zero[:, :], 0.0)


def stage_norm(c, name, gain, x, whole, ahead=None):
    nc = c.nc
    with Stage(nc, name) as ctx:
        sem = ctx.sem
        lg = ctx.enter_context(nc.sbuf_tensor(f"{name}_lg", [P, T], F32))
        rs = ctx.enter_context(nc.sbuf_tensor(f"{name}_rs", [P, T], F32))
        sq = y = whole
        squared, squared_v, summed, logged, inverted, scaled, rounded = (
            sem(n) for n in ("squared", "squared_v", "summed", "logged", "inverted", "scaled", "rounded"))
        with nc.Block(name) as block:
            @block.sync
            def _(sp):
                if ahead:
                    ahead[0](sp)

            @block.scalar
            def _(act):
                for i in range(0, DC, 2):
                    nc.scalar.activation(sq[:, i, :], c.h[:, i, :], ACT.Square).then_inc(squared, 1)
                if ahead:
                    ahead[1](act)
                act.wait_ge(summed, 1)
                nc.scalar.activation(lg[:, :], c.bank(0), ACT.Ln, bias=c.eps[:, 0:1]).then_inc(logged, 1)
                act.wait_ge(logged, 1)
                nc.scalar.activation(rs[:, :], lg[:, :], ACT.Exp, scale=-0.5).then_inc(inverted, 1)
                for i in range(DC if x else 0):
                    act.wait_ge(scaled, i + 1)
                    nc.scalar.copy(x[0][:, i, :], y[:, i, :]).then_inc(rounded, 1)

            @block.tensor
            def _(pe):
                for i in range(DC):
                    pe.wait_ge((squared, squared_v)[i % 2], i // 2 + 1)
                    mm = nc.tensor.matmul(c.bank(0), c.k("inv_d"), sq[:, i, :], start=(i == 0), stop=(i == DC - 1))
                mm.then_inc(summed, 1)

            @block.vector
            def _(dve):
                for i in range(1, DC, 2):
                    nc.vector.tensor_tensor(sq[:, i, :], c.h[:, i, :], c.h[:, i, :], ALU.mult).then_inc(squared_v, 1)
                dve.wait_ge(inverted, 1)
                for i in range(DC):
                    nc.vector.scalar_tensor_tensor(out=y[:, i, :], in0=c.h[:, i, :], scalar=gain[:, i:i + 1],
                                                   in1=rs[:, :], op0=ALU.mult, op1=ALU.mult).then_inc(scaled, 1)
                    if x and i % 2:
                        dve.wait_ge(rounded, i)
                        nc.vector.tensor_tensor(x[1][:, i - 1, :], y[:, i - 1, :], x[0][:, i - 1, :].bitcast(F32),
                                                ALU.subtract)

            @block.gpsimd
            def _(pool):
                if ahead:
                    ahead[2](pool)
                for i in range(1, DC if x else 0, 2):
                    pool.wait_ge(rounded, i + 1)
                    nc.gpsimd.tensor_tensor(x[1][:, i, :], y[:, i, :], x[0][:, i, :].bitcast(F32), ALU.subtract)


def stage_back(c, name, w, src, nk):
    nc = c.nc
    hk = nk // 2
    with Stage(nc, name) as ctx:
        sem = ctx.sem
        slab = [ctx.enter_context(nc.sbuf_tensor(f"{name}_w{i}", [P, hk, P], F32)) for i in range(2)]
        high = [ctx.enter_context(nc.sbuf_tensor(f"{name}_wh{i}", [P, hk, P], F32R)) for i in range(2)]
        low = [ctx.enter_context(nc.sbuf_tensor(f"{name}_wl{i}", [P, hk, P], F32R)) for i in range(2)]
        w_in = [sem(f"w_in{i}") for i in range(2)]
        rounded, split, used, added = (sem(n) for n in ("rounded", "split", "used", "added"))
        with nc.Block(name) as block:
            @block.sync
            def _(sp):
                def load(i):
                    for b in range(2):
                        emit_wait(sp, split, 2 * i - 1 + b)
                        sp.dma_start(slab[b][:, :, :], w[bass.ds(i, 1), :, b * hk:b * hk + hk]
                                     .rearrange("a p k m -> (a p) k m")).then_inc(w_in[b], 16)
                repeat(sp, DC, load)

            @block.scalar
            def _(act):
                def round_(i):
                    for b in range(2):
                        act.wait_ge(w_in[b], 16 * i + 16)
                        emit_wait(act, used, 2 * i - 1 + b)
                        nc.scalar.copy(high[b][:, :, :], slab[b][:, :, :]).then_inc(rounded, 1)
                repeat(act, DC, round_)

            @block.tensor
            def _(pe):
                def project(i):
                    for e in range(2):
                        emit_wait(pe, added, 2 * i - 1 + e)
                        for b in range(2):
                            pe.wait_ge(split, 4 * i + 2 * e + b + 1)
                            for j in range(hk):
                                mm = c.product(c.bank(e), (high[b][:, j, :], low[b][:, j, :]),
                                               (src[0][:, b * hk + j, :], src[1][:, b * hk + j, :]),
                                               b == 0 and j == 0, b == 1 and j == hk - 1)
                            mm.then_inc(used, 1)
                repeat(pe, DC // 2, project)

            @block.vector
            def _(dve):
                def rest(i, b):
                    dve.wait_ge(rounded, 2 * i + b + 1)
                    nc.vector.tensor_tensor(low[b][:, :, :], slab[b][:, :, :], high[b][:, :, :].bitcast(F32),
                                            ALU.subtract).then_inc(split, 1)

                def add(i, last=False):
                    for e in range(2):
                        more = not (last and e == 1)
                        if more:
                            rest(2 * i + e + 1, 0)
                        dve.wait_ge(used, 4 * i + 2 * e + 2)
                        hc = c.h[:, bass.ds(2 * i + e, 1), :].rearrange("p a t -> p (a t)")
                        nc.vector.tensor_tensor(hc, c.bank(e), hc, ALU.add).then_inc(added, 1)
                        if more:
                            rest(2 * i + e + 1, 1)

                rest(0, 0)
                rest(0, 1)
                add(0)
                with dve.Fori(1, DC // 2 - 1) as i:
                    add(i)
                add(DC // 2 - 1, last=True)


class Weights:

    def __init__(self, c, stack, name):
        new = lambda x, dt: stack.enter_context(c.nc.sbuf_tensor(f"{name}_{x}", [P, 3, DC, P], dt))
        self.slab, self.high, self.low = new("w", F32), new("wh", F32R), new("wl", F32R)


def weights_ahead(c, stage, wt, w):
    landed, rounded = ([stage.sem(f"{n}_{j}") for j in "qkv"] for n in ("ahead_in", "ahead_rounded"))

    def load(sp):
        for i in range(3):
            sp.dma_start(wt.slab[:, i, :, :], w[0:1, i].rearrange("a p k m -> (a p) k m")).then_inc(landed[i], 16)

    def round_(act):
        for i in range(3):
            act.wait_ge(landed[i], 16)
            c.nc.scalar.copy(wt.high[:, i, :, :], wt.slab[:, i, :, :]).then_inc(rounded[i], 1)

    def rest(pool):
        for i in range(3):
            pool.wait_ge(rounded[i], 1)
            c.nc.gpsimd.tensor_tensor(wt.low[:, i, :, :], wt.slab[:, i, :, :], wt.high[:, i, :, :].bitcast(F32),
                                      ALU.subtract)

    return load, round_, rest


def stage_attention(c, name, kind, n, wt, w, x, first, bias=None, bias_ready=None, next_w=None, aside=None):
    nc = c.nc
    diff, rope = kind == "diff", kind in ("dsa", "sink")
    banded = kind in ("diff", "rel")
    direct = kind in ("rel", "forget")
    comb = 1 if diff else 2
    order = [(3, 0), (3, 1), (2, 0), (2, 1), (1, 0), (0, 0), (1, 1), (0, 1)]
    col = {(3, 0): 0, (3, 1): 1, (2, 0): 2, (2, 1): 3, (1, 0): 4, (1, 1): 5, (0, 0): 6, (0, 1): 7}
    scored_at = [1, 2, 3, 4, 5, 5, 6, 6]
    seq = {t: i + 1 for i, t in enumerate(order)}

    def keys(qt):
        return (128 * max(qt - 1, 0) if kind == "sink" else 0), 128 * (qt + 1)

    def score_bank(qt, s):
        k0, k1 = keys(qt)
        if qt == 3:
            return c.ps[:, s, 0:k1 - k0]
        if qt == 2:
            return c.ps[:, 2 + s, 0:k1 - k0]
        return c.ps[:, s, 0:k1 - k0] if qt == 1 else c.ps[:, s, 256:384]

    with Stage(nc, name) as ctx:
        sem = ctx.sem
        sb = lambda x, shape: ctx.enter_context(nc.sbuf_tensor(f"{name}_{x}", shape, F32))
        slab, high, low = wt.slab, wt.high, wt.low
        qT, kT, vT, v = sb("qT", [P, T]), sb("kT", [P, T]), sb("vT", [P, T]), sb("v", [P, TT, P])
        raw = None if direct else sb("raw", [P, 2, T])
        tmp = None if direct else sb("tmp", [P, 2, T])
        tmp2 = None if direct else sb("tmp2", [P, 2, T])
        prob = sb("prob", [P, 2, PW])
        probT = sb("probT", [P, comb, TT, T])
        btile = sb("btile", [P, 1 if diff else 2, T]) if banded else None
        nmax, total, inv = sb("nmax", [P, 8]), sb("total", [P, 8]), sb("inv", [P, 8])
        esink = sb("esink", [P, 8]) if kind == "sink" else None
        sink_u = sb("sink_u", [P, 2, 2]) if kind == "sink" else None
        (q_in, k_in, v_in, b_in, b_ok, q_proj, k_proj, v_proj, q_raw, k_raw, q_help, k_help, q_half, k_half, q_half2,
         k_half2, q_ok, k_ok, v_ok, scored, shifted, expd, inv_ok, inv2_ok, scaled, normed, turned, copied, pv_done,
         o_ok, sink_ok) = (
            sem(x) for x in ("q_in", "k_in", "v_in", "b_in", "b_ok", "q_proj", "k_proj", "v_proj", "q_raw", "k_raw",
                             "q_help", "k_help", "q_half", "k_half", "q_half2", "k_half2", "q_ok", "k_ok", "v_ok",
                             "scored", "shifted", "expd", "inv_ok", "inv2_ok", "scaled", "normed", "turned",
                             "copied", "pv_done", "o_ok", "sink_ok"))
        v_copied, v_turned = sem("v_copied"), sem("v_turned")
        rounded, split = ([sem(f"{i}_{j}") for j in "qkv"] for i in ("rounded", "split"))
        o_high, logged = sem("o_high"), sem("logged")
        passed_pe, passed_dve = sem("passed_pe"), sem("passed_dve")
        ngrp = 4 if diff else 8

        def sl(s, qt):
            k0, k1 = keys(qt)
            return prob[:, s, OFF[qt]:OFF[qt] + k1 - k0]

        def bias_tile(s, qt):
            if kind == "diff":
                return btile[:, 0, T - P - P * qt:T]
            if kind == "rel":
                return btile[:, s, T - P - P * qt:T]
            return bias(s, qt)

        def rounds(body, eng):
            body(0, True, False, True)
            with eng.Fori(1, n - 1) as u:
                body(u, True, True, True)
            body(n - 1, True, True, next_w is not None)
            body(n, False, True, False)

        with nc.Block(name) as block:
            @block.sync
            def _(sp):
                def load_bias(u):
                    if banded:
                        emit_wait(sp, shifted, u * 8)
                        nb = 1 if diff else 2
                        src = bias[bass.ds(u * nb, nb)] if not isinstance(u, int) else bias[u * nb:(u + 1) * nb]
                        sp.dma_start(btile[:, :, :], src.rearrange("h p m -> p h m")).then_inc(b_in, 16)
                def load(u, w, at):
                    for i, landed in enumerate((q_in, k_in, v_in)):
                        emit_wait(sp, split[i], u - 1)
                        src = w[bass.ds(at, 1), i] if not isinstance(at, int) else w[at:at + 1, i]
                        sp.dma_start(slab[:, i, :, :], src.rearrange("a p k m -> (a p) k m")).then_inc(landed, 16)

                if bias_ready is not None:
                    sp.wait_ge(bias_ready, 16)
                load(1, w, 1)
                load_bias(0)
                load_bias(1)
                with sp.Fori(2, n) as u:
                    load(u, w, u)
                    load_bias(u)
                if next_w is not None:
                    load(n, next_w, 0)

            @block.gpsimd
            def _(pool):
                def rest(i, u):
                    pool.wait_ge(rounded[i], u)
                    nc.gpsimd.tensor_tensor(low[:, i, :, :], slab[:, i, :, :], high[:, i, :, :].bitcast(F32),
                                            ALU.subtract).then_inc(split[i], 1)

                if kind == "rel":
                    def mask(u):
                        pool.wait_ge(b_in, 16 * u + 16)
                        for s in range(2):
                            d = btile[:, s, T - P:T]
                            nc.gpsimd.tensor_tensor(d, d, c.k("cmask"), ALU.add).then_inc(b_ok, 1)
                if rope:
                    def turn(u, i):
                        have, half, ready = ((q_raw, q_half, q_ok), (k_raw, k_half, k_ok))[i]
                        pool.wait_ge(have, u + 1)
                        emit_wait(pool, ready, u)
                        nc.gpsimd.tensor_tensor(tmp[:, i, :], raw[:, i, :], c.k("cos"), ALU.mult).then_inc(half, 1)

                def body(u, project, attend, ahead):
                    if kind == "rel" and project:
                        mask(u)
                    for i in range(3):
                        if ahead:
                            rest(i, u + 1)
                        if rope and project and i < 2:
                            turn(u, i)

                rounds(body, pool)

            @block.tensor
            def _(pe):
                def scores(u, tiles):
                    for qt, s in tiles:
                        k0, k1 = keys(qt)
                        out, hd = score_bank(qt, s), slice(HD * s, HD * s + HD)
                        if kind == "forget":
                            f = c.fneg[0:1, bass.ds(2 * (u - 1) + s, 1), k0:k1].rearrange("p a t -> p (a t)")
                            nc.tensor.matmul(out, c.k("ones")[0:1, :], f, start=True, stop=False)
                        mm = nc.tensor.matmul(out, qT[hd, P * qt:P * qt + P], kT[hd, k0:k1],
                                              start=(kind != "forget"), stop=True)
                        if qt != 1:
                            mm.then_inc(scored, 1)

                def turn(u, g):
                    for j in range(TT):
                        if g:
                            pe.wait_ge(copied, (u - 1) * 4 * comb + j + 1)
                        for qt in range(j, min(TT, j + 2) if kind == "sink" else TT):
                            k0, _ = keys(qt)
                            at = OFF[qt] + P * j - k0
                            mm = nc.tensor.transpose(c.ps[:, j, P * qt:P * qt + P], prob[:, g, at:at + P],
                                                     c.k("ident"))
                        mm.then_inc(turned, 1)

                def project_fm(slot, bank_i, done, u):
                    emit_wait(pe, split[slot], u)
                    for i in range(DC):
                        mm = c.product(c.bank(bank_i), (high[:, slot, i, :], low[:, slot, i, :]),
                                       (x[0][:, i, :], x[1][:, i, :]), i == 0, i == DC - 1)
                    mm.then_inc(done, 1)

                def turn_v(u):
                    pe.wait_ge(v_copied, u + 1)
                    for j in range(TT):
                        mm = nc.tensor.transpose(c.ps[:, 6, P * j:P * j + P], vT[:, P * j:P * j + P], c.k("ident"))
                    mm.then_inc(v_turned, 1)

                def help_fm(i, bank_i, have, done, u):
                    pe.wait_ge(have, u + 1)
                    nc.tensor.matmul(c.bank(bank_i), c.k("rot") if rope else c.k("blk64"),
                                     raw[:, i, :] if rope else tmp[:, i, :], start=True, stop=True).then_inc(done, 1)

                def body(u, project, attend, ahead):
                    if attend:
                        pe.wait_ge(q_ok, u)
                        wait_apart(pe, k_ok, u, passed_pe)
                        scores(u, order[:4])
                    if project:
                        emit_wait(pe, q_ok, u)
                        project_fm(0, 4, q_proj, u)
                    if attend:
                        wait_apart(pe, shifted, (u - 1) * 8 + 1, passed_pe)
                        scores(u, order[4:6])
                        wait_apart(pe, shifted, (u - 1) * 8 + 2, passed_pe)
                        scores(u, order[6:])
                    if project:
                        emit_wait(pe, k_ok, u)
                        project_fm(1, 5, k_proj, u)
                        if not direct:
                            help_fm(0, 4, q_raw, q_help, u)
                    if attend:
                        pe.wait_ge(normed, ngrp * u)
                        turn(u, 0)
                    if project:
                        if not direct:
                            help_fm(1, 5, k_raw, k_help, u)
                        emit_wait(pe, v_ok, u)
                        project_fm(2, 6, v_proj, u)
                    if attend and comb == 2:
                        turn(u, 1)
                    if attend:
                        pe.wait_ge(v_ok, u)
                        for g in range(comb):
                            rows = slice(0, P) if diff else slice(HD * g, HD * g + HD)
                            if kind != "sink":
                                for j in range(TT):
                                    pe.wait_ge(copied, (u - 1) * 4 * comb + 4 * g + j + 1)
                                    mm = nc.tensor.matmul(c.ps[rows, 7, P * j:T], v[:, j, rows],
                                                          probT[:, g, j, P * j:T], start=(j == 0), stop=(j == TT - 1))
                            else:
                                pe.wait_ge(copied, (u - 1) * 4 * comb + 4 * g + TT)
                                for qt in range(TT):
                                    for j in range(max(qt - 1, 0), qt + 1):
                                        mm = nc.tensor.matmul(
                                            c.ps[rows, 7, P * qt:P * qt + P], v[:, j, rows],
                                            probT[:, g, j, P * qt:P * qt + P], start=(j == max(qt - 1, 0)),
                                            stop=(j == qt))
                        mm.then_inc(pv_done, 1)
                    if project:
                        turn_v(u)
                rounds(body, pe)

            @block.scalar
            def _(act):
                def exps(u, tiles):
                    for qt, s in tiles:
                        i = col[qt, s]
                        act.wait_ge(shifted, (u - 1) * 8 + seq[qt, s])
                        if kind == "sink":
                            nc.scalar.activation(esink[:, i:i + 1], nmax[:, i:i + 1], ACT.Exp,
                                                 bias=sink_u[:, s, 0:1])
                        nc.scalar.activation(sl(s, qt), sl(s, qt), ACT.Exp, bias=nmax[:, i:i + 1], scale=-1.0,
                                             accum_out=total[:, i:i + 1]).then_inc(expd, 1)

                def copy_turned(u, g):
                    for j in range(TT):
                        hi = min(T, P * (j + 2)) if kind == "sink" else T
                        act.wait_ge(turned, (u - 1) * 4 * comb + 4 * g + j + 1)
                        nc.scalar.copy(probT[:, g, j, P * j:hi], c.ps[:, j, P * j:hi]).then_inc(copied, 1)

                def round_(i, landed, used, u):
                    act.wait_ge(landed, 16 * u)
                    act.wait_ge(used, u)
                    nc.scalar.copy(high[:, i, :, :], slab[:, i, :, :]).then_inc(rounded[i], 1)

                def raw_out(i, bank_i, proj, have, u):
                    act.wait_ge(proj, u + 1)
                    if diff:
                        nc.scalar.copy(raw[:, i, :], c.bank(bank_i))
                        nc.scalar.activation(tmp[:, i, :], c.bank(bank_i), ACT.Square).then_inc(have, 1)
                    else:
                        nc.scalar.activation(raw[:, i, :], c.bank(bank_i), ACT.Copy,
                                             scale=QK_SCALE if i == 0 else 1.0).then_inc(have, 1)

                def body(u, project, attend, ahead):
                    if attend:
                        exps(u, order[:4])
                    if project and not direct:
                        emit_wait(act, q_ok, u)
                        raw_out(0, 4, q_proj, q_raw, u)
                    if attend:
                        exps(u, order[4:])
                    if ahead:
                        round_(0, q_in, q_proj, u + 1)
                    if project and not direct:
                        emit_wait(act, k_ok, u)
                        raw_out(1, 5, k_proj, k_raw, u)
                    if ahead and not direct:
                        round_(1, k_in, k_proj, u + 1)
                    if project and direct:
                        if attend:
                            act.wait_ge(scored, 6 * u)
                        act.wait_ge(q_proj, u + 1)
                        nc.scalar.activation(qT[:, :], c.bank(4), ACT.Copy, scale=QK_SCALE).then_inc(q_ok, 1)
                        act.wait_ge(k_proj, u + 1)
                        nc.scalar.activation(kT[:, :], c.bank(5), ACT.Copy).then_inc(k_ok, 1)
                    if ahead and direct:
                        round_(1, k_in, k_proj, u + 1)
                    if attend:
                        for g in range(comb):
                            copy_turned(u, g)
                    if project and diff:
                        for i, (helped, bank_i) in enumerate(((q_help, 4), (k_help, 5))):
                            act.wait_ge(helped, u + 1)
                            nc.scalar.activation(tmp[:, i, :], c.bank(bank_i), ACT.Ln, bias=c.eps[:, 0:1])\
                              .then_inc(logged, 1)
                        for i, half in enumerate((q_half, k_half)):
                            act.wait_ge(logged, 2 * u + i + 1)
                            nc.scalar.activation(tmp[:, i, :], tmp[:, i, :], ACT.Exp, scale=-0.5).then_inc(half, 1)
                    if project:
                        act.wait_ge(v_proj, u + 1)
                        nc.scalar.copy(vT[:, :], c.bank(6)).then_inc(v_copied, 1)
                    if ahead:
                        round_(2, v_in, v_proj, u + 1)
                    if attend:
                        act.wait_ge(pv_done, u)
                        oc = c.o[0][:, bass.ds(first + u - 1, 1), :].rearrange("p a t -> p (a t)")
                        nc.scalar.copy(oc, c.bank(7)).then_inc(o_ok if diff else o_high, 1)

                rounds(body, act)

            @block.vector
            def _(dve):
                def shift(u, tiles, at):
                    for t, (qt, s) in enumerate(tiles):
                        i = col[qt, s]
                        wait_apart(dve, scored, (u - 1) * 6 + scored_at[at + t], passed_dve)
                        nc.vector.tensor_tensor_reduce(
                            out=sl(s, qt), in0=score_bank(qt, s), in1=bias_tile(s, qt), scale=-1.0,
                            scalar=(sink_u[:, s, 1:2] if kind == "sink" else HUGE), op0=ALU.add, op1=ALU.min,
                            accum_out=nmax[:, i:i + 1]).then_inc(shifted, 1)

                def normalise(u, tiles, half):
                    x = slice(4 * half, 4 * half + 4)
                    dve.wait_ge(expd, (u - 1) * 8 + 4 * half + 4)
                    if kind == "sink":
                        nc.vector.tensor_tensor(total[:, x], total[:, x], esink[:, x], ALU.add).then_inc(inv2_ok, 1)
                        dve.wait_ge(inv2_ok, (u - 1) * 2 + half + 1)
                    nc.vector.reciprocal(inv[:, x], total[:, x]).then_inc(inv_ok, 1)
                    dve.wait_ge(inv_ok, (u - 1) * 2 + half + 1)
                    if diff:
                        odd = inv[:, 4 * half + 1:4 * half + 4:2]
                        nc.vector.tensor_scalar(odd, odd, c.neglam[:, 0:1], None, ALU.mult).then_inc(inv2_ok, 1)
                        qts = [3, 2] if half == 0 else [1, 0]
                        for qt in qts:
                            i = col[qt, 0]
                            nc.vector.tensor_scalar(sl(0, qt), sl(0, qt), inv[:, i:i + 1], None, ALU.mult)\
                              .then_inc(scaled, 1)
                        dve.wait_ge(inv2_ok, (u - 1) * 2 + half + 1)
                        for m, qt in enumerate(qts):
                            i = col[qt, 1]
                            dve.wait_ge(scaled, (u - 1) * 4 + 2 * half + m + 1)
                            nc.vector.scalar_tensor_tensor(out=sl(0, qt), in0=sl(1, qt), scalar=inv[:, i:i + 1],
                                                           in1=sl(0, qt), op0=ALU.mult, op1=ALU.add)\
                              .then_inc(normed, 1)
                    else:
                        for qt, s in tiles:
                            i = col[qt, s]
                            nc.vector.tensor_scalar(sl(s, qt), sl(s, qt), inv[:, i:i + 1], None, ALU.mult)\
                              .then_inc(normed, 1)

                def finish(i, bank_i, half, half2, helped, dst, gain, ok, u):
                    if diff:
                        dve.wait_ge(half, u + 1)
                        nc.vector.scalar_tensor_tensor(out=dst, in0=raw[:, i, :], scalar=gain, in1=tmp[:, i, :],
                                                       op0=ALU.mult, op1=ALU.mult).then_inc(ok, 1)
                    else:
                        dve.wait_ge(helped, u + 1)
                        nc.vector.tensor_tensor(tmp2[:, i, :], c.bank(bank_i), c.k("sin"), ALU.mult)\
                          .then_inc(half2, 1)
                        dve.wait_ge(half, u + 1)
                        dve.wait_ge(half2, u + 1)
                        nc.vector.tensor_tensor(dst, tmp[:, i, :], tmp2[:, i, :], ALU.add).then_inc(ok, 1)

                def body(u, project, attend, ahead):
                    if attend:
                        if banded:
                            dve.wait_ge(b_in if diff else b_ok, 16 * u if diff else 2 * u)
                        if kind == "sink":
                            s0 = PARAMS["sinks"][0]
                            pair = c.param[:, bass.ds(s0 + 2 * (u - 1), 2)]
                            nc.vector.tensor_copy(sink_u[:, :, 0], pair).then_inc(sink_ok, 1)
                            nc.vector.tensor_scalar(sink_u[:, :, 1], pair, -1.0, None, ALU.mult).then_inc(sink_ok, 1)
                            dve.wait_ge(sink_ok, 2 * u)
                        shift(u, order[:4], 0)
                        normalise(u, order[:4], 0)
                        shift(u, order[4:], 4)
                        normalise(u, order[4:], 1)
                    if aside:
                        aside(dve, u, passed_dve)
                    if project and not direct:
                        finish(0, 4, q_half, q_half2, q_help, qT[:, :], c.qgain[:, 0:1] if diff else None, q_ok, u)
                        finish(1, 5, k_half, k_half2, k_help, kT[:, :], c.p("kg") if diff else None, k_ok, u)
                    if project:
                        dve.wait_ge(v_turned, u + 1)
                        if attend:
                            dve.wait_ge(pv_done, u)
                        nc.vector.tensor_copy(v[:, :, :].rearrange("p a e -> p (a e)"), c.bank(6)).then_inc(v_ok, 1)
                    if attend and not diff:
                        dve.wait_ge(o_high, u)
                        at = bass.ds(first + u - 1, 1)
                        nc.vector.tensor_tensor(
                            c.o[1][:, at, :].rearrange("p a t -> p (a t)"), c.bank(7),
                            c.o[0][:, at, :].bitcast(F32).rearrange("p a t -> p (a t)"), ALU.subtract)\
                          .then_inc(o_ok, 1)
                rounds(body, dve)


def stage_diff_prepare(c):
    nc = c.nc
    with Stage(nc, "dprep") as ctx:
        sem = ctx.sem
        scratch = ctx.enter_context(nc.sbuf_tensor("dprep_s", [P, 2, HD], F32))
        dots = ctx.enter_context(nc.sbuf_tensor("dprep_d", [P, 2], F32))
        ex = ctx.enter_context(nc.sbuf_tensor("dprep_e", [P, 2], F32))
        dif = ctx.enter_context(nc.sbuf_tensor("dprep_f", [P, 1], F32))
        dotted, expd, step = sem("dotted"), sem("expd"), sem("step")
        with nc.Block("dprep") as block:
            @block.sync
            def _(sp):
                sp.dma_start(c.a["plist"], c.a["empty"]).then_inc(c.list_empty, 16)
                sp.dma_start(c.a["relrows"], bass.AP(c.a["relE"].tensor, 0, [[640, 8], [0, P], [1, 640]]))\
                  .then_inc(c.rel_spread, 16)

            @block.vector
            def _(dve):
                for i in range(2):
                    nc.vector.tensor_tensor_reduce(
                        out=scratch[:, i, :], in0=c.p("lam", 2 * i * HD, HD), in1=c.p("lam", (2 * i + 1) * HD, HD),
                        scale=1.0, scalar=0.0, op0=ALU.mult, op1=ALU.add, accum_out=dots[:, i:i + 1])\
                      .then_inc(dotted, 1)
                nc.vector.tensor_scalar(c.qgain[:, :], c.p("qg"), QK_SCALE, None, ALU.mult)
                dve.wait_ge(expd, 1)
                nc.vector.tensor_tensor(dif[:, :], ex[:, 1:2], ex[:, 0:1], ALU.subtract).then_inc(step, 1)
                dve.wait_ge(step, 1)
                nc.vector.tensor_scalar(c.neglam[:, :], dif[:, :], LAMBDA_INIT, None, ALU.subtract)

            @block.scalar
            def _(act):
                act.wait_ge(dotted, 2)
                nc.scalar.activation(ex[:, :], dots[:, :], ACT.Exp).then_inc(expd, 1)


def stage_subln(c, o, parts):
    nc = c.nc
    with Stage(nc, "subln") as ctx:
        sem = ctx.sem
        sq = ctx.enter_context(nc.sbuf_tensor("subln_sq", [P, DC, T], F32))
        rs = ctx.enter_context(nc.sbuf_tensor("subln_rs", [P, DC, T], F32))
        g = ctx.enter_context(nc.sbuf_tensor("subln_g", [P, 1], F32))
        squared, meaned, logged, inverted, gained, scaled, rounded = (
            sem(n) for n in ("squared", "meaned", "logged", "inverted", "gained", "scaled", "rounded"))
        with nc.Block("subln") as block:
            @block.scalar
            def _(act):
                for i in range(DC):
                    nc.scalar.activation(sq[:, i, :], o[:, i, :], ACT.Square).then_inc(squared, 1)
                for i in range(DC):
                    act.wait_ge(meaned, i + 1)
                    nc.scalar.activation(sq[:, i, :], c.bank(i), ACT.Ln, bias=c.eps[:, 0:1]).then_inc(logged, 1)
                for i in range(DC):
                    act.wait_ge(logged, i + 1)
                    nc.scalar.activation(rs[:, i, :], sq[:, i, :], ACT.Exp, scale=-0.5).then_inc(inverted, 1)
                    act.wait_ge(scaled, i + 1)
                    nc.scalar.copy(parts[0][:, i, :], o[:, i, :]).then_inc(rounded, 1)

            @block.tensor
            def _(pe):
                for i in range(DC):
                    pe.wait_ge(squared, i + 1)
                    nc.tensor.matmul(c.bank(i), c.k("inv_p"), sq[:, i, :], start=True, stop=True)\
                      .then_inc(meaned, 1)

            @block.vector
            def _(dve):
                nc.vector.tensor_scalar(g[:, :], c.p("subln"), 1.0 - LAMBDA_INIT, None, ALU.mult).then_inc(gained, 1)
                dve.wait_ge(gained, 1)
                for i in range(DC):
                    dve.wait_ge(inverted, i + 1)
                    nc.vector.scalar_tensor_tensor(out=o[:, i, :], in0=o[:, i, :], scalar=g[:, 0:1],
                                                   in1=rs[:, i, :], op0=ALU.mult, op1=ALU.mult).then_inc(scaled, 1)

            @block.gpsimd
            def _(pool):
                for i in range(DC):
                    pool.wait_ge(rounded, i + 1)
                    nc.gpsimd.tensor_tensor(parts[1][:, i, :], o[:, i, :], parts[0][:, i, :].bitcast(F32),
                                            ALU.subtract)


def stage_ffn_up(c, name, layer, w, gain, out):
    nc = c.nc
    with Stage(nc, name) as ctx:
        sem = ctx.sem
        sb = lambda x, shape: ctx.enter_context(nc.sbuf_tensor(f"{name}_{x}", shape, F32))
        slab = [sb(f"w{b}", [P, 2, DC, P]) for b in range(2)]
        high, low = ([ctx.enter_context(nc.sbuf_tensor(f"{name}_{i}{v}", [P, DC, P], F32R)) for v in range(2)]
                     for i in ("wh", "wl"))
        work = sb("work", [P, DC, T])
        acc, prod = work[:, 0:4, :], work[:, 4:6, :]
        x = [ctx.enter_context(nc.sbuf_tensor(f"{name}_x{i}", [P, DC, T], F32R)) for i in range(2)]
        w_in = [sem(f"w_in{b}") for b in range(2)]
        rounded, split, projected, based, tap1, tap0, gated, multiplied, out_high, done = (
            sem(n) for n in ("rounded", "split", "projected", "based", "tap1", "tap0", "gated", "multiplied",
                             "out_high", "done"))
        cw, cb = PARAMS["convw"][0] + layer * 2 * FC * 3, PARAMS["convb"][0] + layer * 2 * FC

        def weight(j, v, tap):
            return c.param[:, bass.ds(cw + (j + v * FC) * 3 + tap, 1)]

        def load(sp, i):
            for b in range(2):
                emit_wait(sp, split, 4 * i - 2 + 2 * b)
                sp.dma_start(slab[b][:, :, :, :], w[bass.ds(2 * i + b, 1)].rearrange("a p x k m -> (a p) x k m"))\
                  .then_inc(w_in[b], 16)

        def round_(act, i, b, v):
            act.wait_ge(w_in[b], 16 * i + 16)
            emit_wait(act, projected, 4 * i + 2 * b + v - 1)
            nc.scalar.copy(high[v][:, :, :], slab[b][:, v, :, :]).then_inc(rounded, 1)

        def rest(pool, i, b, v):
            pool.wait_ge(rounded, 4 * i + 2 * b + v + 1)
            nc.gpsimd.tensor_tensor(low[v][:, :, :], slab[b][:, v, :, :],
                                    high[v][:, :, :].bitcast(F32), ALU.subtract).then_inc(split, 1)

        def round_first(act):
            for v in range(2):
                round_(act, 0, 0, v)

        def rest_first(pool):
            for v in range(2):
                rest(pool, 0, 0, v)

        stage_norm(c, f"{name}_norm", gain, x, work, ahead=(lambda sp: load(sp, 0), round_first, rest_first))
        with nc.Block(name) as block:
            @block.sync
            def _(sp):
                load(sp, 1)
                with sp.Fori(2, FC // 2) as i:
                    load(sp, i)

            @block.gpsimd
            def _(pool):
                for v in range(2):
                    rest(pool, 0, 1, v)
                with pool.Fori(1, FC // 2) as i:
                    for b in range(2):
                        for v in range(2):
                            rest(pool, i, b, v)

            @block.tensor
            def _(pe):
                def project(i):
                    for b in range(2):
                        for v in range(2):
                            pe.wait_ge(split, 4 * i + 2 * b + v + 1)
                            emit_wait(pe, tap0, 4 * (i - 1) + 2 * b + v + 1 if not isinstance(i, int) else 0)
                            for j in range(DC):
                                mm = c.product(c.bank(2 * b + v), (high[v][:, j, :], low[v][:, j, :]),
                                               (x[0][:, j, :], x[1][:, j, :]), j == 0, j == DC - 1)
                            mm.then_inc(projected, 1)
                repeat(pe, FC // 2, project)

            @block.scalar
            def _(act):
                def first_tap(i, last):
                    for b in range(2):
                        for v in range(2):
                            act.wait_ge(projected, 4 * i + 2 * b + v + 1)
                            emit_wait(act, multiplied, 2 * i - 1 + b if not isinstance(i, int) else 0)
                            if b == 0:
                                round_(act, i, 1, v)
                            elif not last:
                                round_(act, i + 1, 0, v)
                            nc.scalar.activation(
                                acc[:, 2 * b + v, :], c.bank(2 * b + v), ACT.Identity,
                                bias=c.param[:, bass.ds(cb + 2 * i + b + v * FC, 1)],
                                scale=weight(2 * i + b, v, 2)).then_inc(based, 1)
                            if v == 0:
                                act.wait_ge(tap0, 4 * i + 2 * b + 1)
                                nc.scalar.activation(acc[:, 2 * b, :], acc[:, 2 * b, :], ACT.Silu).then_inc(gated, 1)
                        act.wait_ge(multiplied, 2 * i + b + 1)
                        nc.scalar.copy(out[0][:, bass.ds(2 * i + b, 1), :].rearrange("p a t -> p (a t)"),
                                       prod[:, b, :]).then_inc(out_high, 1)

                first_tap(0, False)
                with act.Fori(1, FC // 2 - 1) as i:
                    first_tap(i, False)
                first_tap(FC // 2 - 1, True)

            @block.vector
            def _(dve):
                def convolve(i):
                    for b in range(2):
                        for v in range(2):
                            n = 4 * i + 2 * b + v + 1
                            y = acc[:, 2 * b + v, :]
                            raw = c.bank(2 * b + v)
                            dve.wait_ge(based, n)
                            nc.vector.scalar_tensor_tensor(
                                out=y[:, 1:T], in0=raw[:, 0:T - 1], scalar=weight(2 * i + b, v, 1), in1=y[:, 1:T],
                                op0=ALU.mult, op1=ALU.add).then_inc(tap1, 1)
                            dve.wait_ge(tap1, n)
                            nc.vector.scalar_tensor_tensor(
                                out=y[:, 2:T], in0=raw[:, 0:T - 2], scalar=weight(2 * i + b, v, 0), in1=y[:, 2:T],
                                op0=ALU.mult, op1=ALU.add).then_inc(tap0, 1)
                        dve.wait_ge(gated, 2 * i + b + 1)
                        dve.wait_ge(tap0, 4 * i + 2 * b + 2)
                        emit_wait(dve, done, 2 * i - 1 + b if not isinstance(i, int) else 0)
                        nc.vector.tensor_tensor(prod[:, b, :], acc[:, 2 * b, :], acc[:, 2 * b + 1, :], ALU.mult)\
                          .then_inc(multiplied, 1)
                        dve.wait_ge(out_high, 2 * i + b + 1)
                        at = bass.ds(2 * i + b, 1)
                        nc.vector.tensor_tensor(
                            out[1][:, at, :].rearrange("p a t -> p (a t)"), prod[:, b, :],
                            out[0][:, at, :].bitcast(F32).rearrange("p a t -> p (a t)"), ALU.subtract)\
                          .then_inc(done, 1)
                repeat(dve, FC // 2, convolve)


def stage_route(c):
    nc, a = c.nc, c.a
    with Stage(nc, "route") as ctx:
        sem = ctx.sem
        sb = lambda x, shape, dt=F32: ctx.enter_context(nc.sbuf_tensor(f"route_{x}", shape, dt))
        wr = sb("w", [P, DC, 20])
        rows = sb("rows", [P, TT, D])
        L = sb("L", [P, TT, 20])
        gmax, taken, fresh = sb("gmax", [P, TT]), sb("taken", [P, TT]), sb("fresh", [P, TT])
        eq = sb("eq", [P, TT, 4])
        selg = sb("selg", [P, TT, 4])
        ex, gsum, gate = sb("ex", [P, TT, 4]), sb("gsum", [P, TT]), sb("gate", [P, TT])
        le, tmp4 = sb("le", [P, TT, 4]), sb("tmp4", [P, TT, 4])
        s12 = sb("s12", [P, 2, TT, 4])
        val = sb("val", [P, 2, TT])
        wt = sb("wt", [P, 2, TT])
        M = sb("M", [P, 2, TT, N_EXP])
        Ms = sb("Ms", [P, TT, N_EXP])
        cnt, tiles, incl, excl = (sb(x, [P, N_EXP]) for x in ("cnt", "tiles", "incl", "excl"))
        pos = sb("pos", [P, TT, N_EXP])
        tm = sb("tm", [P, 2, TT, N_EXP])
        dst = sb("dst", [P, 2, TT])
        dsti = sb("dsti", [P, 2, TT], U32)
        rec = sb("rec", [P, 2, TT, 4], I32)
        cmp = sb("cmp", [1, 24, N_EXP])
        tl = sb("tl", [1, 25])
        w_in, rec_in, turned, copied, logits, step, expd, exp_in, counted, placed, stored, back = (
            sem(x) for x in ("w_in", "rec_in", "turned", "copied", "logits", "step", "expd", "exp_in", "counted",
                             "placed", "stored", "back"))
        listed = ctx.dma_sem("listed")
        fwd_tiles = sem("fwd_tiles")
        with nc.Block("route") as block:
            @block.sync
            def _(sp):
                sp.dma_start(wr[:, :, :], a["w_route"]).then_inc(w_in, 16)
                sp.dma_start(rec[:, :, :, :], a["rec"]).then_inc(rec_in, 16)
                for tt in range(TT):
                    sp.wait_ge(copied, 2 * tt + 2)
                    sp.dma_start(a["hrows"][tt * P:(tt + 1) * P, :], rows[:, tt, :]).then_inc(stored, 16)
                sp.wait_ge(listed, 16 * 8)
                sp.dma_start(c.slots[:, :, :], a["plist"].rearrange("(t p) x -> p t x", p=P)).then_inc(back, 16)
                sp.wait_ge(back, 16)
                sp.wait_ge(stored, 16 * TT)

            @block.tensor
            def _(pe):
                pe.wait_ge(w_in, 16)
                for tt in range(TT):
                    for i in range(DC):
                        mm = nc.tensor.matmul(c.ps[:, 4, 20 * tt:20 * tt + 20], c.xn[:, i, P * tt:P * tt + P],
                                              wr[:, i, :], start=(i == 0), stop=(i == DC - 1))
                mm.then_inc(logits, 1)
                for tt in range(TT):
                    for half in range(2):
                        n = 2 * tt + half
                        if n >= 4:
                            pe.wait_ge(copied, n - 3)
                        for i in range(4):
                            mm = nc.tensor.transpose(c.ps[:, n % 4, P * i:P * i + P],
                                                     c.xn[:, 4 * half + i, P * tt:P * tt + P], c.k("ident"))
                        mm.then_inc(turned, 1)
                pe.wait_ge(counted, 1)
                for tt in range(TT):
                    for j in range(tt + 1):
                        nc.tensor.matmul(c.ps[:, 5, N_EXP * tt:N_EXP * tt + N_EXP],
                                         c.k("tri") if j == tt else c.k("ones"), Ms[:, j, :],
                                         start=(j == 0), stop=(j == tt))
                for j in range(TT):
                    mm = nc.tensor.matmul(c.ps[:, 5, 64:64 + N_EXP], c.k("ones"), Ms[:, j, :],
                                          start=(j == 0), stop=(j == TT - 1))
                mm.then_inc(placed, 1)

            @block.scalar
            def _(act):
                for tt in range(TT):
                    for half in range(2):
                        n = 2 * tt + half
                        act.wait_ge(turned, n + 1)
                        nc.scalar.copy(rows[:, tt, 512 * half:512 * half + 512], c.bank(n % 4)).then_inc(copied, 1)
                for i, t in enumerate((ex, le)):
                    act.wait_ge(exp_in, i + 1)
                    nc.scalar.activation(t[:, :, :], t[:, :, :], ACT.Exp).then_inc(expd, 1)

            @block.vector
            def _(dve):
                n = [0]

                def then(ins):
                    n[0] += 1
                    ins.then_inc(step, 1)
                    dve.wait_ge(step, n[0])

                tt_ = nc.vector.tensor_tensor

                def first_equal(out, x, top):
                    then(nc.vector.tensor_tensor(eq[:, :, :], x, top.unsqueeze(2).broadcast_to([P, TT, 4]), ALU.is_equal))
                    then(nc.vector.memset(taken[:, :], 0.0))
                    for j in range(4):
                        then(nc.vector.tensor_scalar(fresh[:, :], taken[:, :], -1.0, 1.0, ALU.mult, ALU.add))
                        then(tt_(out[:, :, j], eq[:, :, j], fresh[:, :], ALU.mult))
                        if j < 3:
                            then(tt_(taken[:, :], taken[:, :], out[:, :, j], ALU.add))

                def wide(x):
                    return x.unsqueeze(2).broadcast_to([P, TT, 4])

                dve.wait_ge(logits, 1)
                then(tt_(L[:, :, :], c.ps[:, 4, 0:80].rearrange("p (t e) -> p t e", t=TT),
                         c.p("rb").unsqueeze(1).broadcast_to([P, TT, 20]), ALU.add))
                then(nc.vector.tensor_reduce(gmax[:, :], L[:, :, 0:4], AX_X, ALU.max))
                first_equal(selg, L[:, :, 0:4], gmax[:, :])
                n[0] += 0
                tt_(ex[:, :, :], L[:, :, 0:4], wide(gmax[:, :]), ALU.subtract).then_inc(exp_in, 1)
                dve.wait_ge(expd, 1)
                then(nc.vector.tensor_reduce(gsum[:, :], ex[:, :, :], AX_X, ALU.add))
                then(nc.vector.reciprocal(gate[:, :], gsum[:, :]))
                then(tt_(le[:, :, :], L[:, :, 4:8], wide(selg[:, :, 0]), ALU.mult))
                for g in range(1, 4):
                    then(tt_(tmp4[:, :, :], L[:, :, 4 + 4 * g:8 + 4 * g], wide(selg[:, :, g]), ALU.mult))
                    then(tt_(le[:, :, :], le[:, :, :], tmp4[:, :, :], ALU.add))
                then(nc.vector.tensor_reduce(gmax[:, :], le[:, :, :], AX_X, ALU.max))
                tt_(le[:, :, :], le[:, :, :], wide(gmax[:, :]), ALU.subtract).then_inc(exp_in, 1)
                dve.wait_ge(expd, 2)
                then(nc.vector.tensor_reduce(gsum[:, :], le[:, :, :], AX_X, ALU.add))
                then(nc.vector.reciprocal(gsum[:, :], gsum[:, :]))
                then(tt_(le[:, :, :], le[:, :, :], wide(gsum[:, :]), ALU.mult))
                then(nc.vector.tensor_reduce(val[:, 0, :], le[:, :, :], AX_X, ALU.max))
                first_equal(s12[:, 0], le[:, :, :], val[:, 0, :])
                then(nc.vector.scalar_tensor_tensor(out=le[:, :, :], in0=s12[:, 0], scalar=-2.0, in1=le[:, :, :],
                                                    op0=ALU.mult, op1=ALU.add))
                then(nc.vector.tensor_reduce(val[:, 1, :], le[:, :, :], AX_X, ALU.max))
                first_equal(s12[:, 1], le[:, :, :], val[:, 1, :])
                then(tt_(gsum[:, :], val[:, 0, :], val[:, 1, :], ALU.add))
                then(nc.vector.reciprocal(gsum[:, :], gsum[:, :]))
                then(tt_(gsum[:, :], gsum[:, :], gate[:, :], ALU.mult))
                for k in range(2):
                    then(tt_(wt[:, k, :], val[:, k, :], gsum[:, :], ALU.mult))
                for k in range(2):
                    for g in range(4):
                        then(tt_(M[:, k, :, 4 * g:4 * g + 4], s12[:, k], wide(selg[:, :, g]), ALU.mult))
                tt_(Ms[:, :, :], M[:, 0], M[:, 1], ALU.add).then_inc(counted, 1)
                dve.wait_ge(placed, 1)
                then(nc.vector.tensor_copy(cnt[:, :], c.ps[:, 5, 64:64 + N_EXP]))
                then(nc.vector.tensor_scalar(tiles[:, :], cnt[:, :], 0.0, None, ALU.is_gt))
                for k in range(1, 4):
                    then(nc.vector.scalar_tensor_tensor(out=tiles[:, :], in0=cnt[:, :], scalar=float(P * k),
                                                        in1=tiles[:, :], op0=ALU.is_gt, op1=ALU.add))
                then(nc.vector.tensor_tensor_scan(incl[:, :], c.k("ones")[:, 0:N_EXP], tiles[:, :], 0.0,
                                                  ALU.mult, ALU.add))
                then(tt_(excl[:, :], incl[:, :], tiles[:, :], ALU.subtract))
                then(nc.vector.tensor_scalar(excl[:, :], excl[:, :], float(P), None, ALU.mult))
                then(tt_(pos[:, :, :], c.ps[:, 5, 0:64].rearrange("p (t e) -> p t e", t=TT),
                         excl[:, :].unsqueeze(1).broadcast_to([P, TT, N_EXP]), ALU.add))
                for k in range(2):
                    then(tt_(tm[:, k], M[:, k], pos[:, :, :], ALU.mult))
                    then(nc.vector.tensor_reduce(dst[:, k, :], tm[:, k], AX_X, ALU.add))
                then(nc.vector.tensor_copy(dsti[:, :, :], dst[:, :, :]))
                dve.wait_ge(rec_in, 16)
                then(nc.vector.tensor_copy(rec[:, :, :, 2].bitcast(F32), wt[:, :, :]))
                then(tt_(cmp[:, :, :], incl[0:1, :].unsqueeze(1).broadcast_to([1, 24, N_EXP]),
                         c.k("tileid")[0:1, :].rearrange("p (i e) -> p i e", i=24), ALU.is_le))
                then(nc.vector.tensor_reduce(tl[:, 0:24], cmp[:, :, :], AX_X, ALU.add))
                then(nc.vector.tensor_copy(tl[:, 23:24], incl[0:1, 15:16]))
                then(nc.vector.tensor_scalar(tl[:, 24:25], incl[0:1, 15:16], 1.0, None, ALU.subtract))
                nc.vector.tensor_copy(c.tiles[:, :], tl[:, :]).then_inc(fwd_tiles, 1)

            @block.gpsimd
            def _(pool):
                pool.wait_ge(fwd_tiles, 1)
                pool.wait_ge(c.list_empty, 16)
                for k in range(2):
                    for tt in range(TT):
                        nc.gpsimd.indirect_dma_start(
                            out=a["plist"], out_offset=bass.IndirectOffsetOnAxis(ap=dsti[:, k, tt:tt + 1], axis=0),
                            in_=rec[:, k, tt, :], in_offset=None).then_inc(listed, 16)


def stage_experts(c):
    nc, a = c.nc, c.a
    with Stage(nc, "moe") as ctx:
        sem = ctx.sem
        sb = lambda x, shape, dt=F32: ctx.enter_context(nc.sbuf_tensor(f"moe_{x}", shape, dt))
        wg, wu, wd = sb("wg", [P, DC, D_EXP]), sb("wu", [P, DC, D_EXP]), sb("wd", [P, D_EXP // P, D])
        xg, xgT = sb("xg", [P, D]), sb("xgT", [P, DC, P])
        hh, hT, y = sb("hh", [P, D_EXP]), sb("hT", [P, 4, P]), sb("y", [P, D])
        gi, si = sb("gi", [P, 4], I32), sb("si", [P, 4], I32)
        (g_in, u_in, d_in, zeroed, idx, turned, xcopied, gated, upped, silued, hready, hturned, hcopied,
         downed, ycopied, sidx) = (
            sem(x) for x in ("g_in", "u_in", "d_in", "zeroed", "idx", "turned", "xcopied", "gated",
                             "upped", "silued", "hready", "hturned", "hcopied", "downed", "ycopied", "sidx"))
        passed_pool = sem("passed_pool")
        gathered, scattered = ctx.dma_sem("gathered"), ctx.dma_sem("scattered")

        def count(eng):
            return eng.value_load(c.tiles[0:1, 23:24], min_val=PAIRS // P, max_val=MAX_TILES)

        def last(eng):
            return eng.value_load(c.tiles[0:1, 24:25], min_val=PAIRS // P - 1, max_val=MAX_TILES - 1)

        with nc.Block("experts") as block:
            @block.sync
            def _(sp):
                def load(i, free, landed, dst, src):
                    e = sp.value_load(c.tiles[0:1, bass.ds(i, 1)], min_val=0, max_val=N_EXP - 1)
                    emit_wait(sp, free, i)
                    sp.dma_start(dst[:, :, :], src[bass.ds(e, 1)].rearrange("a p k m -> (a p) k m"))\
                      .then_inc(landed, 16)

                def body(i):
                    load(i, gated, g_in, wg, a["w_gate"])
                    load(i, upped, u_in, wu, a["w_up"])
                    if not isinstance(i, int) or i:
                        load(i - 1, downed, d_in, wd, a["w_down"])

                repeat(sp, count(sp), body, peel=2)
                load(last(sp), downed, d_in, wd, a["w_down"])

            @block.gpsimd
            def _(pool):
                nc.gpsimd.memset(xg[:, :], 0.0).then_inc(zeroed, 1)
                pool.wait_ge(zeroed, 1)

                def gather(i):
                    emit_wait(pool, turned, 2 * i)
                    emit_wait(pool, gathered, 16 * i)
                    src = c.slots[:, bass.ds(i, 1), 0:2].rearrange("p a x -> p (a x)")
                    nc.gpsimd.tensor_copy(gi[:, 0:2], src).then_inc(idx, 1)
                    wait_apart(pool, idx, i + 1, passed_pool)
                    nc.gpsimd.indirect_dma_start(
                        out=xg[:, :], out_offset=None, in_=a["hrows"],
                        in_offset=bass.IndirectOffsetOnAxis(ap=gi[:, 0:1].bitcast(U32), axis=0),
                        bounds_check=T - 1, oob_is_err=False).then_inc(gathered, 16)

                def scatter(i):
                    pool.wait_ge(ycopied, 2 * i + 2)
                    src = c.slots[:, bass.ds(i, 1), 0:2].rearrange("p a x -> p (a x)")
                    nc.gpsimd.tensor_copy(si[:, 0:2], src).then_inc(sidx, 1)
                    wait_apart(pool, sidx, i + 1, passed_pool)
                    nc.gpsimd.indirect_dma_start(
                        out=a["yrows"], out_offset=bass.IndirectOffsetOnAxis(ap=si[:, 1:2].bitcast(U32), axis=0),
                        in_=y[:, :], in_offset=None, bounds_check=PAIRS - 1, oob_is_err=False)\
                      .then_inc(scattered, 16)
                    wait_apart(pool, scattered, 16 * i + 16, passed_pool)

                def body(i):
                    gather(i + 1)
                    if not isinstance(i, int) or i:
                        scatter(i - 1)

                gather(0)
                n = count(pool)
                repeat(pool, n, body)
                scatter(last(pool))
                pool.wait_ge(gathered, 16 * n + 16)

            @block.tensor
            def _(pe):
                def turn_x(i):
                    pe.wait_ge(gathered, 16 * i + 16)
                    for half in range(2):
                        emit_wait(pe, xcopied, 2 * i)
                        for j in range(4):
                            mm = nc.tensor.transpose(c.ps[:, half, P * j:P * j + P],
                                                     xg[:, 512 * half + P * j:512 * half + P * j + P], c.k("ident"))
                        mm.then_inc(turned, 1)

                def down(i):
                    pe.wait_ge(hcopied, i + 1)
                    pe.wait_ge(d_in, 16 * i + 16)
                    for half in range(2):
                        emit_wait(pe, ycopied, 2 * i)
                        for j in range(4):
                            mm = nc.tensor.matmul(c.bank(5 + half), hT[:, j, :], wd[:, j, 512 * half:512 * half + 512],
                                                  start=(j == 0), stop=(j == 3))
                    mm.then_inc(downed, 1)

                def body(i):
                    pe.wait_ge(xcopied, 2 * i + 2)
                    for bank_i, slab, landed, done in ((2, wg, g_in, gated), (3, wu, u_in, upped)):
                        pe.wait_ge(landed, 16 * i + 16)
                        emit_wait(pe, hready, i)
                        for j in range(DC):
                            mm = nc.tensor.matmul(c.bank(bank_i), xgT[:, j, :], slab[:, j, :],
                                                  start=(j == 0), stop=(j == DC - 1))
                        mm.then_inc(done, 1)
                    turn_x(i + 1)
                    if not isinstance(i, int) or i:
                        down(i - 1)
                    pe.wait_ge(hready, i + 1)
                    emit_wait(pe, hcopied, i)
                    for j in range(4):
                        mm = nc.tensor.transpose(c.ps[:, 4, P * j:P * j + P], hh[:, P * j:P * j + P], c.k("ident"))
                    mm.then_inc(hturned, 1)

                turn_x(0)
                repeat(pe, count(pe), body, peel=2)
                down(last(pe))

            @block.scalar
            def _(act):
                def copy_x(i):
                    for half in range(2):
                        act.wait_ge(turned, 2 * i + half + 1)
                        emit_wait(act, upped, i)
                        nc.scalar.copy(xgT[:, 4 * half:4 * half + 4, :].rearrange("p a t -> p (a t)"), c.bank(half))\
                          .then_inc(xcopied, 1)

                def copy_y(i):
                    act.wait_ge(downed, i + 1)
                    emit_wait(act, scattered, 16 * i)
                    for half in range(2):
                        nc.scalar.copy(y[:, 512 * half:512 * half + 512], c.bank(5 + half)).then_inc(ycopied, 1)

                def body(i):
                    act.wait_ge(gated, i + 1)
                    emit_wait(act, hturned, i)
                    nc.scalar.activation(hh[:, :], c.bank(2), ACT.Silu).then_inc(silued, 1)
                    copy_x(i + 1)
                    if not isinstance(i, int) or i:
                        copy_y(i - 1)

                copy_x(0)
                repeat(act, count(act), body, peel=2)
                copy_y(last(act))

            @block.vector
            def _(dve):
                def body(i):
                    dve.wait_ge(silued, i + 1)
                    dve.wait_ge(upped, i + 1)
                    wcol = c.slots[:, bass.ds(i, 1), 2:3].bitcast(F32).rearrange("p a x -> p (a x)")
                    nc.vector.scalar_tensor_tensor(out=hh[:, :], in0=hh[:, :], scalar=wcol, in1=c.bank(3),
                                                   op0=ALU.mult, op1=ALU.mult).then_inc(hready, 1)
                    dve.wait_ge(hturned, i + 1)
                    emit_wait(dve, downed, i)
                    nc.vector.tensor_copy(hT[:, :, :].rearrange("p a t -> p (a t)"), c.bank(4)).then_inc(hcopied, 1)
                repeat(dve, count(dve), body, peel=2)


def stage_combine(c):
    nc, a = c.nc, c.a
    with Stage(nc, "comb") as ctx:
        sem = ctx.sem
        y = ctx.enter_context(nc.sbuf_tensor("comb_y", [P, 2, TT, D], F32))
        y_in = [sem(f"y_in{t}") for t in range(TT)]
        summed, turned, added = sem("summed"), sem("turned"), sem("added")
        with nc.Block("combine") as block:
            @block.sync
            def _(sp):
                rows = a["yrows"].rearrange("(k t p) d -> t p k d", k=2, p=P)
                for tt in range(TT):
                    sp.dma_start(y[:, :, tt, :], rows[tt]).then_inc(y_in[tt], 16)

            @block.vector
            def _(dve):
                for tt in range(TT):
                    dve.wait_ge(y_in[tt], 16)
                    nc.vector.tensor_tensor(y[:, 0, tt, :], y[:, 0, tt, :], y[:, 1, tt, :], ALU.add)\
                      .then_inc(summed, 1)
                for i in range(DC):
                    dve.wait_ge(turned, i + 1)
                    nc.vector.tensor_tensor(c.h[:, i, :], c.bank(i), c.h[:, i, :], ALU.add).then_inc(added, 1)

            @block.tensor
            def _(pe):
                for i in range(DC):
                    for tt in range(TT):
                        pe.wait_ge(summed, tt + 1)
                        mm = nc.tensor.transpose(c.ps[:, i, P * tt:P * tt + P], y[:, 0, tt, P * i:P * i + P],
                                                 c.k("ident"))
                    mm.then_inc(turned, 1)


def stage_select(c):
    nc, a = c.nc, c.a
    with Stage(nc, "sel") as ctx:
        sem = ctx.sem
        sb = lambda x, shape: ctx.enter_context(nc.sbuf_tensor(f"sel_{x}", shape, F32))
        w = sb("w", [P, 3, DC, P])
        ww = sb("ww", [P, DC, 4])
        raw, tmp, tmp2 = sb("raw", [P, 3, T]), sb("tmp", [P, 3, T]), sb("tmp2", [P, T])
        fin = sb("fin", [P, 3, T])
        wi = sb("wi", [P, TT, 4])
        rel = sb("rel", [P, 2, 4, T])
        w_in, projected, weighed, evac, meaned, step, sq, varred, rooted, rotated, ready, scored, reluded, accd = (
            sem(x) for x in ("w_in", "projected", "weighed", "evac", "meaned", "step", "sq", "varred", "rooted",
                             "rotated", "ready", "scored", "reluded", "accd"))
        kready = sem("kready")
        with nc.Block("select") as block:
            @block.sync
            def _(sp):
                sp.dma_start(w[:, :, :, :], a["w_idx"].rearrange("i p k m -> p i k m")).then_inc(w_in, 16)
                sp.dma_start(ww[:, :, :], a["w_idxw"]).then_inc(w_in, 16)

            @block.tensor
            def _(pe):
                pe.wait_ge(w_in, 32)
                for i in (2, 0, 1):
                    for j in range(DC):
                        mm = nc.tensor.matmul(c.bank(i), w[:, i, j, :], c.xn[:, j, :], start=(j == 0),
                                              stop=(j == DC - 1))
                    mm.then_inc(projected, 1)
                for tt in range(TT):
                    for j in range(DC):
                        mm = nc.tensor.matmul(c.ps[:, 3, 4 * tt:4 * tt + 4], c.xn[:, j, P * tt:P * tt + P],
                                              ww[:, j, :], start=(j == 0), stop=(j == DC - 1))
                mm.then_inc(weighed, 1)
                pe.wait_ge(evac, 1)
                nc.tensor.matmul(c.bank(4), c.k("blk64"), raw[:, 2, :], start=True, stop=True).then_inc(meaned, 1)
                pe.wait_ge(sq, 1)
                nc.tensor.matmul(c.bank(5), c.k("blk64"), tmp[:, 2, :], start=True, stop=True).then_inc(varred, 1)
                for i in (0, 1):
                    pe.wait_ge(evac, 2 + i)
                    nc.tensor.matmul(c.bank(i), c.k("rot"), raw[:, i, :], start=True, stop=True).then_inc(rotated, 1)
                pe.wait_ge(kready, 1)
                nc.tensor.matmul(c.bank(2), c.k("rot"), raw[:, 2, :], start=True, stop=True).then_inc(rotated, 1)
                pe.wait_ge(ready, 3)
                for t, qt in enumerate((1, 2, 3)):
                    for h in range(4):
                        hd = slice(HD * (h % 2), HD * (h % 2) + HD)
                        if t:
                            pe.wait_ge(reluded, 4 * (t - 1) + h + 1)
                        nc.tensor.matmul(c.ps[:, 4 + h, 0:P * (qt + 1)], fin[hd, h // 2, P * qt:P * qt + P],
                                         fin[hd, 2, 0:P * (qt + 1)], start=True, stop=True).then_inc(scored, 1)

            @block.scalar
            def _(act):
                for n, i in enumerate((2, 0, 1)):
                    act.wait_ge(projected, n + 1)
                    nc.scalar.copy(raw[:, i, :], c.bank(i)).then_inc(evac, 1)
                act.wait_ge(step, 1)
                nc.scalar.activation(tmp[:, 2, :], raw[:, 2, :], ACT.Square).then_inc(sq, 1)
                act.wait_ge(varred, 1)
                nc.scalar.activation(tmp[:, 2, :], c.bank(5), ACT.Sqrt, bias=c.eps[:, 0:1]).then_inc(rooted, 1)
                for t, qt in enumerate((1, 2, 3)):
                    for h in range(4):
                        act.wait_ge(scored, 4 * t + h + 1)
                        if t == 2:
                            act.wait_ge(accd, 4)
                        nc.scalar.activation(rel[:, t % 2, h, 0:P * (qt + 1)], c.ps[:, 4 + h, 0:P * (qt + 1)],
                                             ACT.Relu).then_inc(reluded, 1)

            @block.vector
            def _(dve):
                n = [0]

                def then(ins):
                    n[0] += 1
                    ins.then_inc(step, 1)
                    dve.wait_ge(step, n[0])

                dve.wait_ge(meaned, 1)
                then(nc.vector.tensor_tensor(raw[:, 2, :], raw[:, 2, :], c.bank(4), ALU.subtract))
                dve.wait_ge(rooted, 1)
                then(nc.vector.reciprocal(tmp2[:, :], tmp[:, 2, :]))
                then(nc.vector.tensor_tensor(raw[:, 2, :], raw[:, 2, :], tmp2[:, :], ALU.mult))
                nc.vector.tensor_scalar(raw[:, 2, :], raw[:, 2, :], c.p("lng"), c.p("lnb"), ALU.mult, ALU.add)\
                  .then_inc(kready, 1)
                dve.wait_ge(kready, 1)
                for m, i in enumerate((0, 1, 2)):
                    dve.wait_ge(evac, 3)
                    then(nc.vector.tensor_tensor(tmp[:, i, :], raw[:, i, :], c.k("cos"), ALU.mult))
                    dve.wait_ge(rotated, m + 1)
                    then(nc.vector.tensor_tensor(tmp2[:, :], c.bank(i), c.k("sin"), ALU.mult))
                    nc.vector.tensor_tensor(fin[:, i, :], tmp[:, i, :], tmp2[:, :], ALU.add).then_inc(ready, 1)
                    dve.wait_ge(ready, m + 1)
                dve.wait_ge(weighed, 1)
                then(nc.vector.tensor_copy(wi[:, :, :].rearrange("p a e -> p (a e)"), c.ps[:, 3, 0:4 * TT]))
                nc.vector.tensor_copy(c.selb[:, 0:P], c.k("cmask"))
                for t, qt in enumerate((1, 2, 3)):
                    nk = P * (qt + 1)
                    x = c.selb[:, OFF[qt]:OFF[qt] + nk]
                    for h in range(4):
                        dve.wait_ge(reluded, 4 * t + h + 1)
                        r = rel[:, t % 2, h, 0:nk]
                        if h == 0:
                            then(nc.vector.tensor_scalar(x, r, wi[:, qt, 0:1], None, ALU.mult))
                        else:
                            then(nc.vector.scalar_tensor_tensor(out=x, in0=r, scalar=wi[:, qt, h:h + 1], in1=x,
                                                                op0=ALU.mult, op1=ALU.add))
                    then(nc.vector.tensor_tensor(x[:, nk - P:nk], x[:, nk - P:nk], c.k("cmask"), ALU.add))
                    nc.vector.memset(c.m8[:, :], 0.0).then_inc(accd, 4)


def top_keys(c, stage, rounds):
    nc = c.nc
    taken = stage.sem("taken")
    tiles = [c.selb[:, OFF[qt]:OFF[qt] + P * (qt + 1)] for qt in (1, 2, 3)]
    share = TOPK // 8 // rounds
    steps = 2 * share * len(tiles)

    def aside(dve, u, passed):
        n = [steps * u]

        def then(ins):
            n[0] = n[0] + 1
            ins.then_inc(taken, 1)
            wait_apart(dve, taken, n[0], passed)

        if isinstance(u, int) and u == rounds:
            return
        for x in tiles:
            for r in range(share):
                then(nc.vector.max(c.m8[:, :], x))
                then(nc.vector.match_replace(x, c.m8[:, :], x, TAKEN))
        if isinstance(u, int) and u == rounds - 1:
            for x in tiles:
                then(nc.vector.tensor_scalar(x, x, 0.5 * TAKEN, NEG, ALU.is_gt, ALU.mult))
                d = x[:, -P:]
                nc.vector.tensor_tensor(d, d, c.k("cmask"), ALU.add)

    return aside


def stage_forget_prepare(c):
    nc, a = c.nc, c.a
    with Stage(nc, "fg") as ctx:
        sem = ctx.sem
        sb = lambda x, shape: ctx.enter_context(nc.sbuf_tensor(f"fg_{x}", shape, F32))
        w = sb("w", [P, DC, 8])
        x, ab, e, one, cum = sb("x", [8, T]), sb("ab", [8, T]), sb("e", [8, T]), sb("one", [8, T]), sb("cum", [8, T])
        low = sb("low", [8, T])
        w_in, projected, biased, lg, step, spread = (
            sem(n) for n in ("w_in", "projected", "biased", "lg", "step", "spread"))
        ast = sem("ast")
        with nc.Block("forget") as block:
            @block.sync
            def _(sp):
                sp.dma_start(w[:, :, :], a["w_forget"]).then_inc(w_in, 16)
                sp.wait_ge(step, 4)
                sp.dma_start(c.fneg[0:1, :, :], cum[:, :]).then_inc(spread, 16)
                sp.wait_ge(spread, 16)

            @block.tensor
            def _(pe):
                pe.wait_ge(w_in, 16)
                for j in range(DC):
                    mm = nc.tensor.matmul(c.ps[0:8, 0, :], w[:, j, :], c.xn[:, j, :], start=(j == 0),
                                          stop=(j == DC - 1))
                mm.then_inc(projected, 1)

            @block.scalar
            def _(act):
                act.wait_ge(biased, 1)
                nc.scalar.activation(ab[:, :], x[:, :], ACT.Abs).then_inc(ast, 1)
                act.wait_ge(ast, 1)
                nc.scalar.activation(e[:, :], ab[:, :], ACT.Exp, scale=-1.0).then_inc(ast, 1)
                act.wait_ge(ast, 2)
                nc.scalar.activation(ab[:, :], e[:, :], ACT.Ln, bias=c.k("ones")[0:8, 0:1]).then_inc(lg, 1)

            @block.vector
            def _(dve):
                nc.vector.memset(one[:, :], 1.0).then_inc(step, 1)
                dve.wait_ge(projected, 1)
                fb = PARAMS["fb"][0]
                nc.vector.tensor_scalar(x[:, :], c.ps[0:8, 0, :], c.param[0:8, fb:fb + 1], None, ALU.add)\
                  .then_inc(biased, 1)
                dve.wait_ge(biased, 1)
                nc.vector.tensor_scalar(low[:, :], x[:, :], 0.0, None, ALU.min).then_inc(step, 1)
                dve.wait_ge(lg, 1)
                dve.wait_ge(step, 2)
                nc.vector.tensor_tensor(low[:, :], ab[:, :], low[:, :], ALU.subtract).then_inc(step, 1)
                dve.wait_ge(step, 3)
                nc.vector.tensor_tensor_scan(cum[:, :], one[:, :], low[:, :], 0.0, ALU.mult, ALU.add)\
                  .then_inc(step, 1)


def stage_store(c):
    nc = c.nc
    with Stage(nc, "store") as ctx:
        s = ctx.sem("out")
        with nc.Block("store") as block:
            @block.sync
            def _(sp):
                sp.dma_start(c.a["out"], c.xn[:, :, :]).then_inc(s, 16)
                sp.wait_ge(s, 16)


def build(nc, a, until=None):
    with ExitStack() as ctx:
        c = Chip(nc, ctx, a)

        def tensors(stack, *wanted):
            return [stack.enter_context(nc.sbuf_tensor(n, s, d)) for n, s, d in wanted]

        def parts(stack, name, chunks):
            return tensors(stack, (name + "_high", [P, chunks, T], F32R), (name + "_low", [P, chunks, T], F32R))

        def feed_forward(layer, gain):
            with ExitStack() as outer:
                hidden = parts(outer, f"ff{layer}", FC)
                stage_ffn_up(c, f"up{layer}", layer, a[f"w_ff_up{layer}"], gain, hidden)
                stage_back(c, f"down{layer}", a[f"w_ff_down{layer}"], hidden, FC)

        stage_load(c)
        with ExitStack() as outer:
            c.o = parts(outer, "o1", DC)
            with ExitStack() as inner:
                x = parts(inner, "x1", DC)
                (o,) = tensors(inner, ("o1_whole", [P, DC, T], F32))
                c.qgain, c.neglam = tensors(inner, ("qgain", [P, 1], F32), ("neglam", [P, 1], F32))
                wt = Weights(c, inner, "diff")
                with Stage(nc, "diff_ahead") as st:
                    stage_norm(c, "norm1", c.p("g_mix"), x, o, ahead=weights_ahead(c, st, wt, a["w_da"]))
                    stage_diff_prepare(c)
                c.o, split = (o, None), c.o
                stage_attention(c, "diff", "diff", 8, wt, a["w_da"], x, 0, bias=a["alibi"])
                c.o = split
                stage_subln(c, o, c.o)
            stage_back(c, "da_out", a["w_da_out"], c.o, DC)
        if until == 2:
            return c
        with ExitStack() as outer:
            c.slots, c.tiles = tensors(outer, ("slots", [P, 24, 4], I32), ("tiles", [1, 25], I32))
            with ExitStack() as inner:
                (c.xn,) = tensors(inner, ("x2_whole", [P, DC, T], F32))
                stage_norm(c, "norm2", c.p("g_ffn"), None, c.xn)
                stage_route(c)
            stage_experts(c)
            stage_combine(c)
        if until == 3:
            return c
        with ExitStack() as outer:
            c.o = parts(outer, "o3", DC)
            with ExitStack() as inner:
                x = parts(inner, "x3", DC)
                c.selb, c.m8 = tensors(inner, ("selb", [P, PW], F32), ("m8", [P, 8], F32))
                wt = Weights(c, inner, "even")
                with ExitStack() as whole:
                    (c.xn,) = tensors(whole, ("x3_whole", [P, DC, T], F32))
                    with Stage(nc, "even_ahead") as st:
                        stage_norm(c, "norm3", c.p("g_mix2", 0, DC), x, c.xn,
                                   ahead=weights_ahead(c, st, wt, a["w_rel"]))
                        stage_select(c)
                with Stage(nc, "topk") as st:
                    stage_attention(c, "rel", "rel", 4, wt, a["w_rel"], x, 4,
                                    bias=bass.AP(a["relrows"].tensor, P - 1, [[P * 640, 8], [639, P], [1, T]]),
                                    bias_ready=c.rel_spread, next_w=a["w_dsa"], aside=top_keys(c, st, 4))
                stage_attention(c, "dsa", "dsa", 4, wt, a["w_dsa"], x, 0,
                                bias=lambda s, qt: c.selb[:, OFF[qt]:OFF[qt] + P * (qt + 1)])
            stage_back(c, "even_out", a["w_even_out"], c.o, DC)
        feed_forward(0, c.p("g_ffn2", 0, DC))
        if until == 5:
            return c
        with ExitStack() as outer:
            c.o = parts(outer, "o5", DC)
            with ExitStack() as inner:
                x = parts(inner, "x5", DC)
                (c.fneg,) = tensors(inner, ("fneg", [1, 8, T], F32))
                wt = Weights(c, inner, "odd")
                with ExitStack() as whole:
                    (c.xn,) = tensors(whole, ("x5_whole", [P, DC, T], F32))
                    with Stage(nc, "odd_ahead") as st:
                        stage_norm(c, "norm5", c.p("g_mix2", DC, DC), x, c.xn,
                                   ahead=weights_ahead(c, st, wt, a["w_fgt"]))
                        stage_forget_prepare(c)
                stage_attention(c, "forget_att", "forget", 4, wt, a["w_fgt"], x, 0,
                                bias=lambda s, qt: c.k("cband")[:, T - P - P * qt:T], next_w=a["w_snk"])
                stage_attention(c, "sink", "sink", 4, wt, a["w_snk"], x, 4,
                                bias=lambda s, qt: c.k("sband")[:, (P if qt == 0 else 0):2 * P])
            stage_back(c, "odd_out", a["w_odd_out"], c.o, DC)
        feed_forward(1, c.p("g_ffn2", DC, DC))
        with ExitStack() as inner:
            (c.xn,) = tensors(inner, ("x7_whole", [P, DC, T], F32))
            stage_norm(c, "norm7", c.p("g_out"), None, c.xn)
            stage_store(c)
        return c


def pack(inputs):
    i = {k: np.asarray(v) for k, v in inputs.items()}

    def cols(x):
        return np.ascontiguousarray(x.reshape(-1, P).T)

    def fm(w):
        k, m = w.shape
        return np.ascontiguousarray(w.reshape(k // P, P, m // P, P).transpose(2, 1, 0, 3))

    def mv(w):
        k, m = w.shape
        return np.ascontiguousarray(w.reshape(k // P, P, m).transpose(1, 0, 2))

    def qkv(q, k, v):
        return np.ascontiguousarray(np.stack([fm(q), fm(k), fm(v)], axis=1))

    par = np.zeros((P, N_PARAM), np.float32)

    def put(name, value):
        x, y = PARAMS[name]
        par[:, x:y] = value

    put("g_mix", cols(i["norm_mix"]))
    put("g_ffn", cols(i["norm_ffn"]))
    put("g_mix2", cols(i["norm_mix_g_2"]))
    put("g_ffn2", cols(i["norm_ffn_g_2"]))
    put("g_out", cols(i["norm_out_g_2"]))
    put("qg", np.tile(i["da_q_norm"][0], 2)[:, None])
    put("kg", np.tile(i["da_k_norm"][0], 2)[:, None])
    put("subln", i["da_subln"][0][:, None])
    put("lng", np.tile(i["idx_k_ln_g_2"][0], 2)[:, None])
    put("lnb", np.tile(i["idx_k_ln_b_2"][0], 2)[:, None])
    put("convw", i["ffn_conv_w_2"].reshape(2, 3, 2 * FC, P).transpose(3, 0, 2, 1).reshape(P, -1))
    put("convb", i["ffn_conv_b_2"].reshape(2 * 2 * FC, P).T)
    put("sinks", i["sinks_2"][0][None, :])
    par[0:8, PARAMS["fb"][0]] = i["forget_b_2"][0]
    put("rb", np.concatenate([i["moe_b_group"][0], i["moe_b_router"][0]])[None, :])
    put("lam", np.concatenate([i[f"da_lambda_{x}"][0] for x in ("q1", "k1", "q2", "k2")])[None, :])

    consts, alibi, rec, empty = shape_constants()
    wd = i["da_w_in"][0]
    we, wo = i["even_w_in_2"][0], i["odd_w_in_2"][0]
    ki = we[:, 1792:1856]
    ug = i["ffn_w_up_2"]
    out = {
        "xT": np.ascontiguousarray(i["x"][0].T.reshape(DC, P, T).transpose(1, 0, 2)),
        "params": par, "consts": consts, "alibi": alibi, "rec": rec, "empty": empty,
        "relE": np.ascontiguousarray(i["rel_bias_2"][0][:, np.clip(511 - np.arange(640), -256, 256) + 256]),
        "w_da": qkv(wd[:, 0:1024], wd[:, 1024:2048], wd[:, 2048:3072]),
        "w_da_out": fm(i["da_w_out"][0]),
        "w_route": mv(np.concatenate([i["moe_w_group"][0], i["moe_w_router"][0]], axis=1)),
        "w_gate": np.ascontiguousarray(i["moe_w_gate"][0].reshape(N_EXP, DC, P, D_EXP).transpose(0, 2, 1, 3)),
        "w_up": np.ascontiguousarray(i["moe_w_up"][0].reshape(N_EXP, DC, P, D_EXP).transpose(0, 2, 1, 3)),
        "w_down": np.ascontiguousarray(i["moe_w_down"][0].reshape(N_EXP, 4, P, D).transpose(0, 2, 1, 3)),
        "w_dsa": qkv(we[:, 0:512], we[:, 512:1024], we[:, 1024:1536]),
        "w_idx": fm(np.concatenate([we[:, 1536:1792], ki, ki], axis=1)),
        "w_idxw": mv(we[:, 1856:1860]),
        "w_rel": qkv(we[:, 1860:2372], we[:, 2372:2884], we[:, 2884:3396]),
        "w_even_out": fm(i["even_w_out_2"][0]),
        "w_fgt": qkv(wo[:, 0:512], wo[:, 512:1024], wo[:, 1024:1536]),
        "w_forget": mv(wo[:, 1536:1544]),
        "w_snk": qkv(wo[:, 1544:2056],
                     *(np.concatenate([wo[:, s + HD * g:s + HD * g + HD] for g in (0, 1) for _ in range(4)], axis=1)
                       for s in (2056, 2184))),
        "w_odd_out": fm(i["odd_w_out_2"][0]),
    }
    for layer in range(2):
        f = fm(ug[layer])
        out[f"w_ff_up{layer}"] = np.ascontiguousarray(np.stack([f[:FC], f[FC:]], axis=2))
        out[f"w_ff_down{layer}"] = fm(i["ffn_w_down_2"][layer])
    return out


SCRATCH = {"plist": ((24 * P, 4), I32), "relrows": ((8, P, 640), F32), "hrows": ((T, D), F32),
           "yrows": ((PAIRS, D), F32)}


def kernel(**inputs):
    import concourse.bacc as _bacc
    from concourse.bass_utils import run_bass_kernel_spmd as _run

    nc = _bacc.Bacc("TRN2", target_bir_lowering=False, num_devices=1)
    arrays, a = {}, {}
    for name, x in pack(inputs).items():
        arrays[f"in_{name}"] = x
        a[name] = nc.dram_tensor(f"in_{name}", x.shape, mybir.dt.from_np(x.dtype), kind="ExternalInput").ap()
    for name, (shape, dt) in SCRATCH.items():
        a[name] = nc.dram_tensor(name, shape, dt, kind="Internal").ap()
    a["out"] = nc.dram_tensor("out_0", (P, DC, T), F32, kind="ExternalOutput").ap()
    build(nc, a)
    r = _run(nc, [arrays], core_ids=[0])
    got = r.results[0]["out_0"]
    return np.ascontiguousarray(got.transpose(2, 1, 0).reshape(1, T, D))
```

```python
from contextlib import ExitStack

import numpy as np

import concourse.bass as bass
from concourse import mybir

F32 = mybir.dt.float32
F32R = mybir.dt.float32r
I32 = mybir.dt.int32
U32 = mybir.dt.uint32
ALU = mybir.AluOpType
ACT = mybir.ActivationFunctionType
AX_X = mybir.AxisListType.X

P = 128
T = 512
D = 1024
DC = D // P
TT = T // P
EPS = 1e-6
NEG = -1e30
HUGE = 3e38
TAKEN = -3e38
LAMBDA_INIT = 0.2
HD = 64
QK_SCALE = HD ** -0.5
N_EXP, N_GRP, EPG, D_EXP = 16, 4, 4, 512
PAIRS = 2 * T
MAX_TILES = PAIRS // P + N_EXP - 1
FF = 2816
FC = FF // P
TOPK = min(256, T // 4)
CHUNK = 64
RING = 6

OFF = [0, 128, 384, 768]
PW = 1280

CONSTS = {}
_at = 0
for _n, _w in [("ident", P), ("blk64", P), ("inv_d", P), ("inv_p", P), ("rot", P), ("tri", P), ("ones", P),
               ("cmask", P), ("cband", T), ("sband", 2 * P), ("cos", T), ("sin", T), ("tileid", 24 * N_EXP)]:
    CONSTS[_n] = (_at, _at + _w)
    _at += _w
N_CONST = _at

PARAMS = {}
_at = 0
for _n, _w in [("g_mix", DC), ("g_ffn", DC), ("g_mix2", 2 * DC), ("g_ffn2", 2 * DC), ("g_out", DC), ("qg", 1),
               ("kg", 1), ("subln", 1), ("lng", 1), ("lnb", 1), ("convw", 2 * 2 * FC * 3), ("convb", 2 * 2 * FC),
               ("sinks", 8), ("fb", 1), ("rb", 20), ("lam", 4 * HD)]:
    PARAMS[_n] = (_at, _at + _w)
    _at += _w
N_PARAM = _at


def shape_constants():
    c = np.zeros((P, N_CONST), np.float32)

    def put(name, value):
        a, b = CONSTS[name]
        c[:, a:b] = value

    p = np.arange(P)
    put("ident", np.eye(P))
    put("blk64", (p[:, None] // HD == p[None, :] // HD) / HD)
    put("inv_d", 1.0 / D)
    put("inv_p", 1.0 / P)
    rot = np.zeros((P, P))
    for m in range(P):
        if m % HD < HD // 2:
            rot[m + HD // 2, m] = -1.0
        else:
            rot[m - HD // 2, m] = 1.0
    put("rot", rot)
    put("tri", p[:, None] < p[None, :])
    put("ones", 1.0)
    later = np.where(p[None, :] // CHUNK <= p[:, None] // CHUNK, 0.0, NEG)
    put("cmask", later)
    band = np.arange(T)[None, :] - (T - P)
    dist = p[:, None] - band
    put("cband", np.where(dist >= 0, 0.0, NEG))
    window = np.arange(2 * P)[None, :] - P
    gap = p[:, None] // CHUNK - window // CHUNK
    put("sband", np.where((gap >= 0) & (gap <= 2), 0.0, NEG))
    inv = (1.0 / (np.float32(10000.0) ** (np.arange(0, HD, 2, dtype=np.float32) / np.float32(HD)))).astype(np.float32)
    ang = (np.arange(T, dtype=np.float32)[:, None] * inv[None, :]).astype(np.float32)
    put("cos", np.cos(ang).T[p % (HD // 2)])
    put("sin", np.sin(ang).T[p % (HD // 2)])
    put("tileid", np.repeat(np.arange(24), N_EXP)[None, :])
    slopes = (2.0 ** (-8.0 * np.arange(1, 9) / 8)).astype(np.float32)
    alibi = np.where(dist >= 0, -slopes[:, None, None] * dist.astype(np.float32), np.float32(NEG)).astype(np.float32)
    rec = np.zeros((P, 2, TT, 4), np.int32)
    tok = np.arange(TT)[None, :] * P + p[:, None]
    for k in range(2):
        rec[:, k, :, 0] = tok
        rec[:, k, :, 1] = k * T + tok
    empty = np.zeros((24 * P, 4), np.int32)
    empty[:, 0] = T
    empty[:, 1] = PAIRS
    return c, alibi, rec, empty


def emit_wait(eng, sem, value):
    if isinstance(value, int) and value <= 0:
        return
    eng.wait_ge(sem, value)


def wait_apart(eng, sem, value, passed):
    emit_wait(eng, sem, value)
    eng.sem_inc(passed, 1)


def repeat(eng, n, body, peel=1):
    for i in range(peel):
        body(i)
    with eng.Fori(peel, n) as i:
        body(i)


class Stage(ExitStack):

    def __init__(self, nc, name):
        super().__init__()
        self.nc, self.name, self.sems = nc, name, []

    def sem(self, name):
        s = self.nc.alloc_semaphore(f"{self.name}_{name}")
        self.sems.append(s)
        return s

    def dma_sem(self, name):
        return self.nc.alloc_semaphore(f"{self.name}_{name}")

    def __exit__(self, *exc):
        if exc[0] is None:
            for s in self.sems:
                self.nc.gpsimd.sem_clear(s)
                self.nc.release_semaphore(s)
        return super().__exit__(*exc)


class Chip:

    def __init__(self, nc, ctx, a):
        self.nc, self.ctx, self.a = nc, ctx, a

        def sb(name, shape, dt=F32):
            return ctx.enter_context(nc.sbuf_tensor(name, shape, dt))

        self.ps = ctx.enter_context(nc.psum_tensor("ps", [P, 8, 512], F32))
        self.const = sb("const", [P, N_CONST])
        self.param = sb("param", [P, N_PARAM])
        self.h = sb("h", [P, DC, T])
        self.eps = sb("eps", [P, 1])
        self.list_empty = nc.alloc_semaphore("list_empty")
        self.rel_spread = nc.alloc_semaphore("rel_spread")

    def product(self, out, w, x, start, stop):
        (wh, wl), (xh, xl) = w, x
        mm = self.nc.tensor.matmul
        mm(out, wh, xh, start=start, stop=False)
        mm(out, wh, xl, start=False, stop=False)
        return mm(out, wl, xh, start=False, stop=stop)

    def k(self, name):
        x, y = CONSTS[name]
        return self.const[:, x:y]

    def p(self, name, i=0, n=None):
        x, y = PARAMS[name]
        return self.param[:, x + i:(y if n is None else x + i + n)]

    def bank(self, i):
        return self.ps[:, i, :]


def stage_load(c):
    nc, a = c.nc, c.a
    with Stage(nc, "load") as ctx:
        s_in = ctx.sem("in")
        with nc.Block("load") as block:
            @block.sync
            def _(sp):
                sp.dma_start(c.h[:, :, :], a["xT"]).then_inc(s_in, 16)
                sp.dma_start(c.const[:, :], a["consts"]).then_inc(s_in, 16)
                sp.dma_start(c.param[:, :], a["params"]).then_inc(s_in, 16)
                sp.wait_ge(s_in, 48)

            @block.vector
            def _(dve):
                nc.vector.memset(c.eps[:, :], EPS)


class Scaling:

    def __init__(self, c, stage, name, gain, x, whole):
        self.c, self.gain, self.x, self.whole = c, gain, x, whole
        self.rs = stage.enter_context(c.nc.sbuf_tensor(f"{name}_rs", [P, T], F32))
        self.scaled, self.rounded, self.even, self.odd = (
            stage.sem(n) for n in ("x_scaled", "x_rounded", "x_even", "x_odd"))

    def vector(self, dve):
        c, nc = self.c, self.c.nc
        for i in range(DC):
            nc.vector.scalar_tensor_tensor(out=self.whole[:, i, :], in0=c.h[:, i, :], scalar=self.gain[:, i:i + 1],
                                           in1=self.rs[:, :], op0=ALU.mult, op1=ALU.mult).then_inc(self.scaled, 1)
            if self.x and i % 2:
                dve.wait_ge(self.rounded, i)
                nc.vector.tensor_tensor(self.x[1][:, i - 1, :], self.whole[:, i - 1, :],
                                        self.x[0][:, i - 1, :].bitcast(F32), ALU.subtract).then_inc(self.even, 1)

    def scalar(self, act):
        for i in range(DC if self.x else 0):
            act.wait_ge(self.scaled, i + 1)
            self.c.nc.scalar.copy(self.x[0][:, i, :], self.whole[:, i, :]).then_inc(self.rounded, 1)

    def gpsimd(self, pool):
        for i in range(1, DC if self.x else 0, 2):
            pool.wait_ge(self.rounded, i + 1)
            self.c.nc.gpsimd.tensor_tensor(self.x[1][:, i, :], self.whole[:, i, :],
                                           self.x[0][:, i, :].bitcast(F32), ALU.subtract).then_inc(self.odd, 1)

    def wait(self, pe, i):
        pe.wait_ge(self.odd if i % 2 else self.even, i // 2 + 1)


def stage_norm(c, name, gain, x, whole, ahead=None, scaling=None):
    nc = c.nc
    with Stage(nc, name) as ctx:
        sem = ctx.sem
        last = scaling or Scaling(c, ctx, name, gain, x, whole)
        squared, paired, summed, logged, inverted = (
            sem(n) for n in ("squared", "paired", "summed", "logged", "inverted"))
        sq = whole
        lg = sq[:, 0, :]
        with nc.Block(name) as block:
            @block.sync
            def _(sp):
                if ahead:
                    ahead[0](sp)

            @block.scalar
            def _(act):
                for i in range(DC):
                    nc.scalar.activation(sq[:, i, :], c.h[:, i, :], ACT.Square).then_inc(squared, 1)
                if ahead:
                    ahead[1](act)
                act.wait_ge(summed, 1)
                nc.scalar.activation(lg, c.bank(0), ACT.Ln, bias=c.eps[:, 0:1]).then_inc(logged, 1)
                act.wait_ge(logged, 1)
                nc.scalar.activation(last.rs[:, :], lg, ACT.Exp, scale=-0.5).then_inc(inverted, 1)
                if not scaling:
                    last.scalar(act)

            @block.tensor
            def _(pe):
                for i in range(0, DC, 2):
                    pe.wait_ge(paired, i // 2 + 1)
                    mm = nc.tensor.matmul(c.bank(0), c.k("inv_d"), sq[:, i, :], start=(i == 0), stop=(i == DC - 2))
                mm.then_inc(summed, 1)

            @block.vector
            def _(dve):
                for i in range(0, DC, 2):
                    dve.wait_ge(squared, i + 2)
                    nc.vector.tensor_tensor(sq[:, i, :], sq[:, i, :], sq[:, i + 1, :], ALU.add).then_inc(paired, 1)
                if not scaling:
                    dve.wait_ge(inverted, 1)
                    last.vector(dve)

            @block.gpsimd
            def _(pool):
                if ahead:
                    ahead[2](pool)
                if not scaling:
                    last.gpsimd(pool)


class FirstHalf:

    def __init__(self, c, stage, name, w, nk):
        self.w, self.hk = w, nk // 2
        self.slab = stage.enter_context(c.nc.sbuf_tensor(f"{name}_w0", [P, self.hk, P], F32))
        self.landed = stage.sem(f"{name}_w0")

    def load(self, sp):
        sp.dma_start(self.slab[:, :, :], self.w[0:1, :, 0:self.hk].rearrange("a p k m -> (a p) k m"))\
          .then_inc(self.landed, 16)


def stage_back(c, name, w, src, nk, half):
    nc = c.nc
    hk = nk // 2
    with Stage(nc, name) as ctx:
        sem = ctx.sem
        slab = [half.slab, ctx.enter_context(nc.sbuf_tensor(f"{name}_w1", [P, hk, P], F32))]
        high = [ctx.enter_context(nc.sbuf_tensor(f"{name}_wh{i}", [P, hk, P], F32R)) for i in range(2)]
        low = [ctx.enter_context(nc.sbuf_tensor(f"{name}_wl{i}", [P, hk, P], F32R)) for i in range(2)]
        w_in = [half.landed, sem("w_in1")]
        rounded, split, used, added = (sem(n) for n in ("rounded", "split", "used", "added"))

        with nc.Block(name) as block:
            @block.sync
            def _(sp):
                def load(i, halves=(0, 1)):
                    for b in halves:
                        emit_wait(sp, split, 2 * i - 1 + b)
                        sp.dma_start(slab[b][:, :, :], w[bass.ds(i, 1), :, b * hk:b * hk + hk]
                                     .rearrange("a p k m -> (a p) k m")).then_inc(w_in[b], 16)
                load(0, (1,))
                with sp.Fori(1, DC) as i:
                    load(i)

            @block.scalar
            def _(act):
                def round_(i):
                    for b in range(2):
                        act.wait_ge(w_in[b], 16 * i + 16)
                        emit_wait(act, used, 2 * i - 1 + b)
                        nc.scalar.copy(high[b][:, :, :], slab[b][:, :, :]).then_inc(rounded, 1)
                repeat(act, DC, round_)

            @block.tensor
            def _(pe):
                def project(i):
                    for e in range(2):
                        emit_wait(pe, added, 2 * i - 1 + e)
                        for b in range(2):
                            pe.wait_ge(split, 4 * i + 2 * e + b + 1)
                            for j in range(hk):
                                mm = c.product(c.bank(e), (high[b][:, j, :], low[b][:, j, :]),
                                               (src[0][:, b * hk + j, :], src[1][:, b * hk + j, :]),
                                               b == 0 and j == 0, b == 1 and j == hk - 1)
                            mm.then_inc(used, 1)
                repeat(pe, DC // 2, project)

            @block.vector
            def _(dve):
                def rest(i, b):
                    dve.wait_ge(rounded, 2 * i + b + 1)
                    nc.vector.tensor_tensor(low[b][:, :, :], slab[b][:, :, :], high[b][:, :, :].bitcast(F32),
                                            ALU.subtract).then_inc(split, 1)

                def add(i, last=False):
                    for e in range(2):
                        more = not (last and e == 1)
                        if more:
                            rest(2 * i + e + 1, 0)
                        dve.wait_ge(used, 4 * i + 2 * e + 2)
                        hc = c.h[:, bass.ds(2 * i + e, 1), :].rearrange("p a t -> p (a t)")
                        nc.vector.tensor_tensor(hc, c.bank(e), hc, ALU.add).then_inc(added, 1)
                        if more:
                            rest(2 * i + e + 1, 1)

                rest(0, 0)
                rest(0, 1)
                add(0)
                with dve.Fori(1, DC // 2 - 1) as i:
                    add(i)
                add(DC // 2 - 1, last=True)


class Weights:

    def __init__(self, c, stack, name):
        new = lambda x, dt: stack.enter_context(c.nc.sbuf_tensor(f"{name}_{x}", [P, 3, DC, P], dt))
        self.slab, self.high, self.low = new("w", F32), new("wh", F32R), new("wl", F32R)


def weights_ahead(c, stage, wt, w):
    landed, rounded = ([stage.sem(f"{n}_{j}") for j in "qkv"] for n in ("ahead_in", "ahead_rounded"))

    def load(sp):
        for i in range(3):
            sp.dma_start(wt.slab[:, i, :, :], w[0:1, i].rearrange("a p k m -> (a p) k m")).then_inc(landed[i], 16)

    def round_(act):
        for i in range(3):
            act.wait_ge(landed[i], 16)
            c.nc.scalar.copy(wt.high[:, i, :, :], wt.slab[:, i, :, :]).then_inc(rounded[i], 1)

    def rest(pool):
        for i in range(3):
            pool.wait_ge(rounded[i], 1)
            c.nc.gpsimd.tensor_tensor(wt.low[:, i, :, :], wt.slab[:, i, :, :], wt.high[:, i, :, :].bitcast(F32),
                                      ALU.subtract)

    return load, round_, rest


def stage_attention(c, name, kind, n, wt, w, x, first, bias=None, bias_ready=None, next_w=None, aside=None,
                    also=None):
    nc = c.nc
    diff, rope = kind == "diff", kind in ("dsa", "sink")
    banded = kind in ("diff", "rel")
    direct = kind in ("rel", "forget")
    comb = 1 if diff else 2
    order = [(3, 0), (3, 1), (2, 0), (2, 1), (1, 0), (0, 0), (1, 1), (0, 1)]
    col = {(3, 0): 0, (3, 1): 1, (2, 0): 2, (2, 1): 3, (1, 0): 4, (1, 1): 5, (0, 0): 6, (0, 1): 7}
    scored_at = [1, 2, 3, 4, 5, 5, 6, 6]
    seq = {t: i + 1 for i, t in enumerate(order)}

    def keys(qt):
        return (128 * max(qt - 1, 0) if kind == "sink" else 0), 128 * (qt + 1)

    def score_bank(qt, s):
        k0, k1 = keys(qt)
        if qt == 3:
            return c.ps[:, s, 0:k1 - k0]
        if qt == 2:
            return c.ps[:, 2 + s, 0:k1 - k0]
        return c.ps[:, s, 0:k1 - k0] if qt == 1 else c.ps[:, s, 256:384]

    with Stage(nc, name) as ctx:
        sem = ctx.sem
        sb = lambda x, shape: ctx.enter_context(nc.sbuf_tensor(f"{name}_{x}", shape, F32))
        slab, high, low = wt.slab, wt.high, wt.low
        qT, kT, vT, v = sb("qT", [P, T]), sb("kT", [P, T]), sb("vT", [P, T]), sb("v", [P, TT, P])
        raw = None if direct else sb("raw", [P, 2, T])
        tmp = None if direct else sb("tmp", [P, 2, T])
        tmp2 = None if direct else sb("tmp2", [P, 2, T])
        prob = sb("prob", [P, 2, PW])
        probT = sb("probT", [P, comb, TT, T])
        btile = sb("btile", [P, 1 if diff else 2, T]) if banded else None
        nmax, total, inv = sb("nmax", [P, 8]), sb("total", [P, 8]), sb("inv", [P, 8])
        esink = sb("esink", [P, 8]) if kind == "sink" else None
        sink_u = sb("sink_u", [P, 2, 2]) if kind == "sink" else None
        (q_in, k_in, v_in, b_in, b_ok, q_proj, k_proj, v_proj, q_raw, k_raw, q_help, k_help, q_half, k_half, q_half2,
         k_half2, q_ok, k_ok, v_ok, scored, shifted, expd, inv_ok, inv2_ok, scaled, normed, turned, copied, pv_done,
         o_ok, sink_ok) = (
            sem(x) for x in ("q_in", "k_in", "v_in", "b_in", "b_ok", "q_proj", "k_proj", "v_proj", "q_raw", "k_raw",
                             "q_help", "k_help", "q_half", "k_half", "q_half2", "k_half2", "q_ok", "k_ok", "v_ok",
                             "scored", "shifted", "expd", "inv_ok", "inv2_ok", "scaled", "normed", "turned",
                             "copied", "pv_done", "o_ok", "sink_ok"))
        v_copied, v_turned = sem("v_copied"), sem("v_turned")
        rounded, split = ([sem(f"{i}_{j}") for j in "qkv"] for i in ("rounded", "split"))
        o_high, logged = sem("o_high"), sem("logged")
        passed_pe, passed_dve = sem("passed_pe"), sem("passed_dve")
        ngrp = 4 if diff else 8

        def sl(s, qt):
            k0, k1 = keys(qt)
            return prob[:, s, OFF[qt]:OFF[qt] + k1 - k0]

        def bias_tile(s, qt):
            if kind == "diff":
                return btile[:, 0, T - P - P * qt:T]
            if kind == "rel":
                return btile[:, s, T - P - P * qt:T]
            return bias(s, qt)

        def rounds(body, eng):
            body(0, True, False, True)
            with eng.Fori(1, n - 1) as u:
                body(u, True, True, True)
            body(n - 1, True, True, next_w is not None)
            body(n, False, True, False)

        with nc.Block(name) as block:
            @block.sync
            def _(sp):
                def load_bias(u):
                    if banded:
                        emit_wait(sp, shifted, u * 8)
                        nb = 1 if diff else 2
                        src = bias[bass.ds(u * nb, nb)] if not isinstance(u, int) else bias[u * nb:(u + 1) * nb]
                        sp.dma_start(btile[:, :, :], src.rearrange("h p m -> p h m")).then_inc(b_in, 16)
                def load(u, w, at):
                    for i, landed in enumerate((q_in, k_in, v_in)):
                        emit_wait(sp, split[i], u - 1)
                        src = w[bass.ds(at, 1), i] if not isinstance(at, int) else w[at:at + 1, i]
                        sp.dma_start(slab[:, i, :, :], src.rearrange("a p k m -> (a p) k m")).then_inc(landed, 16)

                if bias_ready is not None:
                    sp.wait_ge(bias_ready, 16)
                if also:
                    also(sp)
                load(1, w, 1)
                load_bias(0)
                load_bias(1)
                with sp.Fori(2, n) as u:
                    load(u, w, u)
                    load_bias(u)
                if next_w is not None:
                    load(n, next_w, 0)

            @block.gpsimd
            def _(pool):
                def rest(i, u):
                    pool.wait_ge(rounded[i], u)
                    nc.gpsimd.tensor_tensor(low[:, i, :, :], slab[:, i, :, :], high[:, i, :, :].bitcast(F32),
                                            ALU.subtract).then_inc(split[i], 1)

                if kind == "rel":
                    def mask(u):
                        pool.wait_ge(b_in, 16 * u + 16)
                        for s in range(2):
                            d = btile[:, s, T - P:T]
                            nc.gpsimd.tensor_tensor(d, d, c.k("cmask"), ALU.add).then_inc(b_ok, 1)
                if rope:
                    def turn(u, i):
                        have, half, ready = ((q_raw, q_half, q_ok), (k_raw, k_half, k_ok))[i]
                        pool.wait_ge(have, u + 1)
                        emit_wait(pool, ready, u)
                        nc.gpsimd.tensor_tensor(tmp[:, i, :], raw[:, i, :], c.k("cos"), ALU.mult).then_inc(half, 1)

                def body(u, project, attend, ahead):
                    if kind == "rel" and project:
                        mask(u)
                    for i in range(3):
                        if ahead:
                            rest(i, u + 1)
                        if rope and project and i < 2:
                            turn(u, i)

                rounds(body, pool)

            @block.tensor
            def _(pe):
                def scores(u, tiles):
                    for qt, s in tiles:
                        k0, k1 = keys(qt)
                        out, hd = score_bank(qt, s), slice(HD * s, HD * s + HD)
                        if kind == "forget":
                            f = c.fneg[0:1, bass.ds(2 * (u - 1) + s, 1), k0:k1].rearrange("p a t -> p (a t)")
                            nc.tensor.matmul(out, c.k("ones")[0:1, :], f, start=True, stop=False)
                        mm = nc.tensor.matmul(out, qT[hd, P * qt:P * qt + P], kT[hd, k0:k1],
                                              start=(kind != "forget"), stop=True)
                        if qt != 1:
                            mm.then_inc(scored, 1)

                def turn(u, g):
                    for j in range(TT):
                        if g:
                            pe.wait_ge(copied, (u - 1) * 4 * comb + j + 1)
                        for qt in range(j, min(TT, j + 2) if kind == "sink" else TT):
                            k0, _ = keys(qt)
                            at = OFF[qt] + P * j - k0
                            mm = nc.tensor.transpose(c.ps[:, j, P * qt:P * qt + P], prob[:, g, at:at + P],
                                                     c.k("ident"))
                        mm.then_inc(turned, 1)

                def project_fm(slot, bank_i, done, u):
                    emit_wait(pe, split[slot], u)
                    for i in range(DC):
                        mm = c.product(c.bank(bank_i), (high[:, slot, i, :], low[:, slot, i, :]),
                                       (x[0][:, i, :], x[1][:, i, :]), i == 0, i == DC - 1)
                    mm.then_inc(done, 1)

                def turn_v(u):
                    pe.wait_ge(v_copied, u + 1)
                    for j in range(TT):
                        mm = nc.tensor.transpose(c.ps[:, 6, P * j:P * j + P], vT[:, P * j:P * j + P], c.k("ident"))
                    mm.then_inc(v_turned, 1)

                def help_fm(i, bank_i, have, done, u):
                    pe.wait_ge(have, u + 1)
                    nc.tensor.matmul(c.bank(bank_i), c.k("rot") if rope else c.k("blk64"),
                                     raw[:, i, :] if rope else tmp[:, i, :], start=True, stop=True).then_inc(done, 1)

                def body(u, project, attend, ahead):
                    if attend:
                        pe.wait_ge(q_ok, u)
                        wait_apart(pe, k_ok, u, passed_pe)
                        scores(u, order[:4])
                    if project:
                        emit_wait(pe, q_ok, u)
                        project_fm(0, 4, q_proj, u)
                    if attend:
                        wait_apart(pe, shifted, (u - 1) * 8 + 1, passed_pe)
                        scores(u, order[4:6])
                        wait_apart(pe, shifted, (u - 1) * 8 + 2, passed_pe)
                        scores(u, order[6:])
                    if project:
                        emit_wait(pe, k_ok, u)
                        project_fm(1, 5, k_proj, u)
                        if not direct:
                            help_fm(0, 4, q_raw, q_help, u)
                    if attend:
                        pe.wait_ge(normed, ngrp * u)
                        turn(u, 0)
                    if project:
                        if not direct:
                            help_fm(1, 5, k_raw, k_help, u)
                        emit_wait(pe, v_ok, u)
                        project_fm(2, 6, v_proj, u)
                    if attend and comb == 2:
                        turn(u, 1)
                    if attend:
                        pe.wait_ge(v_ok, u)
                        for g in range(comb):
                            rows = slice(0, P) if diff else slice(HD * g, HD * g + HD)
                            if kind != "sink":
                                for j in range(TT):
                                    pe.wait_ge(copied, (u - 1) * 4 * comb + 4 * g + j + 1)
                                    mm = nc.tensor.matmul(c.ps[rows, 7, P * j:T], v[:, j, rows],
                                                          probT[:, g, j, P * j:T], start=(j == 0), stop=(j == TT - 1))
                            else:
                                pe.wait_ge(copied, (u - 1) * 4 * comb + 4 * g + TT)
                                for qt in range(TT):
                                    for j in range(max(qt - 1, 0), qt + 1):
                                        mm = nc.tensor.matmul(
                                            c.ps[rows, 7, P * qt:P * qt + P], v[:, j, rows],
                                            probT[:, g, j, P * qt:P * qt + P], start=(j == max(qt - 1, 0)),
                                            stop=(j == qt))
                        mm.then_inc(pv_done, 1)
                    if project:
                        turn_v(u)
                rounds(body, pe)

            @block.scalar
            def _(act):
                def exps(u, tiles):
                    for qt, s in tiles:
                        i = col[qt, s]
                        act.wait_ge(shifted, (u - 1) * 8 + seq[qt, s])
                        if kind == "sink":
                            nc.scalar.activation(esink[:, i:i + 1], nmax[:, i:i + 1], ACT.Exp,
                                                 bias=sink_u[:, s, 0:1])
                        nc.scalar.activation(sl(s, qt), sl(s, qt), ACT.Exp, bias=nmax[:, i:i + 1], scale=-1.0,
                                             accum_out=total[:, i:i + 1]).then_inc(expd, 1)

                def copy_turned(u, g):
                    for j in range(TT):
                        hi = min(T, P * (j + 2)) if kind == "sink" else T
                        act.wait_ge(turned, (u - 1) * 4 * comb + 4 * g + j + 1)
                        nc.scalar.copy(probT[:, g, j, P * j:hi], c.ps[:, j, P * j:hi]).then_inc(copied, 1)

                def round_(i, landed, used, u):
                    act.wait_ge(landed, 16 * u)
                    act.wait_ge(used, u)
                    nc.scalar.copy(high[:, i, :, :], slab[:, i, :, :]).then_inc(rounded[i], 1)

                def raw_out(i, bank_i, proj, have, u):
                    act.wait_ge(proj, u + 1)
                    if diff:
                        nc.scalar.copy(raw[:, i, :], c.bank(bank_i))
                        nc.scalar.activation(tmp[:, i, :], c.bank(bank_i), ACT.Square).then_inc(have, 1)
                    else:
                        nc.scalar.activation(raw[:, i, :], c.bank(bank_i), ACT.Copy,
                                             scale=QK_SCALE if i == 0 else 1.0).then_inc(have, 1)

                def body(u, project, attend, ahead):
                    if attend:
                        exps(u, order[:4])
                    if project and not direct:
                        emit_wait(act, q_ok, u)
                        raw_out(0, 4, q_proj, q_raw, u)
                    if attend:
                        exps(u, order[4:])
                    if ahead:
                        round_(0, q_in, q_proj, u + 1)
                    if project and not direct:
                        emit_wait(act, k_ok, u)
                        raw_out(1, 5, k_proj, k_raw, u)
                    if ahead and not direct:
                        round_(1, k_in, k_proj, u + 1)
                    if project and direct:
                        if attend:
                            act.wait_ge(scored, 6 * u)
                        act.wait_ge(q_proj, u + 1)
                        nc.scalar.activation(qT[:, :], c.bank(4), ACT.Copy, scale=QK_SCALE).then_inc(q_ok, 1)
                        act.wait_ge(k_proj, u + 1)
                        nc.scalar.activation(kT[:, :], c.bank(5), ACT.Copy).then_inc(k_ok, 1)
                    if ahead and direct:
                        round_(1, k_in, k_proj, u + 1)
                    if attend:
                        for g in range(comb):
                            copy_turned(u, g)
                    if project and diff:
                        for i, (helped, bank_i) in enumerate(((q_help, 4), (k_help, 5))):
                            act.wait_ge(helped, u + 1)
                            nc.scalar.activation(tmp[:, i, :], c.bank(bank_i), ACT.Ln, bias=c.eps[:, 0:1])\
                              .then_inc(logged, 1)
                        for i, half in enumerate((q_half, k_half)):
                            act.wait_ge(logged, 2 * u + i + 1)
                            nc.scalar.activation(tmp[:, i, :], tmp[:, i, :], ACT.Exp, scale=-0.5).then_inc(half, 1)
                    if project:
                        act.wait_ge(v_proj, u + 1)
                        nc.scalar.copy(vT[:, :], c.bank(6)).then_inc(v_copied, 1)
                    if ahead:
                        round_(2, v_in, v_proj, u + 1)
                    if attend:
                        act.wait_ge(pv_done, u)
                        oc = c.o[0][:, bass.ds(first + u - 1, 1), :].rearrange("p a t -> p (a t)")
                        nc.scalar.copy(oc, c.bank(7)).then_inc(o_ok if diff else o_high, 1)

                rounds(body, act)

            @block.vector
            def _(dve):
                def shift(u, tiles, at):
                    for t, (qt, s) in enumerate(tiles):
                        i = col[qt, s]
                        wait_apart(dve, scored, (u - 1) * 6 + scored_at[at + t], passed_dve)
                        nc.vector.tensor_tensor_reduce(
                            out=sl(s, qt), in0=score_bank(qt, s), in1=bias_tile(s, qt), scale=-1.0,
                            scalar=(sink_u[:, s, 1:2] if kind == "sink" else HUGE), op0=ALU.add, op1=ALU.min,
                            accum_out=nmax[:, i:i + 1]).then_inc(shifted, 1)

                def normalise(u, tiles, half):
                    x = slice(4 * half, 4 * half + 4)
                    dve.wait_ge(expd, (u - 1) * 8 + 4 * half + 4)
                    if kind == "sink":
                        nc.vector.tensor_tensor(total[:, x], total[:, x], esink[:, x], ALU.add).then_inc(inv2_ok, 1)
                        dve.wait_ge(inv2_ok, (u - 1) * 2 + half + 1)
                    nc.vector.reciprocal(inv[:, x], total[:, x]).then_inc(inv_ok, 1)
                    dve.wait_ge(inv_ok, (u - 1) * 2 + half + 1)
                    if diff:
                        odd = inv[:, 4 * half + 1:4 * half + 4:2]
                        nc.vector.tensor_scalar(odd, odd, c.neglam[:, 0:1], None, ALU.mult).then_inc(inv2_ok, 1)
                        qts = [3, 2] if half == 0 else [1, 0]
                        for qt in qts:
                            i = col[qt, 0]
                            nc.vector.tensor_scalar(sl(0, qt), sl(0, qt), inv[:, i:i + 1], None, ALU.mult)\
                              .then_inc(scaled, 1)
                        dve.wait_ge(inv2_ok, (u - 1) * 2 + half + 1)
                        for m, qt in enumerate(qts):
                            i = col[qt, 1]
                            dve.wait_ge(scaled, (u - 1) * 4 + 2 * half + m + 1)
                            nc.vector.scalar_tensor_tensor(out=sl(0, qt), in0=sl(1, qt), scalar=inv[:, i:i + 1],
                                                           in1=sl(0, qt), op0=ALU.mult, op1=ALU.add)\
                              .then_inc(normed, 1)
                    else:
                        for qt, s in tiles:
                            i = col[qt, s]
                            nc.vector.tensor_scalar(sl(s, qt), sl(s, qt), inv[:, i:i + 1], None, ALU.mult)\
                              .then_inc(normed, 1)

                def finish(i, bank_i, half, half2, helped, dst, gain, ok, u):
                    if diff:
                        dve.wait_ge(half, u + 1)
                        nc.vector.scalar_tensor_tensor(out=dst, in0=raw[:, i, :], scalar=gain, in1=tmp[:, i, :],
                                                       op0=ALU.mult, op1=ALU.mult).then_inc(ok, 1)
                    else:
                        dve.wait_ge(helped, u + 1)
                        nc.vector.tensor_tensor(tmp2[:, i, :], c.bank(bank_i), c.k("sin"), ALU.mult)\
                          .then_inc(half2, 1)
                        dve.wait_ge(half, u + 1)
                        dve.wait_ge(half2, u + 1)
                        nc.vector.tensor_tensor(dst, tmp[:, i, :], tmp2[:, i, :], ALU.add).then_inc(ok, 1)

                def body(u, project, attend, ahead):
                    if attend:
                        if banded:
                            dve.wait_ge(b_in if diff else b_ok, 16 * u if diff else 2 * u)
                        if kind == "sink":
                            s0 = PARAMS["sinks"][0]
                            pair = c.param[:, bass.ds(s0 + 2 * (u - 1), 2)]
                            nc.vector.tensor_copy(sink_u[:, :, 0], pair).then_inc(sink_ok, 1)
                            nc.vector.tensor_scalar(sink_u[:, :, 1], pair, -1.0, None, ALU.mult).then_inc(sink_ok, 1)
                            dve.wait_ge(sink_ok, 2 * u)
                        shift(u, order[:4], 0)
                        normalise(u, order[:4], 0)
                        shift(u, order[4:], 4)
                        normalise(u, order[4:], 1)
                    if aside:
                        aside(dve, u, passed_dve)
                    if project and not direct:
                        finish(0, 4, q_half, q_half2, q_help, qT[:, :], c.qgain[:, 0:1] if diff else None, q_ok, u)
                        finish(1, 5, k_half, k_half2, k_help, kT[:, :], c.p("kg") if diff else None, k_ok, u)
                    if project:
                        dve.wait_ge(v_turned, u + 1)
                        if attend:
                            dve.wait_ge(pv_done, u)
                        nc.vector.tensor_copy(v[:, :, :].rearrange("p a e -> p (a e)"), c.bank(6)).then_inc(v_ok, 1)
                    if attend and not diff:
                        dve.wait_ge(o_high, u)
                        at = bass.ds(first + u - 1, 1)
                        nc.vector.tensor_tensor(
                            c.o[1][:, at, :].rearrange("p a t -> p (a t)"), c.bank(7),
                            c.o[0][:, at, :].bitcast(F32).rearrange("p a t -> p (a t)"), ALU.subtract)\
                          .then_inc(o_ok, 1)
                rounds(body, dve)


def stage_diff_prepare(c):
    nc = c.nc
    with Stage(nc, "dprep") as ctx:
        sem = ctx.sem
        scratch = ctx.enter_context(nc.sbuf_tensor("dprep_s", [P, 2, HD], F32))
        dots = ctx.enter_context(nc.sbuf_tensor("dprep_d", [P, 2], F32))
        ex = ctx.enter_context(nc.sbuf_tensor("dprep_e", [P, 2], F32))
        dif = ctx.enter_context(nc.sbuf_tensor("dprep_f", [P, 1], F32))
        dotted, expd, step = sem("dotted"), sem("expd"), sem("step")
        with nc.Block("dprep") as block:
            @block.sync
            def _(sp):
                sp.dma_start(c.a["plist"], c.a["empty"]).then_inc(c.list_empty, 16)
                sp.dma_start(c.a["relrows"], bass.AP(c.a["relE"].tensor, 0, [[640, 8], [0, P], [1, 640]]))\
                  .then_inc(c.rel_spread, 16)

            @block.vector
            def _(dve):
                for i in range(2):
                    nc.vector.tensor_tensor_reduce(
                        out=scratch[:, i, :], in0=c.p("lam", 2 * i * HD, HD), in1=c.p("lam", (2 * i + 1) * HD, HD),
                        scale=1.0, scalar=0.0, op0=ALU.mult, op1=ALU.add, accum_out=dots[:, i:i + 1])\
                      .then_inc(dotted, 1)
                nc.vector.tensor_scalar(c.qgain[:, :], c.p("qg"), QK_SCALE, None, ALU.mult)
                dve.wait_ge(expd, 1)
                nc.vector.tensor_tensor(dif[:, :], ex[:, 1:2], ex[:, 0:1], ALU.subtract).then_inc(step, 1)
                dve.wait_ge(step, 1)
                nc.vector.tensor_scalar(c.neglam[:, :], dif[:, :], LAMBDA_INIT, None, ALU.subtract)

            @block.scalar
            def _(act):
                act.wait_ge(dotted, 2)
                nc.scalar.activation(ex[:, :], dots[:, :], ACT.Exp).then_inc(expd, 1)


def stage_subln(c, o, parts, ahead):
    nc = c.nc
    with Stage(nc, "subln") as ctx:
        sem = ctx.sem
        sq = ctx.enter_context(nc.sbuf_tensor("subln_sq", [P, DC, T], F32))
        rs = ctx.enter_context(nc.sbuf_tensor("subln_rs", [P, DC, T], F32))
        g = ctx.enter_context(nc.sbuf_tensor("subln_g", [P, 1], F32))
        squared, squared_v, meaned, logged, inverted, gained, scaled, rounded = (
            sem(n) for n in ("squared", "squared_v", "meaned", "logged", "inverted", "gained", "scaled", "rounded"))

        def low(eng, i):
            eng.wait_ge(rounded, i + 1)
            (nc.vector if i % 2 == 0 else nc.gpsimd).tensor_tensor(
                parts[1][:, i, :], o[:, i, :], parts[0][:, i, :].bitcast(F32), ALU.subtract)

        with nc.Block("subln") as block:
            @block.sync
            def _(sp):
                ahead(sp)

            @block.scalar
            def _(act):
                for i in range(0, DC, 2):
                    nc.scalar.activation(sq[:, i, :], o[:, i, :], ACT.Square).then_inc(squared, 1)
                for i in range(DC):
                    act.wait_ge(meaned, i + 1)
                    nc.scalar.activation(sq[:, i, :], c.bank(i), ACT.Ln, bias=c.eps[:, 0:1]).then_inc(logged, 1)
                for i in range(DC + 2):
                    if i < DC:
                        act.wait_ge(logged, i + 1)
                        nc.scalar.activation(rs[:, i, :], sq[:, i, :], ACT.Exp, scale=-0.5).then_inc(inverted, 1)
                    if i >= 2:
                        act.wait_ge(scaled, i - 1)
                        nc.scalar.copy(parts[0][:, i - 2, :], o[:, i - 2, :]).then_inc(rounded, 1)

            @block.tensor
            def _(pe):
                for i in range(DC):
                    pe.wait_ge((squared, squared_v)[i % 2], i // 2 + 1)
                    nc.tensor.matmul(c.bank(i), c.k("inv_p"), sq[:, i, :], start=True, stop=True)\
                      .then_inc(meaned, 1)

            @block.vector
            def _(dve):
                for i in range(1, DC, 2):
                    nc.vector.tensor_tensor(sq[:, i, :], o[:, i, :], o[:, i, :], ALU.mult).then_inc(squared_v, 1)
                nc.vector.tensor_scalar(g[:, :], c.p("subln"), 1.0 - LAMBDA_INIT, None, ALU.mult).then_inc(gained, 1)
                dve.wait_ge(gained, 1)
                for i in range(DC):
                    dve.wait_ge(inverted, i + 1)
                    nc.vector.scalar_tensor_tensor(out=o[:, i, :], in0=o[:, i, :], scalar=g[:, 0:1],
                                                   in1=rs[:, i, :], op0=ALU.mult, op1=ALU.mult).then_inc(scaled, 1)
                    if i >= 3 and i % 2:
                        low(dve, i - 3)
                low(dve, DC - 2)

            @block.gpsimd
            def _(pool):
                for i in range(1, DC, 2):
                    low(pool, i)



def stage_ffn_up(c, name, layer, w, gain, out, also):
    nc = c.nc
    with Stage(nc, name) as ctx:
        sem = ctx.sem
        sb = lambda x, shape: ctx.enter_context(nc.sbuf_tensor(f"{name}_{x}", shape, F32))
        slab = [sb(f"w{b}", [P, 2, DC, P]) for b in range(2)]
        high, low = ([ctx.enter_context(nc.sbuf_tensor(f"{name}_{i}{v}", [P, DC, P], F32R)) for v in range(2)]
                     for i in ("wh", "wl"))
        work = sb("work", [P, DC, T])
        acc, prod = work[:, 0:4, :], work[:, 4:6, :]
        x = [ctx.enter_context(nc.sbuf_tensor(f"{name}_x{i}", [P, DC, T], F32R)) for i in range(2)]
        w_in = [sem(f"w_in{b}") for b in range(2)]
        rounded, split, projected, based, tap1, tap0, gated, multiplied, out_high, done = (
            sem(n) for n in ("rounded", "split", "projected", "based", "tap1", "tap0", "gated", "multiplied",
                             "out_high", "done"))
        cw, cb = PARAMS["convw"][0] + layer * 2 * FC * 3, PARAMS["convb"][0] + layer * 2 * FC

        def weight(j, v, tap):
            return c.param[:, bass.ds(cw + (j + v * FC) * 3 + tap, 1)]

        def load(sp, i):
            for b in range(2):
                emit_wait(sp, split, 4 * i - 2 + 2 * b)
                sp.dma_start(slab[b][:, :, :, :], w[bass.ds(2 * i + b, 1)].rearrange("a p x k m -> (a p) x k m"))\
                  .then_inc(w_in[b], 16)

        def round_(act, i, b, v):
            act.wait_ge(w_in[b], 16 * i + 16)
            emit_wait(act, projected, 4 * i + 2 * b + v - 1)
            nc.scalar.copy(high[v][:, :, :], slab[b][:, v, :, :]).then_inc(rounded, 1)

        def rest(pool, i, b, v):
            pool.wait_ge(rounded, 4 * i + 2 * b + v + 1)
            nc.gpsimd.tensor_tensor(low[v][:, :, :], slab[b][:, v, :, :],
                                    high[v][:, :, :].bitcast(F32), ALU.subtract).then_inc(split, 1)

        def round_first(act):
            for v in range(2):
                round_(act, 0, 0, v)

        def rest_first(pool):
            for v in range(2):
                rest(pool, 0, 0, v)

        scaling = Scaling(c, ctx, name, gain, x, work)
        stage_norm(c, f"{name}_norm", gain, x, work, ahead=(lambda sp: load(sp, 0), round_first, rest_first),
                   scaling=scaling)
        with nc.Block(name) as block:
            @block.sync
            def _(sp):
                load(sp, 1)
                also(sp)
                with sp.Fori(2, FC // 2) as i:
                    load(sp, i)

            @block.gpsimd
            def _(pool):
                scaling.gpsimd(pool)
                for v in range(2):
                    rest(pool, 0, 1, v)
                with pool.Fori(1, FC // 2) as i:
                    for b in range(2):
                        for v in range(2):
                            rest(pool, i, b, v)

            @block.tensor
            def _(pe):
                def project(i):
                    for b in range(2):
                        for v in range(2):
                            pe.wait_ge(split, 4 * i + 2 * b + v + 1)
                            emit_wait(pe, tap0, 4 * (i - 1) + 2 * b + v + 1 if not isinstance(i, int) else 0)
                            for j in range(DC):
                                if isinstance(i, int) and b == 0 and v == 0:
                                    scaling.wait(pe, j)
                                mm = c.product(c.bank(2 * b + v), (high[v][:, j, :], low[v][:, j, :]),
                                               (x[0][:, j, :], x[1][:, j, :]), j == 0, j == DC - 1)
                            mm.then_inc(projected, 1)
                repeat(pe, FC // 2, project)

            @block.scalar
            def _(act):
                def first_tap(i, last):
                    for b in range(2):
                        for v in range(2):
                            act.wait_ge(projected, 4 * i + 2 * b + v + 1)
                            emit_wait(act, multiplied, 2 * i - 1 + b if not isinstance(i, int) else 0)
                            if b == 0:
                                round_(act, i, 1, v)
                            elif not last:
                                round_(act, i + 1, 0, v)
                            nc.scalar.activation(
                                acc[:, 2 * b + v, :], c.bank(2 * b + v), ACT.Identity,
                                bias=c.param[:, bass.ds(cb + 2 * i + b + v * FC, 1)],
                                scale=weight(2 * i + b, v, 2)).then_inc(based, 1)
                            if v == 0:
                                act.wait_ge(tap0, 4 * i + 2 * b + 1)
                                nc.scalar.activation(acc[:, 2 * b, :], acc[:, 2 * b, :], ACT.Silu).then_inc(gated, 1)
                        act.wait_ge(multiplied, 2 * i + b + 1)
                        nc.scalar.copy(out[0][:, bass.ds(2 * i + b, 1), :].rearrange("p a t -> p (a t)"),
                                       prod[:, b, :]).then_inc(out_high, 1)

                scaling.scalar(act)
                for i in (DC - 2, DC - 1):
                    scaling.wait(act, i)
                first_tap(0, False)
                with act.Fori(1, FC // 2 - 1) as i:
                    first_tap(i, False)
                first_tap(FC // 2 - 1, True)

            @block.vector
            def _(dve):
                def convolve(i):
                    for b in range(2):
                        for v in range(2):
                            n = 4 * i + 2 * b + v + 1
                            y = acc[:, 2 * b + v, :]
                            raw = c.bank(2 * b + v)
                            dve.wait_ge(based, n)
                            nc.vector.scalar_tensor_tensor(
                                out=y[:, 1:T], in0=raw[:, 0:T - 1], scalar=weight(2 * i + b, v, 1), in1=y[:, 1:T],
                                op0=ALU.mult, op1=ALU.add).then_inc(tap1, 1)
                            dve.wait_ge(tap1, n)
                            nc.vector.scalar_tensor_tensor(
                                out=y[:, 2:T], in0=raw[:, 0:T - 2], scalar=weight(2 * i + b, v, 0), in1=y[:, 2:T],
                                op0=ALU.mult, op1=ALU.add).then_inc(tap0, 1)
                        dve.wait_ge(gated, 2 * i + b + 1)
                        dve.wait_ge(tap0, 4 * i + 2 * b + 2)
                        emit_wait(dve, done, 2 * i - 1 + b if not isinstance(i, int) else 0)
                        nc.vector.tensor_tensor(prod[:, b, :], acc[:, 2 * b, :], acc[:, 2 * b + 1, :], ALU.mult)\
                          .then_inc(multiplied, 1)
                        dve.wait_ge(out_high, 2 * i + b + 1)
                        at = bass.ds(2 * i + b, 1)
                        nc.vector.tensor_tensor(
                            out[1][:, at, :].rearrange("p a t -> p (a t)"), prod[:, b, :],
                            out[0][:, at, :].bitcast(F32).rearrange("p a t -> p (a t)"), ALU.subtract)\
                          .then_inc(done, 1)
                scaling.vector(dve)
                repeat(dve, FC // 2, convolve)


def stage_route(c):
    nc, a = c.nc, c.a
    with Stage(nc, "route") as ctx:
        sem = ctx.sem
        sb = lambda x, shape, dt=F32: ctx.enter_context(nc.sbuf_tensor(f"route_{x}", shape, dt))
        wr = sb("w", [P, DC, 20])
        rows = sb("rows", [P, TT, D])
        L = sb("L", [P, TT, 20])
        gmax, taken, fresh = sb("gmax", [P, TT]), sb("taken", [P, TT]), sb("fresh", [P, TT])
        selg = sb("selg", [P, TT, 4])
        ex, gsum, gate = sb("ex", [P, TT, 4]), sb("gsum", [P, TT]), sb("gate", [P, TT])
        le, tmp4 = sb("le", [P, TT, 4]), sb("tmp4", [P, TT, 4])
        s12 = sb("s12", [P, 2, TT, 4])
        val = sb("val", [P, 2, TT])
        wt = sb("wt", [P, 2, TT])
        M = sb("M", [P, 2, TT, N_EXP])
        Ms = sb("Ms", [P, TT, N_EXP])
        cnt, tiles, incl, excl = (sb(x, [P, N_EXP]) for x in ("cnt", "tiles", "incl", "excl"))
        pos = sb("pos", [P, TT, N_EXP])
        tm = sb("tm", [P, 2, TT, N_EXP])
        dst = sb("dst", [P, 2, TT])
        dsti = sb("dsti", [P, 2, TT], U32)
        rec = sb("rec", [P, 2, TT, 4], I32)
        cmp = sb("cmp", [1, 24, N_EXP])
        tl = sb("tl", [1, 25])
        w_in, rec_in, turned, copied, logits, step, expd, exp_in, counted, placed, stored, back = (
            sem(x) for x in ("w_in", "rec_in", "turned", "copied", "logits", "step", "expd", "exp_in", "counted",
                             "placed", "stored", "back"))
        listed = ctx.dma_sem("listed")
        fwd_tiles = sem("fwd_tiles")
        with nc.Block("route") as block:
            @block.sync
            def _(sp):
                sp.dma_start(wr[:, :, :], a["w_route"]).then_inc(w_in, 16)
                sp.dma_start(rec[:, :, :, :], a["rec"]).then_inc(rec_in, 16)
                sp.dma_start(c.slots[:, 24, :], a["empty"][0:P, :]).then_inc(rec_in, 16)
                for tt in range(TT):
                    sp.wait_ge(copied, 2 * tt + 2)
                    sp.dma_start(a["hrows"][tt * P:(tt + 1) * P, :], rows[:, tt, :]).then_inc(stored, 16)
                sp.wait_ge(listed, 16 * 8)
                sp.dma_start(c.slots[:, 0:24, :], a["plist"].rearrange("(t p) x -> p t x", p=P)).then_inc(back, 16)
                sp.wait_ge(back, 16)
                sp.wait_ge(stored, 16 * TT)

            @block.tensor
            def _(pe):
                pe.wait_ge(w_in, 16)
                for tt in range(TT):
                    for i in range(DC):
                        mm = nc.tensor.matmul(c.ps[:, 4, 20 * tt:20 * tt + 20], c.xn[:, i, P * tt:P * tt + P],
                                              wr[:, i, :], start=(i == 0), stop=(i == DC - 1))
                mm.then_inc(logits, 1)
                for tt in range(TT):
                    for half in range(2):
                        n = 2 * tt + half
                        if n >= 4:
                            pe.wait_ge(copied, n - 3)
                        for i in range(4):
                            mm = nc.tensor.transpose(c.ps[:, n % 4, P * i:P * i + P],
                                                     c.xn[:, 4 * half + i, P * tt:P * tt + P], c.k("ident"))
                        mm.then_inc(turned, 1)
                pe.wait_ge(counted, 1)
                for tt in range(TT):
                    for j in range(tt + 1):
                        nc.tensor.matmul(c.ps[:, 5, N_EXP * tt:N_EXP * tt + N_EXP],
                                         c.k("tri") if j == tt else c.k("ones"), Ms[:, j, :],
                                         start=(j == 0), stop=(j == tt))
                for j in range(TT):
                    mm = nc.tensor.matmul(c.ps[:, 5, 64:64 + N_EXP], c.k("ones"), Ms[:, j, :],
                                          start=(j == 0), stop=(j == TT - 1))
                mm.then_inc(placed, 1)

            @block.scalar
            def _(act):
                for tt in range(TT):
                    for half in range(2):
                        n = 2 * tt + half
                        act.wait_ge(turned, n + 1)
                        nc.scalar.copy(rows[:, tt, 512 * half:512 * half + 512], c.bank(n % 4)).then_inc(copied, 1)
                for i, t in enumerate((ex, le)):
                    act.wait_ge(exp_in, i + 1)
                    nc.scalar.activation(t[:, :, :], t[:, :, :], ACT.Exp).then_inc(expd, 1)

            @block.vector
            def _(dve):
                n = [0]

                def then(ins):
                    n[0] += 1
                    ins.then_inc(step, 1)
                    dve.wait_ge(step, n[0])

                tt_ = nc.vector.tensor_tensor

                def first_equal(out, x, top):
                    then(tt_(out, x, top.unsqueeze(2).broadcast_to([P, TT, 4]), ALU.is_equal))
                    then(tt_(taken[:, :], out[:, :, 0], out[:, :, 1], ALU.max))
                    then(tt_(fresh[:, :], taken[:, :], out[:, :, 2], ALU.max))
                    then(tt_(out[:, :, 3], out[:, :, 3], fresh[:, :], ALU.is_gt))
                    then(tt_(out[:, :, 2], out[:, :, 2], taken[:, :], ALU.is_gt))
                    then(tt_(out[:, :, 1], out[:, :, 1], out[:, :, 0], ALU.is_gt))

                def wide(x):
                    return x.unsqueeze(2).broadcast_to([P, TT, 4])

                dve.wait_ge(logits, 1)
                then(tt_(L[:, :, :], c.ps[:, 4, 0:80].rearrange("p (t e) -> p t e", t=TT),
                         c.p("rb").unsqueeze(1).broadcast_to([P, TT, 20]), ALU.add))
                then(nc.vector.tensor_reduce(gmax[:, :], L[:, :, 0:4], AX_X, ALU.max))
                first_equal(selg[:, :, :], L[:, :, 0:4], gmax[:, :])
                tt_(ex[:, :, :], L[:, :, 0:4], wide(gmax[:, :]), ALU.subtract).then_inc(exp_in, 1)
                dve.wait_ge(expd, 1)
                then(nc.vector.tensor_reduce(gsum[:, :], ex[:, :, :], AX_X, ALU.add))
                then(nc.vector.reciprocal(gate[:, :], gsum[:, :]))
                then(tt_(le[:, :, :], L[:, :, 4:8], wide(selg[:, :, 0]), ALU.mult))
                for g in range(1, 4):
                    then(tt_(tmp4[:, :, :], L[:, :, 4 + 4 * g:8 + 4 * g], wide(selg[:, :, g]), ALU.mult))
                    then(tt_(le[:, :, :], le[:, :, :], tmp4[:, :, :], ALU.add))
                then(nc.vector.tensor_reduce(gmax[:, :], le[:, :, :], AX_X, ALU.max))
                tt_(le[:, :, :], le[:, :, :], wide(gmax[:, :]), ALU.subtract).then_inc(exp_in, 1)
                dve.wait_ge(expd, 2)
                then(nc.vector.tensor_reduce(gsum[:, :], le[:, :, :], AX_X, ALU.add))
                then(nc.vector.reciprocal(gsum[:, :], gsum[:, :]))
                then(tt_(le[:, :, :], le[:, :, :], wide(gsum[:, :]), ALU.mult))
                then(nc.vector.tensor_reduce(val[:, 0, :], le[:, :, :], AX_X, ALU.max))
                first_equal(s12[:, 0], le[:, :, :], val[:, 0, :])
                then(nc.vector.scalar_tensor_tensor(out=le[:, :, :], in0=s12[:, 0], scalar=-2.0, in1=le[:, :, :],
                                                    op0=ALU.mult, op1=ALU.add))
                then(nc.vector.tensor_reduce(val[:, 1, :], le[:, :, :], AX_X, ALU.max))
                first_equal(s12[:, 1], le[:, :, :], val[:, 1, :])
                then(tt_(gsum[:, :], val[:, 0, :], val[:, 1, :], ALU.add))
                then(nc.vector.reciprocal(gsum[:, :], gsum[:, :]))
                then(tt_(gsum[:, :], gsum[:, :], gate[:, :], ALU.mult))
                for k in range(2):
                    then(tt_(wt[:, k, :], val[:, k, :], gsum[:, :], ALU.mult))
                for k in range(2):
                    for g in range(4):
                        then(tt_(M[:, k, :, 4 * g:4 * g + 4], s12[:, k], wide(selg[:, :, g]), ALU.mult))
                tt_(Ms[:, :, :], M[:, 0], M[:, 1], ALU.add).then_inc(counted, 1)
                dve.wait_ge(placed, 1)
                then(nc.vector.tensor_copy(cnt[:, :], c.ps[:, 5, 64:64 + N_EXP]))
                then(nc.vector.tensor_scalar(tiles[:, :], cnt[:, :], 0.0, None, ALU.is_gt))
                for k in range(1, 4):
                    then(nc.vector.scalar_tensor_tensor(out=tiles[:, :], in0=cnt[:, :], scalar=float(P * k),
                                                        in1=tiles[:, :], op0=ALU.is_gt, op1=ALU.add))
                then(nc.vector.tensor_tensor_scan(incl[:, :], c.k("ones")[:, 0:N_EXP], tiles[:, :], 0.0,
                                                  ALU.mult, ALU.add))
                then(tt_(excl[:, :], incl[:, :], tiles[:, :], ALU.subtract))
                then(nc.vector.tensor_scalar(excl[:, :], excl[:, :], float(P), None, ALU.mult))
                then(tt_(pos[:, :, :], c.ps[:, 5, 0:64].rearrange("p (t e) -> p t e", t=TT),
                         excl[:, :].unsqueeze(1).broadcast_to([P, TT, N_EXP]), ALU.add))
                for k in range(2):
                    then(tt_(tm[:, k], M[:, k], pos[:, :, :], ALU.mult))
                    then(nc.vector.tensor_reduce(dst[:, k, :], tm[:, k], AX_X, ALU.add))
                then(nc.vector.tensor_copy(dsti[:, :, :], dst[:, :, :]))
                dve.wait_ge(rec_in, 32)
                then(nc.vector.tensor_copy(rec[:, :, :, 2].bitcast(F32), wt[:, :, :]))
                then(tt_(cmp[:, :, :], incl[0:1, :].unsqueeze(1).broadcast_to([1, 24, N_EXP]),
                         c.k("tileid")[0:1, :].rearrange("p (i e) -> p i e", i=24), ALU.is_le))
                then(nc.vector.tensor_reduce(tl[:, 0:24], cmp[:, :, :], AX_X, ALU.add))
                then(nc.vector.tensor_copy(tl[:, 23:24], incl[0:1, 15:16]))
                then(nc.vector.tensor_scalar(tl[:, 24:25], incl[0:1, 15:16], 1.0, None, ALU.subtract))
                nc.vector.tensor_copy(c.tiles[:, :], tl[:, :]).then_inc(fwd_tiles, 1)

            @block.gpsimd
            def _(pool):
                pool.wait_ge(fwd_tiles, 1)
                pool.wait_ge(c.list_empty, 16)
                for k in range(2):
                    for tt in range(TT):
                        nc.gpsimd.indirect_dma_start(
                            out=a["plist"], out_offset=bass.IndirectOffsetOnAxis(ap=dsti[:, k, tt:tt + 1], axis=0),
                            in_=rec[:, k, tt, :], in_offset=None).then_inc(listed, 16)


def stage_experts(c):
    nc, a = c.nc, c.a
    with Stage(nc, "moe") as ctx:
        sem = ctx.sem
        sb = lambda x, shape, dt=F32: ctx.enter_context(nc.sbuf_tensor(f"moe_{x}", shape, dt))
        slabs = {"g": sb("wg", [P, DC, D_EXP]), "u": sb("wu", [P, DC, D_EXP]), "d": sb("wd", [P, D_EXP // P, D])}
        high, low = ([sb(f"{x}{i}", [P, 2 * D_EXP], F32R) for i in range(RING)] for x in ("wh", "wl"))
        xg, xT = sb("xg", [P, D]), [sb(f"xT_{i}", [P, DC, P], F32R) for i in ("high", "low")]
        hh, hT, y = sb("hh", [P, D_EXP]), [sb(f"hT_{i}", [P, 4, P], F32R) for i in ("high", "low")], sb("y", [P, D])
        gi, si = sb("gi", [P, 4], I32), sb("si", [P, 6], I32)
        w_in = [sem(f"w_in{half}") for half in range(6)]
        (rounded, split_v, split_p, used, zeroed, idx, turned, xhigh, xlow, silued, hready, hturned, hhigh, hlow,
         ycopied, sidx) = (
            sem(x) for x in ("rounded", "split_v", "split_p", "used", "zeroed", "idx", "turned", "xhigh", "xlow",
                             "silued", "hready", "hturned", "hhigh", "hlow", "ycopied", "sidx"))
        passed_pool, passed_sp, y_free = sem("passed_pool"), sem("passed_sp"), sem("y_free")
        gathered, scattered = ctx.dma_sem("gathered"), ctx.dma_sem("scattered")
        BY_POOL = (5, 8, 11)

        def count(eng):
            return eng.value_load(c.tiles[0:1, 23:24], min_val=PAIRS // P, max_val=MAX_TILES)

        def last(eng):
            return eng.value_load(c.tiles[0:1, 24:25], min_val=PAIRS // P - 1, max_val=MAX_TILES - 1)

        def nth(i, k, end=False):
            if isinstance(i, int) and i == 0:
                return k
            return 12 * i - 4 + (k - 8 if end else k)

        def buffer(i, k, end=False):
            return (k if isinstance(i, int) and i == 0 else (k - 8 if end else k) + 2) % RING

        def parted(i, k, end=False):
            first = isinstance(i, int) and i == 0
            before = sum(p in BY_POOL for p in range(8 if end else 0, k + 1))
            if k in BY_POOL:
                return split_p, (0 if first else 3 * i - 2) + before
            return split_v, (0 if first else 9 * i - 2) + k + 1 - (8 if end else 0) - before

        def piece(k):
            if k < 8:
                return slabs["gu"[k // 4]][:, 2 * (k % 4):2 * (k % 4) + 2, :].rearrange("p a e -> p (a e)")
            return slabs["d"][:, k - 8, :]

        def rest(eng, i, k, end=False):
            b = buffer(i, k, end)
            eng.wait_ge(rounded, nth(i, k, end) + 1)
            (nc.gpsimd if k in BY_POOL else nc.vector).tensor_tensor(
                low[b][:, :], piece(k), high[b][:, :].bitcast(F32), ALU.subtract)\
              .then_inc(split_p if k in BY_POOL else split_v, 1)

        def later(i, rounds):
            return not isinstance(i, int) or i >= rounds

        with nc.Block("experts") as block:
            @block.sync
            def _(sp):
                def load(i, first, before):
                    e = sp.value_load(c.tiles[0:1, bass.ds(i, 1)], min_val=0, max_val=N_EXP - 1)
                    x = first // 4
                    src = a[("w_gate", "w_up", "w_down")[x]]
                    for k in (first, first + 2):
                        if before is not None:
                            for j in (k, k + 1):
                                wait_apart(sp, *parted(before, j), passed_sp)
                        n = slabs["gud"[x]].shape[1] // 2
                        at = slice(n * (k - first) // 2, n * (k - first) // 2 + n)
                        sp.dma_start(slabs["gud"[x]][:, at, :],
                                     src[bass.ds(e, 1), :, at].rearrange("a p k m -> (a p) k m"))\
                          .then_inc(w_in[k // 2], 16)

                def body(i):
                    load(i, 0, i - 1 if later(i, 1) else None)
                    if not later(i, 1):
                        sp.wait_ge(gathered, 16)
                    load(i, 4, i - 1 if later(i, 1) else None)
                    if later(i, 1):
                        load(i - 1, 8, i - 1 if later(i, 2) else None)

                repeat(sp, count(sp), body, peel=2)
                l = last(sp)
                load(l, 8, l)

            @block.gpsimd
            def _(pool):
                nc.gpsimd.memset(xg[:, :], 0.0).then_inc(zeroed, 1)
                pool.wait_ge(zeroed, 1)

                def gather(i):
                    emit_wait(pool, turned, 2 * i)
                    emit_wait(pool, gathered, 16 * i)
                    src = c.slots[:, bass.ds(i, 1), 0:2].rearrange("p a x -> p (a x)")
                    nc.gpsimd.tensor_copy(gi[:, 0:2], src).then_inc(idx, 1)
                    wait_apart(pool, idx, i + 1, passed_pool)
                    nc.gpsimd.indirect_dma_start(
                        out=xg[:, :], out_offset=None, in_=a["hrows"],
                        in_offset=bass.IndirectOffsetOnAxis(ap=gi[:, 0:1].bitcast(U32), axis=0),
                        bounds_check=T - 1, oob_is_err=False).then_inc(gathered, 16)

                def free_y(i):
                    wait_apart(pool, scattered, 16 * i + 32, y_free)

                def scatter(i):
                    pool.wait_ge(ycopied, 2 * i + 2)
                    src = c.slots[:, bass.ds(i, 1), 0:2].rearrange("p a x -> p (a x)")
                    nc.gpsimd.tensor_copy(si[:, 0:2], src).then_inc(sidx, 1)
                    wait_apart(pool, sidx, i + 1, passed_pool)
                    nc.gpsimd.indirect_dma_start(
                        out=a["yrows"], out_offset=bass.IndirectOffsetOnAxis(ap=si[:, 1:2].bitcast(U32), axis=0),
                        in_=y[:, :], in_offset=None, bounds_check=PAIRS - 1, oob_is_err=False)\
                      .then_inc(scattered, 16)

                def body(i):
                    if later(i, 2):
                        free_y(i - 2)
                    rest(pool, i, 5)
                    if later(i, 2):
                        scatter(i - 2)
                    if later(i, 1):
                        rest(pool, i, 8)
                        rest(pool, i, 11)
                    gather(i + 2)

                gather(0)
                for j in (2, 4):
                    pool.dma_start(si[:, j:j + 2], a["empty"][0:P, 0:2]).then_inc(scattered, 16)
                pool.sem_inc(y_free, 1)
                gather(1)
                repeat(pool, count(pool), body, peel=2)
                l = last(pool)
                free_y(l - 1)
                rest(pool, l + 1, 8, end=True)
                scatter(l - 1)
                rest(pool, l + 1, 11, end=True)
                free_y(l)
                scatter(l)
                pool.wait_ge(scattered, 16 * l + 48)
                pool.wait_ge(gathered, 16 * l + 48)

            @block.tensor
            def _(pe):
                def turn_x(i):
                    pe.wait_ge(gathered, 16 * i + 16)
                    for half in range(2):
                        emit_wait(pe, xlow, 2 * i)
                        for j in range(4):
                            mm = nc.tensor.transpose(c.ps[:, half, P * j:P * j + P],
                                                     xg[:, 512 * half + P * j:512 * half + P * j + P], c.k("ident"))
                        mm.then_inc(turned, 1)

                def down(i, at, end=False):
                    pe.wait_ge(hlow, at)
                    emit_wait(pe, ycopied, 2 * (at - 1))
                    for j in range(4):
                        pe.wait_ge(*parted(i, 8 + j, end))
                        b = buffer(i, 8 + j, end)
                        for half in range(2):
                            x = slice(512 * half, 512 * half + 512)
                            mm = c.product(c.bank(5 + half), [h[:, j, :] for h in hT],
                                           (high[b][:, x], low[b][:, x]), j == 0, j == 3)
                        mm.then_inc(used, 1)

                def body(i):
                    pe.wait_ge(xlow, 2 * i + 2)
                    emit_wait(pe, hready, i)
                    for k in range(8):
                        pe.wait_ge(*parted(i, k))
                        b = buffer(i, k)
                        for j in range(2):
                            x = slice(512 * j, 512 * j + 512)
                            mm = c.product(c.bank(2 + k // 4), [h[:, 2 * (k % 4) + j, :] for h in xT],
                                           (high[b][:, x], low[b][:, x]), k % 4 == 0 and j == 0,
                                           k % 4 == 3 and j == 1)
                        mm.then_inc(used, 1)
                    turn_x(i + 1)
                    if later(i, 1):
                        down(i, i)
                    pe.wait_ge(hready, i + 1)
                    emit_wait(pe, hlow, i)
                    for j in range(4):
                        mm = nc.tensor.transpose(c.ps[:, 4, P * j:P * j + P], hh[:, P * j:P * j + P], c.k("ident"))
                    mm.then_inc(hturned, 1)

                turn_x(0)
                repeat(pe, count(pe), body, peel=2)
                n = last(pe) + 1
                down(n, n, end=True)

            @block.scalar
            def _(act):
                def round_(i, k, end=False):
                    if k % 2 == 0:
                        act.wait_ge(w_in[k // 2], 16 * i + (0 if k >= 8 else 16))
                    emit_wait(act, used, nth(i, k, end) - RING + 1)
                    nc.scalar.copy(high[buffer(i, k, end)][:, :], piece(k)).then_inc(rounded, 1)

                def round_x(i):
                    for half in range(2):
                        act.wait_ge(turned, 2 * i + half + 1)
                        if later(i, 1):
                            act.wait_ge(used, nth(i - 1, 8))
                        nc.scalar.copy(xT[0][:, 4 * half:4 * half + 4, :].rearrange("p a t -> p (a t)"), c.bank(half))\
                          .then_inc(xhigh, 1)

                def round_h(i, freed):
                    act.wait_ge(hturned, i + 1)
                    emit_wait(act, used, freed)
                    nc.scalar.copy(hT[0][:, :, :].rearrange("p a t -> p (a t)"), c.bank(4)).then_inc(hhigh, 1)

                def copy_y(i, ready):
                    act.wait_ge(used, ready)
                    act.wait_ge(y_free, i + 2)
                    for half in range(2):
                        nc.scalar.copy(y[:, 512 * half:512 * half + 512], c.bank(5 + half)).then_inc(ycopied, 1)

                def body(i):
                    for k in range(4):
                        round_(i, k)
                    if later(i, 1):
                        round_h(i - 1, nth(i, 0) if later(i, 2) else 0)
                    for k in (4, 5):
                        round_(i, k)
                    if later(i, 2):
                        copy_y(i - 2, nth(i, 0))
                    for k in (6, 7):
                        round_(i, k)
                    act.wait_ge(used, nth(i, 4))
                    emit_wait(act, hturned, i)
                    nc.scalar.activation(hh[:, :], c.bank(2), ACT.Silu).then_inc(silued, 1)
                    if later(i, 1):
                        for k in range(8, 12):
                            round_(i, k)
                    round_x(i + 1)

                round_x(0)
                repeat(act, count(act), body, peel=2)
                l = last(act)
                n = l + 1
                round_h(l, nth(n, 0))
                copy_y(l - 1, nth(n, 0))
                for k in range(8, 12):
                    round_(n, k, end=True)
                copy_y(l, nth(n, 4))

            @block.vector
            def _(dve):
                def rest_x(i):
                    for half in range(2):
                        dve.wait_ge(xhigh, 2 * i + half + 1)
                        d = [t[:, 4 * half:4 * half + 4, :].rearrange("p a t -> p (a t)") for t in xT]
                        nc.vector.tensor_tensor(d[1], c.bank(half), d[0].bitcast(F32), ALU.subtract)\
                          .then_inc(xlow, 1)

                def rest_h(i):
                    dve.wait_ge(hhigh, i + 1)
                    d = [t[:, :, :].rearrange("p a t -> p (a t)") for t in hT]
                    nc.vector.tensor_tensor(d[1], c.bank(4), d[0].bitcast(F32), ALU.subtract).then_inc(hlow, 1)

                def body(i):
                    for k in range(4):
                        rest(dve, i, k)
                    if later(i, 1):
                        rest_h(i - 1)
                    for k in (4, 6, 7) + ((9, 10) if later(i, 1) else ()):
                        rest(dve, i, k)
                    dve.wait_ge(silued, i + 1)
                    dve.wait_ge(used, nth(i, 8))
                    wcol = c.slots[:, bass.ds(i, 1), 2:3].bitcast(F32).rearrange("p a x -> p (a x)")
                    nc.vector.scalar_tensor_tensor(out=hh[:, :], in0=hh[:, :], scalar=wcol, in1=c.bank(3),
                                                   op0=ALU.mult, op1=ALU.mult).then_inc(hready, 1)
                    rest_x(i + 1)

                rest_x(0)
                repeat(dve, count(dve), body, peel=2)
                l = last(dve)
                rest_h(l)
                for k in (9, 10):
                    rest(dve, l + 1, k, end=True)


def stage_combine(c):
    nc, a = c.nc, c.a
    with Stage(nc, "comb") as ctx:
        sem = ctx.sem
        y = ctx.enter_context(nc.sbuf_tensor("comb_y", [P, 2, TT, D], F32))
        y_in = [sem(f"y_in{t}") for t in range(TT)]
        summed, turned, added = sem("summed"), sem("turned"), sem("added")
        with nc.Block("combine") as block:
            @block.sync
            def _(sp):
                rows = a["yrows"].rearrange("(k t p) d -> t p k d", k=2, p=P)
                for tt in range(TT):
                    sp.dma_start(y[:, :, tt, :], rows[tt]).then_inc(y_in[tt], 16)

            @block.vector
            def _(dve):
                for tt in range(TT):
                    dve.wait_ge(y_in[tt], 16)
                    nc.vector.tensor_tensor(y[:, 0, tt, :], y[:, 0, tt, :], y[:, 1, tt, :], ALU.add)\
                      .then_inc(summed, 1)
                for i in range(DC):
                    dve.wait_ge(turned, i + 1)
                    nc.vector.tensor_tensor(c.h[:, i, :], c.bank(i), c.h[:, i, :], ALU.add).then_inc(added, 1)

            @block.tensor
            def _(pe):
                for i in range(DC):
                    for tt in range(TT):
                        pe.wait_ge(summed, tt + 1)
                        mm = nc.tensor.transpose(c.ps[:, i, P * tt:P * tt + P], y[:, 0, tt, P * i:P * i + P],
                                                 c.k("ident"))
                    mm.then_inc(turned, 1)


def stage_select(c, weights):
    nc, a = c.nc, c.a
    with Stage(nc, "sel") as ctx:
        sem = ctx.sem
        sb = lambda x, shape: ctx.enter_context(nc.sbuf_tensor(f"sel_{x}", shape, F32))
        w, ww, w_in = weights
        raw, tmp, tmp2 = sb("raw", [P, 3, T]), sb("tmp", [P, 3, T]), sb("tmp2", [P, T])
        fin = sb("fin", [P, 3, T])
        wi = sb("wi", [P, TT, 4])
        rel = sb("rel", [P, 2, 4, T])
        projected, weighed, evac, meaned, step, sq, varred, rooted, rotated, ready, scored, reluded, accd = (
            sem(x) for x in ("projected", "weighed", "evac", "meaned", "step", "sq", "varred", "rooted",
                             "rotated", "ready", "scored", "reluded", "accd"))
        kready, logged = sem("kready"), sem("logged")
        with nc.Block("select") as block:
            @block.tensor
            def _(pe):
                pe.wait_ge(w_in, 32)
                for i in (2, 0, 1):
                    for j in range(DC):
                        mm = nc.tensor.matmul(c.bank(i), w[:, i, j, :], c.xn[:, j, :], start=(j == 0),
                                              stop=(j == DC - 1))
                    mm.then_inc(projected, 1)
                pe.wait_ge(evac, 1)
                nc.tensor.matmul(c.bank(4), c.k("blk64"), raw[:, 2, :], start=True, stop=True).then_inc(meaned, 1)
                pe.wait_ge(sq, 1)
                nc.tensor.matmul(c.bank(5), c.k("blk64"), tmp[:, 2, :], start=True, stop=True).then_inc(varred, 1)
                for i in (0, 1):
                    pe.wait_ge(evac, 2 + i)
                    nc.tensor.matmul(c.bank(i), c.k("rot"), raw[:, i, :], start=True, stop=True).then_inc(rotated, 1)
                for tt in range(TT):
                    for j in range(DC):
                        mm = nc.tensor.matmul(c.ps[:, 3, 4 * tt:4 * tt + 4], c.xn[:, j, P * tt:P * tt + P],
                                              ww[:, j, :], start=(j == 0), stop=(j == DC - 1))
                mm.then_inc(weighed, 1)
                pe.wait_ge(kready, 1)
                nc.tensor.matmul(c.bank(2), c.k("rot"), raw[:, 2, :], start=True, stop=True).then_inc(rotated, 1)
                pe.wait_ge(ready, 3)
                for t, qt in enumerate((1, 2, 3)):
                    for h in range(4):
                        hd = slice(HD * (h % 2), HD * (h % 2) + HD)
                        if t:
                            pe.wait_ge(reluded, 4 * (t - 1) + h + 1)
                        nc.tensor.matmul(c.ps[:, 4 + h, 0:P * (qt + 1)], fin[hd, h // 2, P * qt:P * qt + P],
                                         fin[hd, 2, 0:P * (qt + 1)], start=True, stop=True).then_inc(scored, 1)

            @block.scalar
            def _(act):
                for n, i in enumerate((2, 0, 1)):
                    act.wait_ge(projected, n + 1)
                    nc.scalar.copy(raw[:, i, :], c.bank(i)).then_inc(evac, 1)
                act.wait_ge(step, 1)
                nc.scalar.activation(tmp[:, 2, :], raw[:, 2, :], ACT.Square).then_inc(sq, 1)
                act.wait_ge(varred, 1)
                nc.scalar.activation(tmp[:, 2, :], c.bank(5), ACT.Ln, bias=c.eps[:, 0:1]).then_inc(logged, 1)
                act.wait_ge(logged, 1)
                nc.scalar.activation(tmp2[:, :], tmp[:, 2, :], ACT.Exp, scale=-0.5).then_inc(rooted, 1)
                for t, qt in enumerate((1, 2, 3)):
                    for h in range(4):
                        act.wait_ge(scored, 4 * t + h + 1)
                        if t == 2:
                            act.wait_ge(accd, 4)
                        nc.scalar.activation(rel[:, t % 2, h, 0:P * (qt + 1)], c.ps[:, 4 + h, 0:P * (qt + 1)],
                                             ACT.Relu).then_inc(reluded, 1)

            @block.vector
            def _(dve):
                n = [0]

                def then(ins):
                    n[0] += 1
                    ins.then_inc(step, 1)
                    dve.wait_ge(step, n[0])

                dve.wait_ge(meaned, 1)
                then(nc.vector.tensor_tensor(raw[:, 2, :], raw[:, 2, :], c.bank(4), ALU.subtract))
                dve.wait_ge(rooted, 1)
                then(nc.vector.tensor_tensor(raw[:, 2, :], raw[:, 2, :], tmp2[:, :], ALU.mult))
                nc.vector.tensor_scalar(raw[:, 2, :], raw[:, 2, :], c.p("lng"), c.p("lnb"), ALU.mult, ALU.add)\
                  .then_inc(kready, 1)
                dve.wait_ge(kready, 1)
                for m, i in enumerate((0, 1, 2)):
                    dve.wait_ge(evac, 3)
                    then(nc.vector.tensor_tensor(tmp[:, i, :], raw[:, i, :], c.k("cos"), ALU.mult))
                    dve.wait_ge(rotated, m + 1)
                    then(nc.vector.tensor_tensor(tmp2[:, :], c.bank(i), c.k("sin"), ALU.mult))
                    nc.vector.tensor_tensor(fin[:, i, :], tmp[:, i, :], tmp2[:, :], ALU.add).then_inc(ready, 1)
                    dve.wait_ge(ready, m + 1)
                dve.wait_ge(weighed, 1)
                then(nc.vector.tensor_copy(wi[:, :, :].rearrange("p a e -> p (a e)"), c.ps[:, 3, 0:4 * TT]))
                nc.vector.tensor_copy(c.selb[:, 0:P], c.k("cmask"))
                for t, qt in enumerate((1, 2, 3)):
                    nk = P * (qt + 1)
                    x = c.selb[:, OFF[qt]:OFF[qt] + nk]
                    for h in range(4):
                        dve.wait_ge(reluded, 4 * t + h + 1)
                        r = rel[:, t % 2, h, 0:nk]
                        if h == 0:
                            then(nc.vector.tensor_scalar(x, r, wi[:, qt, 0:1], None, ALU.mult))
                        else:
                            then(nc.vector.scalar_tensor_tensor(out=x, in0=r, scalar=wi[:, qt, h:h + 1], in1=x,
                                                                op0=ALU.mult, op1=ALU.add))
                    then(nc.vector.tensor_tensor(x[:, nk - P:nk], x[:, nk - P:nk], c.k("cmask"), ALU.add))
                    nc.vector.memset(c.m8[:, :], 0.0).then_inc(accd, 4)


def top_keys(c, stage, rounds):
    nc = c.nc
    taken = stage.sem("taken")
    tiles = [c.selb[:, OFF[qt]:OFF[qt] + P * (qt + 1)] for qt in (1, 2, 3)]
    share = TOPK // 8 // rounds
    steps = 2 * share * len(tiles)

    def aside(dve, u, passed):
        n = [steps * u]

        def then(ins):
            n[0] = n[0] + 1
            ins.then_inc(taken, 1)
            wait_apart(dve, taken, n[0], passed)

        if isinstance(u, int) and u == rounds:
            return
        for x in tiles:
            for r in range(share):
                then(nc.vector.max(c.m8[:, :], x))
                then(nc.vector.match_replace(x, c.m8[:, :], x, TAKEN))
        if isinstance(u, int) and u == rounds - 1:
            for x in tiles:
                then(nc.vector.tensor_scalar(x, x, 0.5 * TAKEN, NEG, ALU.is_gt, ALU.mult))
                d = x[:, -P:]
                nc.vector.tensor_tensor(d, d, c.k("cmask"), ALU.add)

    return aside


def stage_forget_prepare(c):
    nc, a = c.nc, c.a
    with Stage(nc, "fg") as ctx:
        sem = ctx.sem
        sb = lambda x, shape: ctx.enter_context(nc.sbuf_tensor(f"fg_{x}", shape, F32))
        w = sb("w", [P, DC, 8])
        x, ab, e, one, cum = sb("x", [8, T]), sb("ab", [8, T]), sb("e", [8, T]), sb("one", [8, T]), sb("cum", [8, T])
        low = sb("low", [8, T])
        w_in, projected, biased, lg, step, spread = (
            sem(n) for n in ("w_in", "projected", "biased", "lg", "step", "spread"))
        ast = sem("ast")
        with nc.Block("forget") as block:
            @block.sync
            def _(sp):
                sp.dma_start(w[:, :, :], a["w_forget"]).then_inc(w_in, 16)
                sp.wait_ge(step, 4)
                sp.dma_start(c.fneg[0:1, :, :], cum[:, :]).then_inc(spread, 16)
                sp.wait_ge(spread, 16)

            @block.tensor
            def _(pe):
                pe.wait_ge(w_in, 16)
                for j in range(DC):
                    mm = nc.tensor.matmul(c.ps[0:8, 0, :], w[:, j, :], c.xn[:, j, :], start=(j == 0),
                                          stop=(j == DC - 1))
                mm.then_inc(projected, 1)

            @block.scalar
            def _(act):
                act.wait_ge(biased, 1)
                nc.scalar.activation(ab[:, :], x[:, :], ACT.Abs).then_inc(ast, 1)
                act.wait_ge(ast, 1)
                nc.scalar.activation(e[:, :], ab[:, :], ACT.Exp, scale=-1.0).then_inc(ast, 1)
                act.wait_ge(ast, 2)
                nc.scalar.activation(ab[:, :], e[:, :], ACT.Ln, bias=c.k("ones")[0:8, 0:1]).then_inc(lg, 1)

            @block.vector
            def _(dve):
                nc.vector.memset(one[:, :], 1.0).then_inc(step, 1)
                dve.wait_ge(projected, 1)
                fb = PARAMS["fb"][0]
                nc.vector.tensor_scalar(x[:, :], c.ps[0:8, 0, :], c.param[0:8, fb:fb + 1], None, ALU.add)\
                  .then_inc(biased, 1)
                dve.wait_ge(biased, 1)
                nc.vector.tensor_scalar(low[:, :], x[:, :], 0.0, None, ALU.min).then_inc(step, 1)
                dve.wait_ge(lg, 1)
                dve.wait_ge(step, 2)
                nc.vector.tensor_tensor(low[:, :], ab[:, :], low[:, :], ALU.subtract).then_inc(step, 1)
                dve.wait_ge(step, 3)
                nc.vector.tensor_tensor_scan(cum[:, :], one[:, :], low[:, :], 0.0, ALU.mult, ALU.add)\
                  .then_inc(step, 1)


def stage_store(c):
    nc = c.nc
    with Stage(nc, "store") as ctx:
        s = ctx.sem("out")
        with nc.Block("store") as block:
            @block.sync
            def _(sp):
                sp.dma_start(c.a["out"], c.xn[:, :, :]).then_inc(s, 16)
                sp.wait_ge(s, 16)


def build(nc, a, until=None):
    with ExitStack() as ctx:
        c = Chip(nc, ctx, a)

        def tensors(stack, *wanted):
            return [stack.enter_context(nc.sbuf_tensor(n, s, d)) for n, s, d in wanted]

        def parts(stack, name, chunks):
            return tensors(stack, (name + "_high", [P, chunks, T], F32R), (name + "_low", [P, chunks, T], F32R))

        def feed_forward(layer, gain):
            with ExitStack() as outer:
                hidden = parts(outer, f"ff{layer}", FC)
                w_down = a[f"w_ff_down{layer}"]
                with Stage(nc, f"ff_ahead{layer}") as st:
                    half = FirstHalf(c, st, f"down{layer}", w_down, FC)
                    stage_ffn_up(c, f"up{layer}", layer, a[f"w_ff_up{layer}"], gain, hidden, half.load)
                    stage_back(c, f"down{layer}", w_down, hidden, FC, half)

        stage_load(c)
        with ExitStack() as outer:
            c.o = parts(outer, "o1", DC)
            (o,) = tensors(outer, ("o1_whole", [P, DC, T], F32))
            with ExitStack() as inner:
                x = parts(inner, "x1", DC)
                c.qgain, c.neglam = tensors(inner, ("qgain", [P, 1], F32), ("neglam", [P, 1], F32))
                wt = Weights(c, inner, "diff")
                with Stage(nc, "diff_ahead") as st:
                    stage_norm(c, "norm1", c.p("g_mix"), x, o, ahead=weights_ahead(c, st, wt, a["w_da"]))
                    stage_diff_prepare(c)
                c.o, split = (o, None), c.o
                stage_attention(c, "diff", "diff", 8, wt, a["w_da"], x, 0, bias=a["alibi"])
                c.o = split
            with Stage(nc, "out_ahead1") as st:
                half = FirstHalf(c, st, "da_out", a["w_da_out"], DC)
                stage_subln(c, o, c.o, half.load)
                stage_back(c, "da_out", a["w_da_out"], c.o, DC, half)
        if until == 2:
            return c
        with ExitStack() as outer:
            c.slots, c.tiles = tensors(outer, ("slots", [P, 25, 4], I32), ("tiles", [1, 25], I32))
            with ExitStack() as inner:
                (c.xn,) = tensors(inner, ("x2_whole", [P, DC, T], F32))
                stage_norm(c, "norm2", c.p("g_ffn"), None, c.xn)
                stage_route(c)
            stage_experts(c)
            stage_combine(c)
        if until == 3:
            return c
        with ExitStack() as outer:
            c.o = parts(outer, "o3", DC)
            half = FirstHalf(c, outer.enter_context(Stage(nc, "out_ahead3")), "even_out", a["w_even_out"], DC)
            with ExitStack() as inner:
                x = parts(inner, "x3", DC)
                c.selb, c.m8 = tensors(inner, ("selb", [P, PW], F32), ("m8", [P, 8], F32))
                wt = Weights(c, inner, "even")
                with ExitStack() as whole:
                    (c.xn,) = tensors(whole, ("x3_whole", [P, DC, T], F32))
                    w_idx, w_idxw = tensors(whole, ("w_idx", [P, 3, DC, P], F32), ("w_idxw", [P, DC, 4], F32))
                    with Stage(nc, "even_ahead") as st:
                        idx_in = st.sem("idx_in")
                        load, round_, rest = weights_ahead(c, st, wt, a["w_rel"])

                        def load_all(sp):
                            load(sp)
                            sp.dma_start(w_idx[:, :, :, :], a["w_idx"].rearrange("i p k m -> p i k m"))\
                              .then_inc(idx_in, 16)
                            sp.dma_start(w_idxw[:, :, :], a["w_idxw"]).then_inc(idx_in, 16)

                        stage_norm(c, "norm3", c.p("g_mix2", 0, DC), x, c.xn, ahead=(load_all, round_, rest))
                        stage_select(c, (w_idx, w_idxw, idx_in))
                with Stage(nc, "topk") as st:
                    stage_attention(c, "rel", "rel", 4, wt, a["w_rel"], x, 4,
                                    bias=bass.AP(a["relrows"].tensor, P - 1, [[P * 640, 8], [639, P], [1, T]]),
                                    bias_ready=c.rel_spread, next_w=a["w_dsa"], aside=top_keys(c, st, 4))
                stage_attention(c, "dsa", "dsa", 4, wt, a["w_dsa"], x, 0,
                                bias=lambda s, qt: c.selb[:, OFF[qt]:OFF[qt] + P * (qt + 1)], also=half.load)
            stage_back(c, "even_out", a["w_even_out"], c.o, DC, half)
        feed_forward(0, c.p("g_ffn2", 0, DC))
        if until == 5:
            return c
        with ExitStack() as outer:
            c.o = parts(outer, "o5", DC)
            half = FirstHalf(c, outer.enter_context(Stage(nc, "out_ahead5")), "odd_out", a["w_odd_out"], DC)
            with ExitStack() as inner:
                x = parts(inner, "x5", DC)
                (c.fneg,) = tensors(inner, ("fneg", [1, 8, T], F32))
                wt = Weights(c, inner, "odd")
                with ExitStack() as whole:
                    (c.xn,) = tensors(whole, ("x5_whole", [P, DC, T], F32))
                    with Stage(nc, "odd_ahead") as st:
                        stage_norm(c, "norm5", c.p("g_mix2", DC, DC), x, c.xn,
                                   ahead=weights_ahead(c, st, wt, a["w_fgt"]))
                        stage_forget_prepare(c)
                stage_attention(c, "forget_att", "forget", 4, wt, a["w_fgt"], x, 0,
                                bias=lambda s, qt: c.k("cband")[:, T - P - P * qt:T], next_w=a["w_snk"])
                stage_attention(c, "sink", "sink", 4, wt, a["w_snk"], x, 4,
                                bias=lambda s, qt: c.k("sband")[:, (P if qt == 0 else 0):2 * P], also=half.load)
            stage_back(c, "odd_out", a["w_odd_out"], c.o, DC, half)
        feed_forward(1, c.p("g_ffn2", DC, DC))
        with ExitStack() as inner:
            (c.xn,) = tensors(inner, ("x7_whole", [P, DC, T], F32))
            stage_norm(c, "norm7", c.p("g_out"), None, c.xn)
            stage_store(c)
        return c


def pack(inputs):
    i = {k: np.asarray(v) for k, v in inputs.items()}

    def cols(x):
        return np.ascontiguousarray(x.reshape(-1, P).T)

    def fm(w):
        k, m = w.shape
        return np.ascontiguousarray(w.reshape(k // P, P, m // P, P).transpose(2, 1, 0, 3))

    def mv(w):
        k, m = w.shape
        return np.ascontiguousarray(w.reshape(k // P, P, m).transpose(1, 0, 2))

    def qkv(q, k, v):
        return np.ascontiguousarray(np.stack([fm(q), fm(k), fm(v)], axis=1))

    par = np.zeros((P, N_PARAM), np.float32)

    def put(name, value):
        x, y = PARAMS[name]
        par[:, x:y] = value

    put("g_mix", cols(i["norm_mix"]))
    put("g_ffn", cols(i["norm_ffn"]))
    put("g_mix2", cols(i["norm_mix_g_2"]))
    put("g_ffn2", cols(i["norm_ffn_g_2"]))
    put("g_out", cols(i["norm_out_g_2"]))
    put("qg", np.tile(i["da_q_norm"][0], 2)[:, None])
    put("kg", np.tile(i["da_k_norm"][0], 2)[:, None])
    put("subln", i["da_subln"][0][:, None])
    put("lng", np.tile(i["idx_k_ln_g_2"][0], 2)[:, None])
    put("lnb", np.tile(i["idx_k_ln_b_2"][0], 2)[:, None])
    put("convw", i["ffn_conv_w_2"].reshape(2, 3, 2 * FC, P).transpose(3, 0, 2, 1).reshape(P, -1))
    put("convb", i["ffn_conv_b_2"].reshape(2 * 2 * FC, P).T)
    put("sinks", i["sinks_2"][0][None, :])
    par[0:8, PARAMS["fb"][0]] = i["forget_b_2"][0]
    put("rb", np.concatenate([i["moe_b_group"][0], i["moe_b_router"][0]])[None, :])
    put("lam", np.concatenate([i[f"da_lambda_{x}"][0] for x in ("q1", "k1", "q2", "k2")])[None, :])

    consts, alibi, rec, empty = shape_constants()
    wd = i["da_w_in"][0]
    we, wo = i["even_w_in_2"][0], i["odd_w_in_2"][0]
    ki = we[:, 1792:1856]
    ug = i["ffn_w_up_2"]
    out = {
        "xT": np.ascontiguousarray(i["x"][0].T.reshape(DC, P, T).transpose(1, 0, 2)),
        "params": par, "consts": consts, "alibi": alibi, "rec": rec, "empty": empty,
        "relE": np.ascontiguousarray(i["rel_bias_2"][0][:, np.clip(511 - np.arange(640), -256, 256) + 256]),
        "w_da": qkv(wd[:, 0:1024], wd[:, 1024:2048], wd[:, 2048:3072]),
        "w_da_out": fm(i["da_w_out"][0]),
        "w_route": mv(np.concatenate([i["moe_w_group"][0], i["moe_w_router"][0]], axis=1)),
        "w_gate": np.ascontiguousarray(i["moe_w_gate"][0].reshape(N_EXP, DC, P, D_EXP).transpose(0, 2, 1, 3)),
        "w_up": np.ascontiguousarray(i["moe_w_up"][0].reshape(N_EXP, DC, P, D_EXP).transpose(0, 2, 1, 3)),
        "w_down": np.ascontiguousarray(i["moe_w_down"][0].reshape(N_EXP, 4, P, D).transpose(0, 2, 1, 3)),
        "w_dsa": qkv(we[:, 0:512], we[:, 512:1024], we[:, 1024:1536]),
        "w_idx": fm(np.concatenate([we[:, 1536:1792], ki, ki], axis=1)),
        "w_idxw": mv(we[:, 1856:1860]),
        "w_rel": qkv(we[:, 1860:2372], we[:, 2372:2884], we[:, 2884:3396]),
        "w_even_out": fm(i["even_w_out_2"][0]),
        "w_fgt": qkv(wo[:, 0:512], wo[:, 512:1024], wo[:, 1024:1536]),
        "w_forget": mv(wo[:, 1536:1544]),
        "w_snk": qkv(wo[:, 1544:2056],
                     *(np.concatenate([wo[:, s + HD * g:s + HD * g + HD] for g in (0, 1) for _ in range(4)], axis=1)
                       for s in (2056, 2184))),
        "w_odd_out": fm(i["odd_w_out_2"][0]),
    }
    for layer in range(2):
        f = fm(ug[layer])
        out[f"w_ff_up{layer}"] = np.ascontiguousarray(np.stack([f[:FC], f[FC:]], axis=2))
        out[f"w_ff_down{layer}"] = fm(i["ffn_w_down_2"][layer])
    return out


SCRATCH = {"plist": ((24 * P, 4), I32), "relrows": ((8, P, 640), F32), "hrows": ((T, D), F32),
           "yrows": ((PAIRS, D), F32)}


def kernel(**inputs):
    import concourse.bacc as _bacc
    from concourse.bass_utils import run_bass_kernel_spmd as _run

    nc = _bacc.Bacc("TRN2", target_bir_lowering=False, num_devices=1)
    arrays, a = {}, {}
    for name, x in pack(inputs).items():
        arrays[f"in_{name}"] = x
        a[name] = nc.dram_tensor(f"in_{name}", x.shape, mybir.dt.from_np(x.dtype), kind="ExternalInput").ap()
    for name, (shape, dt) in SCRATCH.items():
        a[name] = nc.dram_tensor(name, shape, dt, kind="Internal").ap()
    a["out"] = nc.dram_tensor("out_0", (P, DC, T), F32, kind="ExternalOutput").ap()
    build(nc, a)
    r = _run(nc, [arrays], core_ids=[0])
    got = r.results[0]["out_0"]
    return np.ascontiguousarray(got.transpose(2, 1, 0).reshape(1, T, D))
```
